# Optimizing a Trainium2 kernel written in Bass

```python
import jax, jax.numpy as jnp
from jax import lax
import numpy as np

D_MODEL = 1024
BATCH = 1
SEQ = 128
DEPTH = 2
DEC_BATCH = 1
DEC_SEQ = 128
PAST_LEN = 128

GRID_W = 64
GLA_HEADS = 4
GLA_DK = 64
GLA_DV = 128
GLA_KEY = GLA_HEADS * GLA_DK
GLA_VAL = GLA_HEADS * GLA_DV
GLA_GATE_RANK = 16
GLA_GATE_NORM = 16.0
GLA_CHUNK = 64
CONV_CH = 256
CONV_WIDTH = 31
NA_HEADS = 4
NA_HD = 64
NA_DIM = NA_HEADS * NA_HD
NA_WIN_ROWS = 8
NA_WIN_COLS = 16
NA_QBLOCK = 16
NA_KBLOCK = NA_QBLOCK + NA_WIN_COLS
MIX_WIDTH = GLA_VAL + CONV_CH + NA_DIM
IN_SPLITS = (GLA_KEY, GLA_KEY, GLA_VAL, GLA_VAL, 2 * GLA_GATE_RANK, 2 * CONV_CH, NA_DIM, NA_DIM, NA_DIM)
IN_WIDTH = 2 * GLA_KEY + 2 * GLA_VAL + 2 * GLA_GATE_RANK + 2 * CONV_CH + 3 * NA_DIM
N_EXPERTS = 64
TOP_K = 8
N_GROUPS = 8
TOPK_GROUPS = 4
EXPERT_DIM = 256
SHARED_DIM = 256
ROUTED_SCALE = 2.5
MOE_BLOCK = 128
EPS = 1e-6

kernel_name = 'hybrid_gla_conv_natten_moe_diffusion_step'

def rms_norm(x, g):
    xf = x.astype(jnp.float32)
    y = xf * lax.rsqrt(jnp.mean(xf * xf, axis=-1, keepdims=True) + EPS)
    return (y * g.astype(jnp.float32)).astype(x.dtype)

def layer_norm(x, g, b):
    xf = x.astype(jnp.float32)
    xc = xf - jnp.mean(xf, axis=-1, keepdims=True)
    y = xc * lax.rsqrt(jnp.mean(xc * xc, axis=-1, keepdims=True) + EPS)
    return (y * g.astype(jnp.float32) + b.astype(jnp.float32)).astype(x.dtype)

def to_heads(t, n_heads):
    b, n, w = t.shape
    return t.reshape(b, n, n_heads, w // n_heads).transpose(0, 2, 1, 3)

def from_heads(t):
    b, h, n, d = t.shape
    return t.transpose(0, 2, 1, 3).reshape(b, n, h * d)

def ada_mod(cvec, w_ada, b_ada):
    m = jax.nn.silu(cvec) @ w_ada + b_ada
    return jnp.split(m[..., None, :], 6, axis=-1)

def gla_chunked(q, k, v, log_a, s0):
    b, h, n, dk = q.shape
    dv = v.shape[-1]
    nc = n // GLA_CHUNK
    q = q.reshape(b, h, nc, GLA_CHUNK, dk)
    k = k.reshape(b, h, nc, GLA_CHUNK, dk)
    v = v.reshape(b, h, nc, GLA_CHUNK, dv)
    bc = jnp.cumsum(log_a.reshape(b, h, nc, GLA_CHUNK, dk), axis=3)
    causal = np.tril(np.ones((GLA_CHUNK, GLA_CHUNK), dtype=bool))[:, :, None]
    diff = bc[:, :, :, :, None, :] - bc[:, :, :, None, :, :]
    decay = jnp.exp(jnp.where(causal, diff, -jnp.inf))
    attn = jnp.sum(q[:, :, :, :, None, :] * k[:, :, :, None, :, :] * decay, axis=-1)
    o_intra = jnp.einsum('bhnij,bhnjv->bhniv', attn, v)
    b_last = bc[:, :, :, -1:, :]
    u = jnp.einsum('bhncd,bhncv->bhndv', k * jnp.exp(b_last - bc), v)
    g = jnp.exp(b_last[:, :, :, 0, :])

    def step(s, inp):
        g_n, u_n = inp
        return g_n[..., None] * s + u_n, s

    s_fin, s_prev = lax.scan(step, s0, (jnp.moveaxis(g, 2, 0), jnp.moveaxis(u, 2, 0)))
    s_prev = jnp.moveaxis(s_prev, 0, 2)
    o_inter = jnp.einsum('bhncd,bhndv->bhncv', q * jnp.exp(bc), s_prev)
    return (o_intra + o_inter).reshape(b, h, n, dv), s_fin

def gla_mixer(gq, gk, gv, gg, glr, w_gk, b_gk, out_norm, s0):
    f32 = jnp.float32
    b, n, _ = gq.shape
    q = to_heads(gq, GLA_HEADS).astype(f32) * GLA_DK ** -0.5
    k = to_heads(gk, GLA_HEADS).astype(f32)
    v = to_heads(gv, GLA_HEADS).astype(f32)
    lr = glr.reshape(b, n, 2, GLA_GATE_RANK).astype(f32)
    z = jnp.einsum('bnsr,srk->bnsk', lr, w_gk.astype(f32)) + b_gk.astype(f32)
    log_a = jax.nn.log_sigmoid(z) / GLA_GATE_NORM
    la_f = to_heads(log_a[:, :, 0], GLA_HEADS)
    la_b = to_heads(log_a[:, :, 1], GLA_HEADS)
    s0 = s0.astype(f32)
    o_f, s_f = gla_chunked(q, k, v, la_f, s0[:, 0])
    flip = lambda t: jnp.flip(t, axis=2)
    o_b, s_b = gla_chunked(flip(q), flip(k), flip(v), flip(la_b), s0[:, 1])
    o = rms_norm(o_f + flip(o_b), out_norm)
    out = from_heads(o) * jax.nn.silu(gg.astype(f32))
    return out.astype(gq.dtype), jnp.stack([s_f, s_b], axis=1).astype(gq.dtype)

def conv_module(a, dw_w, dw_b, ln_g, ln_b, w_pw):
    h = a[..., :CONV_CH] * jax.nn.sigmoid(a[..., CONV_CH:])
    pad = CONV_WIDTH // 2
    h = lax.conv_general_dilated(h, dw_w[:, None, :], window_strides=(1,), padding=[(pad, pad)],
                                 dimension_numbers=('NWC', 'WIO', 'NWC'), feature_group_count=CONV_CH) + dw_b
    h = jax.nn.silu(layer_norm(h, ln_g, ln_b))
    return h @ w_pw

def attend_dense(q, k, v):
    s = jnp.einsum('bhnd,bhld->bhnl', q, k).astype(jnp.float32) * NA_HD ** -0.5
    p = jax.nn.softmax(s, axis=-1).astype(v.dtype)
    return jnp.einsum('bhnl,bhld->bhnd', p, v)

def neighborhood_attention(q, k, v, k_ctx, v_ctx, rpb):
    b, nh, n, d = q.shape
    rows = n // GRID_W
    kr = min(NA_WIN_ROWS, rows)
    nb = GRID_W // NA_QBLOCK
    kw = kr * NA_KBLOCK
    r = np.arange(rows)
    key_rows = np.clip(r - kr // 2, 0, rows - kr)[:, None] + np.arange(kr)[None, :]
    blk = np.arange(nb)
    key_cols = np.clip(blk * NA_QBLOCK - NA_WIN_COLS // 2, 0, GRID_W - NA_KBLOCK)[:, None] + np.arange(NA_KBLOCK)[None, :]
    kidx = (key_rows[:, None, :, None] * GRID_W + key_cols[None, :, None, :]).reshape(rows, nb, kw)
    kg = k[:, :, kidx]
    vg = v[:, :, kidx]
    q_cols = blk[:, None] * NA_QBLOCK + np.arange(NA_QBLOCK)[None, :]
    win_start = np.clip(q_cols - NA_WIN_COLS // 2, 0, GRID_W - NA_WIN_COLS)
    kc = key_cols[:, None, :]
    in_win = (kc >= win_start[:, :, None]) & (kc < win_start[:, :, None] + NA_WIN_COLS)
    mask = np.broadcast_to(in_win[:, :, None, :], (nb, NA_QBLOCK, kr, NA_KBLOCK)).reshape(nb, NA_QBLOCK, kw)
    row_off = key_rows - r[:, None] + NA_WIN_ROWS - 1
    col_off = np.clip(kc - q_cols[:, :, None] + NA_WIN_COLS - 1, 0, 2 * NA_WIN_COLS - 2)
    bias = rpb[:, row_off[:, :, None, None, None], col_off[None, None, :, :, :]]
    bias = bias.transpose(0, 1, 3, 4, 2, 5).reshape(nh, rows, nb, NA_QBLOCK, kw).astype(jnp.float32)
    scale = NA_HD ** -0.5
    qb = q.reshape(b, nh, rows, nb, NA_QBLOCK, d)
    s_loc = jnp.einsum('bhrnqd,bhrnkd->bhrnqk', qb, kg).astype(jnp.float32) * scale + bias[None]
    s_loc = jnp.where(mask, s_loc, -jnp.inf)
    s_ctx = jnp.einsum('bhrnqd,bhld->bhrnql', qb, k_ctx).astype(jnp.float32) * scale
    p = jax.nn.softmax(jnp.concatenate([s_loc, s_ctx], axis=-1), axis=-1).astype(v.dtype)
    o = (jnp.einsum('bhrnqk,bhrnkd->bhrnqd', p[..., :kw], vg)
         + jnp.einsum('bhrnql,bhld->bhrnqd', p[..., kw:], v_ctx))
    return o.reshape(b, nh, n, d)

def moe(h, router_w, router_bias, w_gate, w_up, w_down, sh_gate, sh_up, sh_down):
    b, n, d = h.shape
    per_group = N_EXPERTS // N_GROUPS

    def block(t):
        scores = jax.nn.sigmoid((t @ router_w).astype(jnp.float32))
        biased = scores + router_bias.astype(jnp.float32)
        grp_score = jnp.sum(lax.top_k(biased.reshape(-1, N_GROUPS, per_group), 2)[0], axis=-1)
        top_grp = lax.top_k(grp_score, TOPK_GROUPS)[1]
        grp_keep = jnp.sum(jax.nn.one_hot(top_grp, N_GROUPS, dtype=jnp.float32), axis=1) > 0
        masked = jnp.where(jnp.repeat(grp_keep, per_group, axis=-1), biased, -jnp.inf)
        top_e = lax.top_k(masked, TOP_K)[1]
        sel = jnp.take_along_axis(scores, top_e, axis=-1)
        wts = sel / jnp.sum(sel, axis=-1, keepdims=True) * ROUTED_SCALE
        gate = jnp.einsum('tk,tke->te', wts, jax.nn.one_hot(top_e, N_EXPERTS, dtype=jnp.float32)).astype(t.dtype)
        act = jax.nn.silu(jnp.einsum('td,edf->tef', t, w_gate)) * jnp.einsum('td,edf->tef', t, w_up)
        routed = jnp.einsum('tef,efd->td', act * gate[:, :, None], w_down)
        shared = (jax.nn.silu(t @ sh_gate) * (t @ sh_up)) @ sh_down
        return routed + shared

    y = lax.map(block, h.reshape(-1, MOE_BLOCK, d))
    return y.reshape(b, n, d)

def trunk_layer(x, cvec, lw, gla_s0, k_ctx, v_ctx):
    sh1, sc1, g1, sh2, sc2, g2 = ada_mod(cvec, lw['w_ada'], lw['b_ada'])
    h = rms_norm(x, lw['norm_mix']) * (1 + sc1) + sh1
    split_points = [int(s) for s in np.cumsum(IN_SPLITS)[:-1]]
    gq, gk, gv, gg, glr, conv_in, nq, nk, nv = jnp.split(h @ lw['w_in'], split_points, axis=-1)
    gla_o, gla_state = gla_mixer(gq, gk, gv, gg, glr, lw['gla_w_gate'], lw['gla_b_gate'], lw['gla_out_norm'], gla_s0)
    conv_o = conv_module(conv_in, lw['conv_dw'], lw['conv_dw_b'], lw['conv_ln_g'], lw['conv_ln_b'], lw['conv_pw'])
    q = rms_norm(to_heads(nq, NA_HEADS), lw['na_q_norm'])
    k = rms_norm(to_heads(nk, NA_HEADS), lw['na_k_norm'])
    v = to_heads(nv, NA_HEADS)
    if k_ctx is None:
        na = attend_dense(q, k, v)
    else:
        na = neighborhood_attention(q, k, v, k_ctx, v_ctx, lw['na_rpb'])
    mix = jnp.concatenate([gla_o, conv_o, from_heads(na)], axis=-1) @ lw['w_out']
    x = x + g1 * mix
    h = rms_norm(x, lw['norm_ffn']) * (1 + sc2) + sh2
    x = x + g2 * moe(h, lw['router_w'], lw['router_bias'], lw['exp_w_gate'], lw['exp_w_up'], lw['exp_w_down'],
                     lw['sh_w_gate'], lw['sh_w_up'], lw['sh_w_down'])
    return x, gla_state, k, v

def setup_inputs(seed: int = 0) -> dict:
    key = jax.random.key(seed)
    keys = iter(jax.random.split(key, 40))

    def rnd(shape, scale):
        return jax.random.normal(next(keys), shape, jnp.float32) * scale

    L = DEPTH
    return {
        'x_prompt': rnd((BATCH, SEQ, D_MODEL), 1.0),
        'x_sample': rnd((DEC_BATCH, DEC_SEQ, D_MODEL), 1.0),
        'state_gla': rnd((DEC_BATCH, DEPTH, 2, GLA_HEADS, GLA_DK, GLA_DV), 0.3),
        'cache_na_k': rnd((DEC_BATCH, DEPTH, NA_HEADS, PAST_LEN, NA_HD), 1.0),
        'cache_na_v': rnd((DEC_BATCH, DEPTH, NA_HEADS, PAST_LEN, NA_HD), 1.0),
        'c': rnd((DEC_BATCH, D_MODEL), 1.0),
        'c_ctx': rnd((D_MODEL,), 1.0),
        'w_ada': rnd((L, D_MODEL, 6 * D_MODEL), 0.5 * D_MODEL ** -0.5),
        'b_ada': rnd((L, 6 * D_MODEL), 0.01),
        'norm_mix': 1.0 + rnd((L, D_MODEL), 0.01),
        'norm_ffn': 1.0 + rnd((L, D_MODEL), 0.01),
        'w_in': rnd((L, D_MODEL, IN_WIDTH), D_MODEL ** -0.5),
        'gla_w_gate': rnd((L, 2, GLA_GATE_RANK, GLA_KEY), GLA_GATE_RANK ** -0.5),
        'gla_b_gate': rnd((L, 2, GLA_KEY), 0.1),
        'gla_out_norm': 1.0 + rnd((L, GLA_DV), 0.01),
        'conv_dw': rnd((L, CONV_WIDTH, CONV_CH), CONV_WIDTH ** -0.5),
        'conv_dw_b': rnd((L, CONV_CH), 0.01),
        'conv_ln_g': 1.0 + rnd((L, CONV_CH), 0.01),
        'conv_ln_b': rnd((L, CONV_CH), 0.01),
        'conv_pw': rnd((L, CONV_CH, CONV_CH), CONV_CH ** -0.5),
        'na_q_norm': 1.0 + rnd((L, NA_HD), 0.01),
        'na_k_norm': 1.0 + rnd((L, NA_HD), 0.01),
        'na_rpb': rnd((L, NA_HEADS, 2 * NA_WIN_ROWS - 1, 2 * NA_WIN_COLS - 1), 0.1),
        'w_out': rnd((L, MIX_WIDTH, D_MODEL), MIX_WIDTH ** -0.5),
        'router_w': rnd((L, D_MODEL, N_EXPERTS), D_MODEL ** -0.5),
        'router_bias': rnd((L, N_EXPERTS), 0.01),
        'exp_w_gate': rnd((L, N_EXPERTS, D_MODEL, EXPERT_DIM), D_MODEL ** -0.5),
        'exp_w_up': rnd((L, N_EXPERTS, D_MODEL, EXPERT_DIM), D_MODEL ** -0.5),
        'exp_w_down': rnd((L, N_EXPERTS, EXPERT_DIM, D_MODEL), EXPERT_DIM ** -0.5),
        'sh_w_gate': rnd((L, D_MODEL, SHARED_DIM), D_MODEL ** -0.5),
        'sh_w_up': rnd((L, D_MODEL, SHARED_DIM), D_MODEL ** -0.5),
        'sh_w_down': rnd((L, SHARED_DIM, D_MODEL), SHARED_DIM ** -0.5),
    }

def reference(x_prompt, x_sample, state_gla, cache_na_k, cache_na_v, c, c_ctx, w_ada, b_ada, norm_mix, norm_ffn,
              w_in, gla_w_gate, gla_b_gate, gla_out_norm, conv_dw, conv_dw_b, conv_ln_g, conv_ln_b, conv_pw,
              na_q_norm, na_k_norm, na_rpb, w_out, router_w, router_bias, exp_w_gate, exp_w_up, exp_w_down,
              sh_w_gate, sh_w_up, sh_w_down):
    y_prompt = x_prompt
    y_sample = x_sample
    gla_states, ctx_keys, ctx_vals = [], [], []
    zero_state = jnp.zeros((x_prompt.shape[0], 2, GLA_HEADS, GLA_DK, GLA_DV), x_prompt.dtype)
    for l in range(DEPTH):
        lw = dict(w_ada=w_ada[l], b_ada=b_ada[l], norm_mix=norm_mix[l], norm_ffn=norm_ffn[l], w_in=w_in[l],
                  gla_w_gate=gla_w_gate[l], gla_b_gate=gla_b_gate[l], gla_out_norm=gla_out_norm[l],
                  conv_dw=conv_dw[l], conv_dw_b=conv_dw_b[l], conv_ln_g=conv_ln_g[l], conv_ln_b=conv_ln_b[l],
                  conv_pw=conv_pw[l], na_q_norm=na_q_norm[l], na_k_norm=na_k_norm[l], na_rpb=na_rpb[l],
                  w_out=w_out[l], router_w=router_w[l], router_bias=router_bias[l], exp_w_gate=exp_w_gate[l],
                  exp_w_up=exp_w_up[l], exp_w_down=exp_w_down[l], sh_w_gate=sh_w_gate[l], sh_w_up=sh_w_up[l],
                  sh_w_down=sh_w_down[l])
        y_prompt, s_l, k_l, v_l = trunk_layer(y_prompt, c_ctx, lw, zero_state, None, None)
        gla_states.append(s_l)
        ctx_keys.append(k_l)
        ctx_vals.append(v_l)
        y_sample, _, _, _ = trunk_layer(y_sample, c, lw, state_gla[:, l], cache_na_k[:, l], cache_na_v[:, l])
    new_state_gla = jnp.stack(gla_states, axis=1)
    new_cache_na_k = jnp.stack(ctx_keys, axis=1)
    new_cache_na_v = jnp.stack(ctx_vals, axis=1)
    return (y_prompt, y_sample, new_state_gla, new_cache_na_k, new_cache_na_v)


_drawn_inputs = setup_inputs


def setup_inputs(seed=0):
    import zlib

    import numpy as np

    out = dict(_drawn_inputs(seed))
    spreads = {}
    factors = {'state_gla': 16.096,
     'norm_mix': 2.793,
     'gla_out_norm': 17.209,
     'conv_dw_b': 8.201,
     'conv_ln_g': 76.699,
     'conv_ln_b': 87.179,
     'na_q_norm': 8.0,
     'na_k_norm': 21.453,
     'na_rpb': 37.144,
     'cache_na_k': 8.0,
     'cache_na_v': 8.0,
     'norm_ffn': 5.349}
    for name, (base, spread) in spreads.items():
        noise = np.random.default_rng([zlib.crc32(name.encode()), seed]).standard_normal(out[name].shape)
        drawn = base * np.exp(spread * noise) if base else spread * noise
        out[name] = __import__('jax').numpy.asarray(drawn.astype(out[name].dtype))
    for name, factor in factors.items():
        out[name] = (out[name] * factor).astype(out[name].dtype)
    return out
```

```python
import concourse.bass as bass
from concourse import mybir

F32 = mybir.dt.float32
BF16 = mybir.dt.bfloat16
ALU = mybir.AluOpType
ACT = mybir.ActivationFunctionType
AX = mybir.AxisListType

P = 128
D = 1024
KT = D // P
DEPTH = 2
STREAMS = 2
HEADS = 4
DK = 64
DV = 128
PAIRS = HEADS // 2
RANK = 16
CONV_CH = 256
TAPS = 31
HALO = TAPS // 2
GRID_W = 64
WIN_ROWS = 8
WIN_COLS = 16
RPB_COLS = 2 * WIN_COLS - 1
RPB_HEAD = (2 * WIN_ROWS - 1) * RPB_COLS
IN_WIDTH = 2848
EXPERTS = 64
GROUPS = 8
PER_GROUP = EXPERTS // GROUPS
TOP_K = 8
TOP_GROUPS = 4
FF = 256
ROUTED_SCALE = 2.5
EPS = 1e-6
LEVELS = 7
NEVER = -1e30

SLOTS = 4
SLOT = 3 * KT * FF
ADA_CHUNKS = 12
IN_CHUNKS = [(1536, 544), (0, 512), (512, 512), (2080, 768), (1024, 512)]
OUT_CHUNKS = 2
PRE = ADA_CHUNKS + len(IN_CHUNKS) + OUT_CHUNKS + 1
PRE_SLOTS = 3

C_IN = ADA_CHUNKS
C_OUT = C_IN + len(IN_CHUNKS)
C_SH = PRE - 1

UNITS_IN = [(0, 0, 2 * RANK, True, None)] + [(0, 2 * RANK + P * j, P, True, None) for j in range(4)]
UNITS_IN += [(1, P * j, P, True, None) for j in range(4)]
UNITS_IN += [(2, 0, 512, False, st) for st in range(STREAMS)]
UNITS_IN += [(3, c0, w, False, st) for st in range(STREAMS) for c0, w in ((0, 512), (512, 256))]
UNITS_IN += [(4, 0, 512, False, st) for st in range(STREAMS)]
LAST_UNIT = [max(u for u, unit in enumerate(UNITS_IN) if unit[0] == c) for c in range(len(IN_CHUNKS))]
PROJ_BANKS = (2, 3, 6, 7)
STORES = 4
STEPS = 2 * SLOTS

R_DW, R_DWB, R_LNG, R_LNB, R_ON, R_QN, R_KN, R_END = 0, 31, 32, 33, 34, 35, 36, 37


SIGNALS = """x_loaded const_step c_sig c_step small_in vec_in norm_in attn_in shared_in chunk_in0 chunk_in1 chunk_in2
expert_in0 expert_in1 expert_in2 expert_in3 act_step dve_step ada_done ada_kept bias_in square_done var_ready
root_ready mod_shown h_ready hT_shown hT_ready vec_shown vec_ready proj_done proj_kept z_shown la_log la_ready conv_sig
tap conv_ready convT_shown ctok_ready convB_shown conv_neg cact_ready pw_shown cat_conv nq_ready kco_ready nT_shown
nT_ready bias_ready scores_shown max_ready p_exp p_ready pT_shown pT_ready pv_shown cat_na gg_sig decay_shown
E_ready X_ready pair_shown masked att_ready o_shown go_ready goT_shown cat_gla st_pre st_exp kd_ready st_shown st_kept
mix_shown x_mid logits_shown scored g2_shown g2_kept gu_done silu_done act_done actT_shown actT_kept
down_done stored y_out""".split()


def rpb_window(rpb, layer, head, half):
    flat = rpb.rearrange("l h r c -> l (h r c)")
    first = head * RPB_HEAD + (WIN_ROWS - 2 + half) * RPB_COLS + (WIN_COLS - 1) - (GRID_W - 1)
    row = flat[layer, first:first + 1]
    ap = [list(d) for d in row.ap]
    return bass.AP(row.tensor, row.offset, [[1, GRID_W], [RPB_COLS, 2], [1, GRID_W]])


def expert_slot(e):
    return (e + 2) % SLOTS


def build(nc, A):
    def sb(name, shape, dt=F32):
        return nc.alloc_sbuf_tensor(name, shape, dt)

    s = {name: nc.alloc_semaphore(name) for name in SIGNALS}

    ring = sb("ring", [P, SLOTS, SLOT])
    x = sb("x", [P, STREAMS, D])
    ada = sb("ada", [P, ADA_CHUNKS, P])
    h = sb("h", [P, STREAMS, D])
    gbc = sb("gbc", [P, D])
    hT = sb("hT", [P, KT, STREAMS * P])
    qT = sb("qT", [P, PAIRS, STREAMS * P])
    kT = sb("kT", [P, PAIRS, STREAMS * P])
    v = sb("v", [P, STREAMS, HEADS * DV])
    gg = sb("gg", [P, STREAMS, HEADS * DV])
    lrT = sb("lrT", [33, STREAMS * P])
    la = sb("la", [P, STREAMS, 2, HEADS * DK])
    ci = sb("ci", [P, 4, STREAMS * P])
    nax = sb("nax", [P, STREAMS, 3 * HEADS * DK])
    cat = sb("cat", [P, KT, STREAMS * P])
    sm = sb("sm", [P, 256])
    ident = sb("ident", [P, P])
    flip = sb("flip", [P, P])
    pick = sb("pick", [P, 4, STREAMS, P])
    mf = sb("mf", [P, LEVELS + 1, P])
    mb = sb("mb", [P, LEVELS + 1, P])
    suf = sb("suf", [P, 2, P])
    maskf = sb("maskf", [P, LEVELS + 1, P], BF16)
    maskb = sb("maskb", [P, LEVELS, P], BF16)
    maskr = sb("maskr", [P, P])
    tri8 = sb("tri8", [P, GROUPS, GROUPS])
    zero = sb("zero", [P, P])
    cs = sb("cs", [P, KT, 32])
    craw = sb("craw", [P, 3, 2, KT])
    vec = sb("vec", [R_END, CONV_CH])
    vecT = sb("vecT", [P, 2, R_END])
    wg = sb("wg", [33, 2 * HEADS * DK])
    s0 = sb("s0", [P, 2, HEADS, DV])
    gk = sb("gk", [P, DK])
    wpw = sb("wpw", [P, 2, CONV_CH])
    wr = sb("wr", [P, KT, EXPERTS])
    rbias = sb("rbias", [P, EXPERTS])
    hpad = sb("hpad", [P, 2, STREAMS, P + 2 * HALO])
    gate = sb("gate", [P, STREAMS, EXPERTS + 1])

    class Scratch:
        def __init__(self, base):
            self.base, self.at = base, 0

        def take(self, n):
            self.at += n
            return self.base[:, self.at - n:self.at]

    arena = Scratch(ring[:, 3, :])
    cacc = arena.take(512).rearrange("p (c s t) -> p c s t", c=2, s=2)
    csig = arena.take(512).rearrange("p (c n) -> p c n", c=2)
    biasr = arena.take(512).rearrange("p (h k) -> p h k", h=HEADS)
    kvc = arena.take(512).rearrange("p (a n) -> p a n", a=2)
    kcT = arena.take(256).rearrange("p (a n) -> p a n", a=PAIRS)
    qnT = arena.take(512).rearrange("p (a n) -> p a n", a=PAIRS)
    knT = arena.take(512).rearrange("p (a n) -> p a n", a=PAIRS)
    p0 = arena.take(512).rearrange("p (h k) -> p h k", h=HEADS)
    p1 = arena.take(1024).rearrange("p (h k) -> p h k", h=HEADS)
    kd = arena.take(512).rearrange("p (a n) -> p a n", a=2)
    kco = arena.take(HEADS * DK)
    att = p0.rearrange("p (b e) i -> p b e i", b=2)
    att2 = p1[:, 0, :]
    qd = p1[:, 2:4, :].rearrange("p b (r i) -> p b r i", r=2)
    assert arena.at <= SLOT
    sq = h[:, :, :].rearrange("p s n -> p (s n)")[:, 0:1024].rearrange("p (s n) -> p s n", s=2)
    nq = h[:, :, :].rearrange("p s n -> p (s n)")[:, 1024:2048].rearrange("p (s n) -> p s n", s=2)
    pT = hT[:, :, :].rearrange("p k n -> p (k n)")[:, 0:12 * P].rearrange("p (b n) -> p b n", n=P)
    E = h[:, :, :].rearrange("p s (l n) -> p s l n", n=P)
    X = hT[:, :, :].rearrange("p k n -> p (k n)").rearrange("p (b l n) -> p b l n", b=2, n=P)
    tm = sb("tm", [P, LEVELS + 1, P])
    hflat = h[:, :, :].rearrange("p s n -> p (s n)")
    cTok = tm[:, 0:4, :].rearrange("p (s a) n -> p s (a n)", s=2)
    cSq = tm[:, 4:8, :].rearrange("p (s a) n -> p s (a n)", s=2)
    g2 = cat[:, :, :].rearrange("p k n -> p (k n)").rearrange("p (s n) -> p s n", s=2)
    silu = qT[:, :, :]
    acts = kT[:, :, :]
    actT = v[:, :, 0:FF]
    naf = nax[:].rearrange("p s n -> p (s n)")
    scores = naf[:, 0:128].rearrange("p (s n) -> p s n", s=2)
    biased = naf[:, 128:256].rearrange("p (s n) -> p s n", s=2)
    chosen = naf[:, 256:384].rearrange("p (s n) -> p s n", s=2)
    top = naf[:, 384:512].rearrange("p (s g n) -> p s g n", s=2, n=8)
    beats = naf[:, 512:640].rearrange("p (b g n) -> p b g n", b=2, n=8)
    grp = naf[:, 640:656].rearrange("p (s g) -> p s g", s=2)
    rank, best, tot = naf[:, 656:664], naf[:, 664:672], naf[:, 672:673]
    ps = nc.alloc_psum_tensor("ps", [P, 8, 512], F32)

    def bank(b, lo=0, hi=512):
        return ps[:, b, lo:hi]

    with nc.Block() as block:
        @block.gpsimd
        def _(pool):
            count = [0]

            def link(ins):
                count[0] += 1
                ins.then_inc(s["const_step"], 1)
                pool.wait_ge(s["const_step"], count[0])

            def keep(view, cond, fill, base, pattern, mult):
                link(nc.gpsimd.affine_select(out=view, in_=view, compare_op=cond, fill=fill, base=base,
                                             pattern=pattern, channel_multiplier=mult))

            for t, val in ((ident, 0.0), (flip, 0.0), (pick, 0.0), (mf, 1.0), (mb, 1.0), (suf, 1.0), (maskf, 1.0),
                           (maskb, 1.0), (maskr, 0.0), (tri8, 1.0), (zero, 0.0), (cs, 0.0), (s0, 0.0), (wg, 0.0),
                           (lrT, 1.0), (hpad, 0.0), (gate, 1.0)):
                link(nc.gpsimd.memset(t[:], val))
            keep(ident[:], ALU.not_equal, 1.0, 0, [[-1, P]], 1)
            keep(flip[:], ALU.not_equal, 1.0, -(P - 1), [[1, P]], 1)
            for c in range(4):
                for st in range(STREAMS):
                    keep(pick[:, c, st, :], ALU.not_equal, 1.0, -(32 * c + st), [[0, P]], 1)
                    keep(pick[:, c, st, :], ALU.not_equal, 1.0, -(32 * c + 2), [[0, P]], 1)
            for lv in range(LEVELS):
                w = P >> (lv + 1)
                nb = P // (2 * w)
                early = [t[:, lv, :].rearrange("p (b a r) -> p b a r", a=2, r=w)[:, :, 0, :] for t in (mf, mb, maskf, maskb)]
                late = [t[:, lv, :].rearrange("p (b a r) -> p b a r", a=2, r=w)[:, :, 1, :] for t in (mf, mb, maskf, maskb)]
                blocks = [[-2 * w, nb], [0, w]]
                blocks_up = [[2 * w, nb], [0, w]]
                tok = [[-2 * w, nb], [-1, w]]
                tok_up = [[2 * w, nb], [1, w]]
                keep(late[0], ALU.is_ge, 0.0, -w, blocks, 1)
                keep(late[0], ALU.is_ge, 0.0, w, tok_up, -1)
                keep(early[0], ALU.is_ge, 0.0, -1, tok, 1)
                keep(early[0], ALU.is_ge, 0.0, w - 1, blocks_up, -1)
                keep(early[1], ALU.is_ge, 0.0, 0, tok, 1)
                keep(early[1], ALU.is_ge, 0.0, w - 1, blocks_up, -1)
                keep(late[1], ALU.is_ge, 0.0, -w, blocks, 1)
                keep(late[1], ALU.is_ge, 0.0, w - 1, tok_up, -1)
                keep(late[2], ALU.is_ge, 0.0, 0, blocks, 1)
                keep(late[2], ALU.is_ge, 0.0, w - 1, blocks_up, -1)
                link(nc.gpsimd.memset(early[2], 0.0))
                keep(early[3], ALU.is_ge, 0.0, -w, blocks, 1)
                keep(early[3], ALU.is_ge, 0.0, 2 * w - 1, blocks_up, -1)
                link(nc.gpsimd.memset(late[3], 0.0))
            keep(mf[:, LEVELS, :], ALU.is_ge, 0.0, 0, [[1, P]], -1)
            keep(mb[:, LEVELS, :], ALU.is_ge, 0.0, 0, [[-1, P]], 1)
            keep(suf[:, 0, :], ALU.is_ge, 0.0, -1, [[-1, P]], 1)
            keep(suf[:, 1, :], ALU.is_ge, 0.0, -1, [[1, P]], -1)
            link(nc.gpsimd.memset(maskf[:, LEVELS, :], 0.0))
            keep(maskf[:, LEVELS, :], ALU.not_equal, 2.0, 0, [[-1, P]], 1)
            for half in range(2):
                rows = maskr[64 * half:64 * half + 64, :].rearrange("p (r k) -> p r k", k=GRID_W)
                link(nc.gpsimd.affine_select(out=rows[:, :, 0:48], in_=rows[:, :, 0:48], compare_op=ALU.is_ge,
                                             fill=NEVER, base=-(GRID_W - 1 - 8), pattern=[[0, 2], [1, 48]],
                                             channel_multiplier=1))
                link(nc.gpsimd.affine_select(out=rows[:, :, 16:64], in_=rows[:, :, 16:64], compare_op=ALU.is_ge,
                                             fill=NEVER, base=GRID_W - 1 + 7 - 16, pattern=[[0, 2], [-1, 48]],
                                             channel_multiplier=-1))
            keep(tri8[:], ALU.is_ge, 0.0, -1, [[1, GROUPS], [-1, GROUPS]], 0)

        @block.sync
        def _(sp):
            for st, name in ((0, "x_prompt"), (1, "x_sample")):
                sp.dma_start(x[:, st, :], A[name][0]).then_inc(s["x_loaded"], 16)
            sp.dma_start(craw[:, 0, 0, :], A["c_ctx"].rearrange("(p k) -> p k", k=KT)).then_inc(s["x_loaded"], 16)
            sp.dma_start(craw[:, 0, 1, :], A["c"][0].rearrange("(p k) -> p k", k=KT)).then_inc(s["x_loaded"], 16)
            sp.wait_ge(s["x_loaded"], 64)

        @block.scalar
        def _(act):
            act.wait_ge(s["x_loaded"], 64)
            nc.scalar.activation(craw[:, 1], craw[:, 0], ACT.Sigmoid).then_inc(s["c_sig"], 1)

        @block.vector
        def _(dve):
            dve.wait_ge(s["c_sig"], 1)
            dve.wait_ge(s["const_step"], 17)
            nc.vector.tensor_tensor(cs[:, :, 0:2].rearrange("p k s -> p s k"), craw[:, 0], craw[:, 1],
                                    ALU.mult).then_inc(s["c_step"], 1)

    def dma_in(eng, out, in_, sem):
        eng.dma_start(out, in_).then_inc(sem, 16)

    def pre_slot(n):
        return n % PRE_SLOTS

    def pre_loaded(eng, n):
        eng.wait_ge(chunk_in[pre_slot(n)], 16 * (n // PRE_SLOTS + 1))

    def load_expert(eng, slot, weights, sem):
        gate_w, up_w, down_w = weights
        for j, w in enumerate((gate_w, up_w)):
            dma_in(eng, slot[:, KT * FF * j:KT * FF * (j + 1)].rearrange("p (k n) -> p k n", k=KT),
                   w.rearrange("(p k) n -> p k n", k=KT), sem)
        dma_in(eng, slot[:, 2 * KT * FF:SLOT].rearrange("p (j n) -> p j n", j=2),
               down_w.rearrange("(p j) n -> p j n", j=2), sem)

    def gate_up(slot, k):
        return slot[:, 0:2 * KT * FF].rearrange("p (a k n) -> p a k n", a=2, k=KT)[:, :, k, :]

    def down(slot, j, half):
        return slot[:, 2 * KT * FF:SLOT].rearrange("p (j n) -> p j n", j=2)[:, j, 512 * half:512 * (half + 1)]

    def chunk_used(eng, n):
        if n < C_IN:
            eng.wait_ge(s["ada_done"], n + 1)
        elif n < C_OUT:
            eng.wait_ge(s["proj_done"], LAST_UNIT[n - C_IN] + 1)
        elif n < C_SH:
            eng.wait_ge(s["mix_shown"], 2 * (n - C_OUT + 1))
        else:
            eng.wait_ge(s["down_done"], 1 + STREAMS)

    chunk_in = [s["chunk_in0"], s["chunk_in1"], s["chunk_in2"]]
    expert_in = [s["expert_in0"], s["expert_in1"], s["expert_in2"], s["expert_in3"]]
    N_SMALL, N_VEC, N_ATTN = 18, 8, 2 * HEADS + 2

    layers = nc.Fori(0, DEPTH)
    layer = layers.__enter__()
    with nc.Block() as block:
        @block.sync
        def _(sp):
            for r0, r1, name in ((R_DW, R_DWB, "conv_dw"),):
                dma_in(sp, vec[r0:r1, :], A[name][layer], s["small_in"])
            for r, name in ((R_DWB, "conv_dw_b"), (R_LNG, "conv_ln_g"), (R_LNB, "conv_ln_b")):
                dma_in(sp, vec[r:r + 1, :], A[name][bass.ds(layer, 1), :], s["small_in"])
            dma_in(sp, vec[R_ON:R_ON + 1, 0:DV], A["gla_out_norm"][bass.ds(layer, 1), :], s["small_in"])
            dma_in(sp, vec[R_ON:R_ON + 1, DV:2 * DV], A["gla_out_norm"][bass.ds(layer, 1), :], s["small_in"])
            for r, name in ((R_QN, "na_q_norm"), (R_KN, "na_k_norm")):
                for j in range(CONV_CH // DK):
                    dma_in(sp, vec[r:r + 1, DK * j:DK * (j + 1)], A[name][bass.ds(layer, 1), :], s["vec_in"])
            dma_in(sp, gbc[:], A["norm_mix"][bass.ds(layer, 1), :].partition_broadcast(P)[:, 0, :], s["norm_in"])
            dma_in(sp, gk[:], A["na_k_norm"][bass.ds(layer, 1), :].partition_broadcast(P)[:, 0, :], s["small_in"])
            for dr in range(2):
                dma_in(sp, wg[RANK * dr:RANK * (dr + 1), 256 * dr:256 * (dr + 1)],
                       A["gla_w_gate"][layer, dr], s["small_in"])
                dma_in(sp, wg[32:33, 256 * dr:256 * (dr + 1)],
                       A["gla_b_gate"][layer, dr:dr + 1, :], s["small_in"])
                for e in range(2):
                    dma_in(sp, s0[DK * e:DK * (e + 1), dr, e::2, :],
                           A["state_gla"][0, layer, dr, e::2].rearrange("h d v -> d h v"), s["small_in"])
            dma_in(sp, wpw[:], A["conv_pw"][layer].rearrange("(c p) n -> p c n", p=P), s["small_in"])
            dma_in(sp, wr[:], A["router_w"][layer].rearrange("(p k) n -> p k n", k=KT), s["small_in"])
            dma_in(sp, rbias[:], A["router_bias"][bass.ds(layer, 1), :].partition_broadcast(P)[:, 0, :], s["small_in"])
            for n in range(PRE):
                if n >= PRE_SLOTS:
                    chunk_used(sp, n - PRE_SLOTS)
                slot = ring[:, pre_slot(n), :]
                sem = chunk_in[pre_slot(n)]
                if n < C_IN:
                    dma_in(sp, slot[:, 0:KT * 512].rearrange("p (k n) -> p k n", k=KT),
                           A["w_ada"][layer, :, 512 * n:512 * (n + 1)].rearrange("(p k) n -> p k n", k=KT), sem)
                elif n < C_OUT:
                    c0, cw = IN_CHUNKS[n - C_IN]
                    dma_in(sp, slot[:, 0:KT * cw].rearrange("p (k n) -> p k n", k=KT),
                           A["w_in"][layer, :, c0:c0 + cw].rearrange("(p k) n -> p k n", k=KT), sem)
                elif n < C_SH:
                    c0 = 512 * (n - C_OUT)
                    dma_in(sp, slot[:, 0:KT * 512].rearrange("p (k n) -> p k n", k=KT),
                           A["w_out"][layer, :, c0:c0 + 512].rearrange("(k p) n -> p k n", p=P), sem)
                else:
                    load_expert(sp, slot, [A[w][layer] for w in ("sh_w_gate", "sh_w_up", "sh_w_down")], s["shared_in"])
                if n == C_IN + PRE_SLOTS:
                    sp.wait_ge(s["h_ready"], STREAMS)
                    dma_in(sp, gbc[:], A["norm_ffn"][bass.ds(layer, 1), :].partition_broadcast(P)[:, 0, :], s["norm_in"])
                if n == PRE_SLOTS + 1:
                    for half in range(2):
                        for hh in range(HEADS):
                            sp.dma_start(
                                biasr[64 * half:64 * (half + 1), hh, :].rearrange("p (r k) -> p r k", k=GRID_W),
                                rpb_window(A["na_rpb"], layer, hh, half)).then_inc(s["attn_in"], 16)
                    for a, name in enumerate(("cache_na_k", "cache_na_v")):
                        dma_in(sp, kvc[:, a, :].rearrange("p (h d) -> p h d", h=HEADS),
                               A[name][0, layer].rearrange("h t d -> t h d"), s["attn_in"])
            for k in range(SLOTS):
                slot = expert_slot(k)
                if slot < PRE_SLOTS:
                    last = max(n for n in range(PRE) if pre_slot(n) == slot)
                    chunk_used(sp, last)
                else:
                    sp.wait_ge(s["st_kept"], 1)
                    sp.wait_ge(s["go_ready"], STREAMS)
                    sp.wait_ge(s["stored"], 16 * STORES * (layer + 1))
                load_expert(sp, ring[:, slot, :],
                            [A[w][layer, k] for w in ("exp_w_gate", "exp_w_up", "exp_w_down")],
                            expert_in[slot])
            with sp.Fori(1, EXPERTS // SLOTS) as i:
                for q in range(SLOTS):
                    sp.wait_ge(s["down_done"], i * STEPS + (2 * (q - 3) + 3))
                    slot = expert_slot(q)
                    load_expert(sp, ring[:, slot, :],
                                [A[w][layer, bass.ds(i * SLOTS + q, 1)][0]
                                 for w in ("exp_w_gate", "exp_w_up", "exp_w_down")],
                                expert_in[slot])

        def rsqrt_dve(dve, link, k, ss, v, r0, t, r, scale):
            nc.vector.tensor_scalar(v, ss, scale, EPS, ALU.mult, ALU.add).then_inc(s["var_ready"], 1)
            dve.wait_ge(s["root_ready"], k + 1)
            link(nc.vector.tensor_tensor(t, r0, r0, ALU.mult))
            link(nc.vector.tensor_tensor(t, t, v, ALU.mult))
            link(nc.vector.tensor_scalar(t, t, -0.5, 1.5, ALU.mult, ALU.add))
            link(nc.vector.tensor_tensor(r, r0, t, ALU.mult))

        def rsqrt_act(act, link, k, v, r0):
            act.wait_ge(s["var_ready"], k + 1)
            link(nc.scalar.activation(r0, v, ACT.Ln))
            nc.scalar.activation(r0, r0, ACT.Exp, scale=-0.5).then_inc(s["root_ready"], 1)

        def numbers(k, part):
            at, n = ((0, 2), (10, 2), (20, 16), (100, 4), (120, 4), (140, 2))[k]
            return sm[:, at + n * part:at + n * (part + 1)]

        N_IN, N_CONV, N_QK, N_GLA, N_FFN = 0, 1, 2, 3, 5
        conv_mean = sm[:, 150:152]
        mx = sm[:, 152:160]
        p_sum = sm[:, 160:168]
        p_inv = sm[:, 168:176]

        @block.tensor
        def _(pe):
            mm = nc.tensor.matmul

            def show(n, st, b):
                for c in range(4):
                    last = mm(bank(b, P * c, P * (c + 1)), pick[:, c, st, :], ada[:, n, :], start=True, stop=True)
                return last

            def modulation(k):
                for st in range(STREAMS):
                    for half in range(2):
                        show(6 * k + 2 + half, st, 4 * st + half)
                    for half in range(2):
                        last = show(6 * k + half, st, 4 * st + 2 + half)
                    last.then_inc(s["mod_shown"], 1)

            def turn_h(k):
                for st in range(STREAMS):
                    pe.wait_ge(s["h_ready"], STREAMS * k + st + 1)
                    ht = h[:, st, :].rearrange("t (p k) -> t k p", k=KT)
                    for kt in range(KT):
                        last = nc.tensor.transpose(bank(4 * st + kt // 4, P * (kt % 4), P * (kt % 4 + 1)),
                                                   ht[:, kt, :], ident[:])
                    last.then_inc(s["hT_shown"], 1)

            for n in range(ADA_CHUNKS):
                pre_loaded(pe, n)
                if n >= 2:
                    pe.wait_ge(s["ada_kept"], n - 1)
                w = ring[:, pre_slot(n), 0:KT * 512].rearrange("p (k n) -> p k n", k=KT)
                for kt in range(KT):
                    for c in range(4):
                        last = mm(ps[32 * c:32 * (c + 1), n % 2, 0:P], cs[:, kt, :], w[:, kt, P * c:P * (c + 1)],
                                  start=(kt == 0), stop=(kt == KT - 1))
                last.then_inc(s["ada_done"], 1)
            pe.wait_ge(s["bias_in"], 64)
            modulation(0)
            turn_h(0)
            pe.wait_ge(s["small_in"], 16 * N_SMALL)
            pe.wait_ge(s["vec_in"], 16 * N_VEC)
            pe.wait_ge(s["hT_ready"], STREAMS)
            for c in range(2):
                last = nc.tensor.transpose(bank(5, 64 * c, 64 * c + R_END), vec[:, P * c:P * (c + 1)],
                                           ident[0:R_END, 0:R_END])
            last.then_inc(s["vec_shown"], 1)
            for u, (c, c0, w, by_channel, st) in enumerate(UNITS_IN):
                if u == 0 or UNITS_IN[u - 1][0] != c:
                    pre_loaded(pe, C_IN + c)
                if u >= len(PROJ_BANKS):
                    pe.wait_ge(s["proj_kept"], u - len(PROJ_BANKS) + 1)
                cw = IN_CHUNKS[c][1]
                wt = ring[:, pre_slot(C_IN + c), 0:KT * cw].rearrange("p (k n) -> p k n", k=KT)[:, :, c0:c0 + w]
                b = PROJ_BANKS[u % len(PROJ_BANKS)]
                for kt in range(KT):
                    if by_channel:
                        last = mm(ps[0:w, b, 0:STREAMS * P], wt[:, kt, :], hT[:, kt, :],
                                  start=(kt == 0), stop=(kt == KT - 1))
                    else:
                        last = mm(bank(b, 0, w), hT[:, kt, P * st:P * (st + 1)], wt[:, kt, :],
                                  start=(kt == 0), stop=(kt == KT - 1))
                last.then_inc(s["proj_done"], 1)
                if u == 4:
                    pe.wait_ge(s["proj_kept"], 1)
                    for st2 in range(STREAMS):
                        mm(bank(st2), lrT[:, P * st2:P * (st2 + 1)], wg[:], start=True,
                           stop=True).then_inc(s["z_shown"], 1)
            pe.wait_ge(s["vec_ready"], 1)
            pe.wait_ge(s["conv_ready"], 1)
            for st in range(STREAMS):
                for c in range(2):
                    at = 256 * st + P * c
                    last = nc.tensor.transpose(bank(4, at, at + P), cacc[:, c, st, :], ident[:])
            last.then_inc(s["convT_shown"], 1)
            pe.wait_ge(s["ctok_ready"], 1)
            for c in range(2):
                for st in range(STREAMS):
                    at = 256 * c + P * st
                    last = nc.tensor.transpose(bank(5, at, at + P), cTok[:, st, P * c:P * (c + 1)], ident[:])
            last.then_inc(s["convB_shown"], 1)
            pe.wait_ge(s["cact_ready"], 1)
            for o in range(2):
                for c in range(2):
                    last = mm(bank(4, 256 * o, 256 * (o + 1)), wpw[:, c, P * o:P * (o + 1)],
                              cacc[:, c, :, :].rearrange("p s t -> p (s t)"), start=(c == 0), stop=(c == 1))
            last.then_inc(s["pw_shown"], 1)
            pe.wait_ge(s["nq_ready"], 1)
            pe.wait_ge(s["proj_kept"], len(UNITS_IN))
            pe.wait_ge(s["attn_in"], 16 * N_ATTN)
            for b, c0 in ((2, 0), (3, 256)):
                for a in range(PAIRS):
                    for st in range(STREAMS):
                        at = 256 * a + P * st
                        nc.tensor.transpose(bank(b, at, at + P), nq[:, st, c0 + P * a:c0 + P * (a + 1)], ident[:])
            for a in range(PAIRS):
                last = nc.tensor.transpose(bank(6, P * a, P * (a + 1)), kvc[:, 0, P * a:P * (a + 1)], ident[:])
            last.then_inc(s["nT_shown"], 1)
            pe.wait_ge(s["nT_ready"], 1)
            pe.wait_ge(s["bias_ready"], 1)
            for e in range(2):
                r = slice(DK * e, DK * (e + 1))
                for a in range(PAIRS):
                    last = mm(bank(2 + e, P * a, P * (a + 1)), qnT[r, a, 0:P], knT[r, a, 0:P], start=True, stop=True)
            last.then_inc(s["scores_shown"], 1)
            for e in range(2):
                r = slice(DK * e, DK * (e + 1))
                for a in range(PAIRS):
                    local = bank(6 + e, 256 * a, 256 * a + P)
                    mm(local, qnT[r, a, P:2 * P], knT[r, a, P:2 * P], start=True, stop=False)
                    mm(local, flip[:], biasr[:, 2 * a + e, :], start=False, stop=True)
                    last = mm(bank(6 + e, 256 * a + P, 256 * (a + 1)), qnT[r, a, P:2 * P], kcT[r, a, :],
                              start=True, stop=True)
            last.then_inc(s["scores_shown"], 1)
            pe.wait_ge(s["p_ready"], 1)
            pe.wait_ge(s["la_ready"], STREAMS)
            blocks = [(p0[:, i, :]) for i in range(HEADS)]
            blocks += [p1[:, i, P * j:P * (j + 1)] for i in range(HEADS) for j in range(2)]
            for i, block_in in enumerate(blocks):
                last = nc.tensor.transpose(bank(i // 4, P * (i % 4), P * (i % 4 + 1)), block_in, ident[:])
            last.then_inc(s["pT_shown"], 1)
            pe.wait_ge(s["pT_ready"], 1)
            for e in range(2):
                for a in range(PAIRS):
                    hh, i = 2 * a + e, 2 * e + a
                    c0 = 2 * HEADS * DK + DK * hh
                    out = ps[DK * e:DK * (e + 1), 3, :]
                    mm(out[:, 256 * a:256 * a + P], nax[:, 0, c0:c0 + DK], pT[:, i, :], start=True, stop=True)
                    out1 = out[:, 256 * a + P:256 * (a + 1)]
                    mm(out1, nax[:, 1, c0:c0 + DK], pT[:, HEADS + 2 * i, :], start=True, stop=False)
                    last = mm(out1, kvc[:, 1, DK * hh:DK * (hh + 1)], pT[:, HEADS + 2 * i + 1, :],
                              start=False, stop=True)
            last.then_inc(s["pv_shown"], 1)

            def decays(g):
                st, a, dr = g // 4, g // 2 % 2, g % 2
                if g:
                    pe.wait_ge(s["E_ready"], g)
                m = (mf, mb)[dr]
                for b in range(2):
                    last = mm(bank(b), la[:, st, dr, P * a:P * (a + 1)],
                              m[:, 4 * b:4 * (b + 1), :].rearrange("p l n -> p (l n)"), start=True, stop=True)
                last.then_inc(s["decay_shown"], 1)

            def pairs(g):
                st, a, dr = g // 4, g // 2 % 2, g % 2
                pe.wait_ge(s["X_ready"], g + 1)
                for e in range(2):
                    if g:
                        pe.wait_ge(s["masked"], 2 * (g - 1) + e + 1)
                    r = slice(DK * e, DK * (e + 1))
                    for lv in range(LEVELS + (dr == 0)):
                        out = bank((2, 6)[e] + lv // 4, P * (lv % 4), P * (lv % 4 + 1))
                        if lv < LEVELS:
                            last = mm(out, X[r, dr, lv, :], X[r, dr, lv, :], start=True, stop=True)
                        else:
                            last = mm(out, kT[r, a, P * st:P * (st + 1)], qT[r, a, P * st:P * (st + 1)],
                                      start=True, stop=True)
                    last.then_inc(s["pair_shown"], 1)

            def outputs(g):
                st, a = g // 4, g // 2 % 2
                for e in range(2):
                    pe.wait_ge(s["att_ready"], 2 * (g // 2) + e + 1)
                    hh = 2 * a + e
                    out = bank(4 + st, DV * hh, DV * (hh + 1))
                    last = mm(out, att[:, a, e, :], v[:, st, DV * hh:DV * (hh + 1)], start=True, stop=(st == 0))
                    if st == 1:
                        for dr in range(2):
                            last = mm(out, qd[:, a, dr, :], s0[:, dr, hh, :], start=False, stop=(dr == 1))
                    last.then_inc(s["o_shown"], 1)

            pe.wait_ge(s["cat_na"], 1)
            pe.wait_ge(s["cat_conv"], 1)
            decays(0)
            for g in range(8):
                if g + 1 < 8:
                    decays(g + 1)
                pairs(g)
                if g % 2:
                    outputs(g)
            pe.wait_ge(s["masked"], 16)
            for a in range(PAIRS):
                nc.tensor.transpose(bank(2, P * a, P * (a + 1)), kT[:, a, 0:P], ident[:])
            for dr in range(2):
                last = mm(bank(3, 256 * dr, 256 * (dr + 1)), suf[:, dr, :], la[:, 0, dr, :], start=True, stop=True)
            last.then_inc(s["st_pre"], 1)
            pe.wait_ge(s["kd_ready"], 1)
            for dr in range(2):
                for hh in range(HEADS):
                    last = mm(ps[0:DK, 6 + dr, DV * hh:DV * (hh + 1)], kd[:, dr, DK * hh:DK * (hh + 1)],
                              v[:, 0, DV * hh:DV * (hh + 1)], start=True, stop=True)
            last.then_inc(s["st_shown"], 1)
            for st in range(STREAMS):
                pe.wait_ge(s["go_ready"], st + 1)
                for hh in range(HEADS):
                    last = nc.tensor.transpose(bank(st, P * hh, P * (hh + 1)), gg[:, st, P * hh:P * (hh + 1)], ident[:])
                last.then_inc(s["goT_shown"], 1)
            pe.wait_ge(s["cat_gla"], STREAMS)
            pe.wait_ge(s["st_kept"], 1)
            for half in range(2):
                pre_loaded(pe, C_OUT + half)
                w = ring[:, pre_slot(C_OUT + half), 0:KT * 512].rearrange("p (k n) -> p k n", k=KT)
                for st in range(STREAMS):
                    show(4 + half, st, (4, 5, 0, 1)[2 * half + st])
                    for kt in range(KT):
                        last = mm(bank(PROJ_BANKS[2 * half + st]), cat[:, kt, P * st:P * (st + 1)], w[:, kt, :],
                                  start=(kt == 0), stop=(kt == KT - 1))
                    last.then_inc(s["mix_shown"], 1)
            pe.wait_ge(s["x_mid"], 4)
            modulation(1)
            turn_h(1)
            pe.wait_ge(s["hT_ready"], 2 * STREAMS)
            for st in range(STREAMS):
                for kt in range(KT):
                    last = mm(bank(2 + 4 * st, 0, EXPERTS), hT[:, kt, P * st:P * (st + 1)], wr[:, kt, :],
                              start=(kt == 0), stop=(kt == KT - 1))
                last.then_inc(s["logits_shown"], 1)
            for st in range(STREAMS):
                for half in range(2):
                    last = show(10 + half, st, 4 * st + half)
            last.then_inc(s["g2_shown"], 1)

            def gate_up_step(u_bank, st, slot):
                for kt in range(KT):
                    last = mm(bank(4 + u_bank), hT[:, kt, P * st:P * (st + 1)], gate_up(slot, kt),
                              start=(kt == 0), stop=(kt == KT - 1))
                last.then_inc(s["gu_done"], 1)

            def turn_step(u_bank):
                a_in = acts[:, u_bank, :].rearrange("t (p j) -> t j p", j=2)
                for j in range(2):
                    last = nc.tensor.transpose(bank(6 + u_bank, P * j, P * (j + 1)), a_in[:, j, :], ident[:])
                last.then_inc(s["actT_shown"], 1)

            def down_step(u_bank, st, slot):
                for half in range(2):
                    for j in range(2):
                        last = mm(bank(2 * st + half), actT[:, u_bank, P * j:P * (j + 1)], down(slot, j, half),
                                  start=False, stop=False, skip_group_check=True)
                last.then_inc(s["down_done"], 1)

            pe.wait_ge(s["g2_kept"], 1)
            pe.wait_ge(s["scored"], STREAMS)
            for b in range(4):
                last = mm(bank(b), zero[:], mf[:, 0:4, :].rearrange("p l n -> p (l n)"), start=True, stop=False,
                          skip_group_check=True)
            last.then_inc(s["down_done"], 1)
            shared = ring[:, pre_slot(C_SH), :]
            pe.wait_ge(s["shared_in"], 48)
            gate_up_step(0, 0, shared)
            gate_up_step(1, 1, shared)
            pe.wait_ge(s["act_done"], 1)
            turn_step(0)
            with pe.Fori(0, EXPERTS // SLOTS) as i:
                for q in range(STEPS):
                    e, st = q // 2, q % 2
                    if st == 0:
                        pe.wait_ge(expert_in[expert_slot(e)], i * 48 + 48)
                    pe.wait_ge(s["act_done"], i * STEPS + q + 1)
                    gate_up_step(st, st, ring[:, expert_slot(e), :])
                    pe.wait_ge(s["actT_kept"], i * STEPS + q + 1)
                    down_step(st, st, ring[:, expert_slot(e - 1), :])
                    pe.wait_ge(s["act_done"], i * STEPS + q + 2)
                    turn_step(1 - st)
            n = 2 * EXPERTS
            pe.wait_ge(s["actT_kept"], n + 1)
            down_step(0, 0, ring[:, expert_slot(EXPERTS - 1), :])
            pe.wait_ge(s["act_done"], n + 2)
            turn_step(1)
            pe.wait_ge(s["actT_kept"], n + 2)
            down_step(1, 1, ring[:, expert_slot(EXPERTS - 1), :])

        @block.scalar
        def _(act):
            count = [0]

            def link(ins):
                count[0] += 1
                ins.then_inc(s["act_step"], 1)
                act.wait_ge(s["act_step"], count[0])

            def two(b):
                return ps[:, b:b + 2, :].rearrange("p b n -> p (b n)")

            def squares(k):
                for st in range(STREAMS):
                    last = nc.scalar.activation(h[:, st, :], x[:, st, :], ACT.Square,
                                                accum_out=numbers(k, 0)[:, st:st + 1])
                last.then_inc(s["square_done"], 1)

            def keep_hT(k):
                for st in range(STREAMS):
                    act.wait_ge(s["hT_shown"], STREAMS * k + st + 1)
                    nc.scalar.copy(hT[:, :, P * st:P * (st + 1)], two(4 * st).rearrange("p (k n) -> p k n", n=P))\
                      .then_inc(s["hT_ready"], 1)

            squares(0)
            rsqrt_act(act, link, N_IN, numbers(N_IN, 1), numbers(N_IN, 2))
            for n in range(ADA_CHUNKS):
                act.wait_ge(s["ada_done"], n + 1)
                nc.scalar.copy(ada[:, n, :], bank(n % 2, 0, P)).then_inc(s["ada_kept"], 1)
            act.wait_ge(s["ada_kept"], ADA_CHUNKS)
            for c in range(4):
                dma_in(act, ada[32 * c + 2:32 * c + 3, :, :],
                       A["b_ada"][bass.ds(layer, 1), :].rearrange("l (n c m) -> l n c m", c=4, m=P)[:, :, c, :],
                       s["bias_in"])
            keep_hT(0)
            act.wait_ge(s["vec_shown"], 1)
            nc.scalar.copy(vecT[:], bank(5, 0, 2 * 64).rearrange("p (c r) -> p c r", c=2)[:, :, 0:R_END])\
              .then_inc(s["vec_ready"], 1)
            for u, (c, c0, w, by_channel, st) in enumerate(UNITS_IN):
                act.wait_ge(s["proj_done"], u + 1)
                b = PROJ_BANKS[u % len(PROJ_BANKS)]
                wide = bank(b, 0, STREAMS * P)
                if u == 0:
                    last = nc.scalar.copy(lrT[0:2 * RANK, :], ps[0:2 * RANK, b, 0:STREAMS * P])
                elif c == 0:
                    last = nc.scalar.copy(ci[:, u - 1, :], wide)
                elif c == 1 and u < 7:
                    last = nc.scalar.mul(qT[:, u - 5, :], wide, float(DK) ** -0.5)
                elif c == 1:
                    last = nc.scalar.copy(kT[:, u - 7, :], wide)
                else:
                    last = nc.scalar.copy(((v, nax, gg)[c - 2])[:, st, c0:c0 + w], bank(b, 0, w))
                last.then_inc(s["proj_kept"], 1)
                if u == 4:
                    for st2 in range(STREAMS):
                        act.wait_ge(s["z_shown"], st2 + 1)
                        z = la[:, st2, :, :].rearrange("p a n -> p (a n)")
                        link(nc.scalar.activation(z, bank(st2), ACT.Abs))
                        link(nc.scalar.activation(z, z, ACT.Exp, scale=-1.0))
                        nc.scalar.activation(z, z, ACT.Ln, bias=1.0).then_inc(s["la_log"], 1)
                    act.wait_ge(s["proj_kept"], 5)
                    nc.scalar.activation(csig, ci[:, 2:4, :], ACT.Sigmoid).then_inc(s["conv_sig"], 1)
            rsqrt_act(act, link, N_CONV, numbers(N_CONV, 1), numbers(N_CONV, 2))
            act.wait_ge(s["convB_shown"], 1)
            for c in range(2):
                y = cacc[:, c, :, :].rearrange("p s t -> p (s t)")
                nc.scalar.activation(y, bank(5, 256 * c, 256 * (c + 1)), ACT.Identity,
                                     scale=vecT[:, c, R_LNG:R_LNG + 1], bias=vecT[:, c, R_LNB:R_LNB + 1])\
                  .then_inc(s["conv_neg"], 1)
            act.wait_ge(s["conv_neg"], 2)
            nc.scalar.activation(csig, cacc[:].rearrange("p c s t -> p c (s t)"), ACT.Sigmoid)\
              .then_inc(s["conv_sig"], 1)
            act.wait_ge(s["pw_shown"], 1)
            nc.scalar.copy(cat[:, 4:6, :], bank(4).rearrange("p (o n) -> p o n", o=2)).then_inc(s["cat_conv"], 1)
            rsqrt_act(act, link, N_QK, numbers(N_QK, 1), numbers(N_QK, 2))
            act.wait_ge(s["nT_shown"], 1)
            nc.scalar.mul(qnT, bank(2).rearrange("p (a n) -> p a n", a=2), vecT[:, 0, R_QN:R_QN + 1])
            nc.scalar.mul(knT, bank(3).rearrange("p (a n) -> p a n", a=2), vecT[:, 0, R_KN:R_KN + 1])
            nc.scalar.copy(kcT, bank(6, 0, 256).rearrange("p (a n) -> p a n", a=2)).then_inc(s["nT_ready"], 1)
            for st in range(STREAMS):
                act.wait_ge(s["max_ready"], st + 1)
                pr = (p0, p1)[st]
                w = (P, 2 * P)[st]
                for e in range(2):
                    for a in range(PAIRS):
                        i = 2 * e + a
                        last = nc.scalar.activation(pr[:, i, :], bank((2, 6)[st] + e, w * a, w * (a + 1)), ACT.Exp,
                                                    bias=mx[:, 4 * st + i:4 * st + i + 1],
                                                    accum_out=p_sum[:, 4 * st + i:4 * st + i + 1])
                last.then_inc(s["p_exp"], 1)
            act.wait_ge(s["pT_shown"], 1)
            nc.scalar.copy(pT, ps[:, 0:3, :].rearrange("p b (i n) -> p (b i) n", n=P)).then_inc(s["pT_ready"], 1)
            act.wait_ge(s["pv_shown"], 1)
            nc.scalar.copy(cat[:, 6:8, :], bank(3).rearrange("p (a n) -> p a n", a=2)).then_inc(s["cat_na"], 1)
            nc.scalar.activation(tm[:].rearrange("p l n -> p (l n)"), gg[:].rearrange("p s n -> p (s n)"),
                                 ACT.Sigmoid).then_inc(s["gg_sig"], 1)
            for g in range(8):
                act.wait_ge(s["decay_shown"], g + 1)
                if g == 1:
                    act.wait_ge(s["kco_ready"], 1)
                if g >= 2:
                    act.wait_ge(s["X_ready"], g - 1)
                nc.scalar.activation(E[:, g % 2, :, :], two(0).rearrange("p (l n) -> p l n", n=P), ACT.Exp)\
                  .then_inc(s["E_ready"], 1)
            act.wait_ge(s["st_pre"], 1)
            nc.scalar.activation(kd.rearrange("p a n -> p (a n)"), bank(3), ACT.Exp).then_inc(s["st_exp"], 1)
            act.wait_ge(s["st_shown"], 1)
            act.wait_ge(s["X_ready"], 8)
            nc.scalar.copy(hflat[0:DK, 0:1024], ps[0:DK, 6:8, :].rearrange("p b n -> p (b n)")).then_inc(s["st_kept"], 1)
            for st in range(STREAMS):
                rsqrt_act(act, link, N_GLA + st, numbers(N_GLA + st, 1), numbers(N_GLA + st, 2))
            for st in range(STREAMS):
                act.wait_ge(s["goT_shown"], st + 1)
                nc.scalar.mul(cat[:, 0:4, P * st:P * (st + 1)], bank(st).rearrange("p (k n) -> p k n", n=P),
                              vecT[:, 0, R_ON:R_ON + 1]).then_inc(s["cat_gla"], 1)
            act.wait_ge(s["x_mid"], 4)
            act.wait_ge(s["stored"], layer * (16 * STORES) + 16 * STORES)
            squares(N_FFN)
            rsqrt_act(act, link, N_FFN, numbers(N_FFN, 1), numbers(N_FFN, 2))
            keep_hT(1)
            act.wait_ge(s["logits_shown"], STREAMS)
            for st in range(STREAMS):
                nc.scalar.activation(scores[:, st, :], bank(2 + 4 * st, 0, EXPERTS), ACT.Sigmoid)\
                  .then_inc(s["scored"], 1)
            act.wait_ge(s["g2_shown"], 1)
            for st in range(STREAMS):
                last = nc.scalar.copy(g2[:, st, :], two(4 * st))
            last.then_inc(s["g2_kept"], 1)

            def silu_step(b):
                nc.scalar.activation(silu[:, b, :], bank(4 + b, 0, FF), ACT.Silu).then_inc(s["silu_done"], 1)

            def keep_step(b):
                nc.scalar.copy(actT[:, b, :], bank(6 + b, 0, FF)).then_inc(s["actT_kept"], 1)

            for st in range(STREAMS):
                act.wait_ge(s["gu_done"], st + 1)
                silu_step(st)
            act.wait_ge(s["actT_shown"], 1)
            keep_step(0)
            with act.Fori(0, EXPERTS // SLOTS) as i:
                for q in range(STEPS):
                    b = q % 2
                    act.wait_ge(s["gu_done"], i * STEPS + q + 3)
                    act.wait_ge(s["act_done"], i * STEPS + q + 1)
                    silu_step(b)
                    act.wait_ge(s["actT_shown"], i * STEPS + q + 2)
                    act.wait_ge(s["down_done"], i * STEPS + q + 1)
                    keep_step(1 - b)
            act.wait_ge(s["actT_shown"], 2 * EXPERTS + 2)
            act.wait_ge(s["down_done"], 2 * EXPERTS + 1)
            keep_step(1)

        @block.vector
        def _(dve):
            count = [0]

            def link(ins):
                count[0] += 1
                ins.then_inc(s["dve_step"], 1)
                dve.wait_ge(s["dve_step"], count[0])

            tt, ts, stt = nc.vector.tensor_tensor, nc.vector.tensor_scalar, nc.vector.scalar_tensor_tensor

            def two(b):
                return ps[:, b:b + 2, :].rearrange("p b n -> p (b n)")

            tmflat = tm[:].rearrange("p l n -> p (l n)")

            def modulate(k, norm):
                dve.wait_ge(s["square_done"], k + 1)
                rsqrt_dve(dve, link, norm, *[numbers(norm, j) for j in range(5)], 1.0 / D)
                dve.wait_ge(s["norm_in"], 16 * (k + 1))
                for st in range(STREAMS):
                    dve.wait_ge(s["mod_shown"], STREAMS * k + st + 1)
                    link(stt(out=tmflat, in0=two(4 * st), scalar=1.0, in1=gbc[:], op0=ALU.add, op1=ALU.mult))
                    link(stt(out=h[:, st, :], in0=x[:, st, :], scalar=numbers(norm, 4)[:, st:st + 1], in1=tmflat,
                             op0=ALU.mult, op1=ALU.mult))
                    tt(h[:, st, :], h[:, st, :], two(4 * st + 2), ALU.add).then_inc(s["h_ready"], 1)

            modulate(0, N_IN)
            for st in range(STREAMS):
                dve.wait_ge(s["la_log"], st + 1)
                z = la[:, st, :, :].rearrange("p a n -> p (a n)")
                link(stt(out=z, in0=bank(st), scalar=0.0, in1=z, op0=ALU.min, op1=ALU.subtract))
                ts(z, z, 1.0 / 16.0, None, ALU.mult).then_inc(s["la_ready"], 1)
            dve.wait_ge(s["conv_sig"], 1)
            for c in range(2):
                link(tt(hpad[:, c, :, HALO:HALO + P], ci[:, c, :].rearrange("p (s t) -> p s t", s=2),
                        csig[:, c, :].rearrange("p (s t) -> p s t", s=2), ALU.mult))
            dve.wait_ge(s["vec_ready"], 1)
            for t in range(TAPS):
                for c in range(2):
                    k = 2 * t + c
                    shifted = hpad[:, c, :, t:t + P]
                    wt = vecT[:, c, R_DW + t:R_DW + t + 1]
                    if t == 0:
                        ins = ts(cacc[:, c, :, :], shifted, wt, vecT[:, c, R_DWB:R_DWB + 1], ALU.mult, ALU.add)
                    else:
                        dve.wait_ge(s["tap"], k - 1)
                        ins = stt(out=cacc[:, c, :, :], in0=shifted, scalar=wt, in1=cacc[:, c, :, :],
                                  op0=ALU.mult, op1=ALU.add)
                    ins.then_inc(s["tap"], 1)
            dve.wait_ge(s["tap"], 2 * TAPS)
            nc.vector.memset(sm[:, 176:177], 0.0).then_inc(s["conv_ready"], 1)
            dve.wait_ge(s["convT_shown"], 1)
            tok = bank(4).rearrange("p (s n) -> p s n", s=2)
            link(nc.vector.tensor_reduce(conv_mean, tok, AX.X, ALU.add))
            link(ts(conv_mean, conv_mean, -1.0 / CONV_CH, None, ALU.mult))
            for st in range(STREAMS):
                link(ts(cTok[:, st, :], tok[:, st, :], conv_mean[:, st:st + 1], None, ALU.add))
            link(tt(cSq, cTok, cTok, ALU.mult))
            link(nc.vector.tensor_reduce(numbers(N_CONV, 0), cSq, AX.X, ALU.add))
            rsqrt_dve(dve, link, N_CONV, *[numbers(N_CONV, j) for j in range(5)], 1.0 / CONV_CH)
            for st in range(STREAMS):
                last = ts(cTok[:, st, :], cTok[:, st, :], numbers(N_CONV, 4)[:, st:st + 1], None, ALU.mult)
            last.then_inc(s["ctok_ready"], 1)
            dve.wait_ge(s["conv_sig"], 2)
            y = cacc[:].rearrange("p c s t -> p c (s t)")
            tt(y, y, csig, ALU.mult).then_inc(s["cact_ready"], 1)
            dve.wait_ge(s["proj_kept"], LAST_UNIT[3] + 1)
            dve.wait_ge(s["hT_ready"], STREAMS)
            link(tt(sq, nax[:, :, 0:512], nax[:, :, 0:512], ALU.mult))
            link(nc.vector.tensor_reduce(numbers(N_QK, 0), sq.rearrange("p s (g d) -> p (s g) d", d=DK), AX.X, ALU.add))
            rsqrt_dve(dve, link, N_QK, *[numbers(N_QK, j) for j in range(5)], 1.0 / DK)
            r = numbers(N_QK, 4)
            link(ts(r.rearrange("p (s g) -> p s g", s=2)[:, :, 0:HEADS], r.rearrange("p (s g) -> p s g", s=2)[:, :, 0:HEADS],
                    float(DK) ** -0.5, None, ALU.mult))
            for st in range(STREAMS):
                last = tt(nq[:, st, :].rearrange("p (g d) -> p g d", d=DK),
                          nax[:, st, 0:512].rearrange("p (g d) -> p g d", d=DK),
                          r[:, 8 * st:8 * (st + 1)].unsqueeze(2).broadcast_to([P, 8, DK]), ALU.mult)
            last.then_inc(s["nq_ready"], 1)
            for st in range(STREAMS):
                dve.wait_ge(s["scores_shown"], st + 1)
                sc = ps[:, 2:4, 0:256] if st == 0 else ps[:, 6:8, :]
                link(nc.vector.tensor_reduce(mx[:, 4 * st:4 * st + 4].rearrange("p (e a) -> p e a", e=2),
                                             sc.rearrange("p e (a k) -> p e a k", a=2), AX.X, ALU.max))
                ts(mx[:, 4 * st:4 * st + 4], mx[:, 4 * st:4 * st + 4], -1.0, None, ALU.mult).then_inc(s["max_ready"], 1)
            dve.wait_ge(s["p_exp"], STREAMS)
            link(nc.vector.reciprocal(p_inv, p_sum))
            tt(p0, p0, p_inv[:, 0:4].unsqueeze(2).broadcast_to([P, 4, P]), ALU.mult)
            tt(p1, p1, p_inv[:, 4:8].unsqueeze(2).broadcast_to([P, 4, 2 * P]), ALU.mult).then_inc(s["p_ready"], 1)
            dve.wait_ge(s["gg_sig"], 1)
            ggf = gg[:].rearrange("p s n -> p (s n)")
            link(tt(ggf, ggf, tmflat, ALU.mult))

            def decayed(g):
                st, a, dr = g // 4, g // 2 % 2, g % 2
                dve.wait_ge(s["E_ready"], g + 1)
                if g >= 2:
                    dve.wait_ge(s["pair_shown"], 2 * (g - 1))
                q_, k_ = (t[:, a, P * st:P * (st + 1)] for t in (qT, kT))
                for lv in range(LEVELS):
                    w = P >> (lv + 1)
                    for part, src in ((0, (k_, q_)[dr]), (1, (q_, k_)[dr])):
                        views = [t.rearrange("p (b a r) -> p b a r", a=2, r=w)[:, :, part, :]
                                 for t in (X[:, dr, lv, :], E[:, dr, lv, :], src)]
                        last = tt(*views, ALU.mult)
                if st == 1:
                    last = tt(qd[:, a, dr, :], E[:, dr, LEVELS, :], q_, ALU.mult)
                last.then_inc(s["X_ready"], 1)

            def combine(g):
                st, a, dr = g // 4, g // 2 % 2, g % 2
                n = LEVELS + (dr == 0)
                for e in range(2):
                    dve.wait_ge(s["pair_shown"], 2 * g + e + 1)
                    if st == 1 and dr == 0:
                        dve.wait_ge(s["o_shown"], 2 * a + e + 1)
                    b = (2, 6)[e]
                    tt(tm[:, 0:n, :], two(b).rearrange("p (l n) -> p l n", n=P)[:, 0:n, :],
                       (maskf, maskb)[dr][:, 0:n, :], ALU.mult).then_inc(s["masked"], 1)
                    dve.wait_ge(s["masked"], 2 * g + e + 1)
                    levels = tm[:, 0:n, :].rearrange("p l n -> p n l")
                    if dr == 0:
                        link(nc.vector.tensor_reduce(att[:, a, e, :], levels, AX.X, ALU.add))
                    else:
                        link(nc.vector.tensor_reduce(att2[:, 0:P], levels, AX.X, ALU.add))
                        tt(att[:, a, e, :], att[:, a, e, :], att2[:, 0:P], ALU.add).then_inc(s["att_ready"], 1)
                        dve.wait_ge(s["att_ready"], 2 * (g // 2) + e + 1)

            dve.wait_ge(s["pv_shown"], 1)
            decayed(0)
            for g in range(8):
                if g + 1 < 8:
                    decayed(g + 1)
                combine(g)
            dve.wait_ge(s["st_exp"], 1)
            for dr in range(2):
                last = tt(kd[:, dr, :], kd[:, dr, :], bank(2, 0, 256), ALU.mult)
            last.then_inc(s["kd_ready"], 1)
            for st in range(STREAMS):
                dve.wait_ge(s["o_shown"], 4 * (st + 1))
                o = bank(4 + st).rearrange("p (h n) -> p h n", n=DV)
                t4 = tm[:, 4 * st:4 * (st + 1), :]
                o_copy = hflat[:, 1024 + 512 * st:1536 + 512 * st].rearrange("p (h n) -> p h n", n=DV)
                link(nc.vector.tensor_copy(o_copy, o))
                link(tt(t4, o_copy, o_copy, ALU.mult))
                link(nc.vector.tensor_reduce(numbers(N_GLA + st, 0), t4, AX.X, ALU.add))
                rsqrt_dve(dve, link, N_GLA + st, *[numbers(N_GLA + st, j) for j in range(5)], 1.0 / DV)
                link(tt(t4, o_copy, numbers(N_GLA + st, 4).unsqueeze(2).broadcast_to([P, HEADS, DV]), ALU.mult))
                g4 = gg[:, st, :].rearrange("p (h n) -> p h n", n=DV)
                tt(g4, g4, t4, ALU.mult).then_inc(s["go_ready"], 1)
            dve.wait_ge(s["go_ready"], STREAMS)
            for half in range(2):
                for st in range(STREAMS):
                    u = 2 * half + st
                    dve.wait_ge(s["mix_shown"], u + 1)
                    t = tmflat[:, 512 * (u % 2):512 * (u % 2 + 1)]
                    nc.vector.tensor_copy(t, bank((4, 5, 0, 1)[u])).then_inc(s["dve_step"], 1)
                    count[0] += 1
                    dve.wait_ge(s["dve_step"], count[0])
                    link(tt(t, t, bank(PROJ_BANKS[u]), ALU.mult))
                    xs = x[:, st, 512 * half:512 * (half + 1)]
                    tt(xs, xs, t, ALU.add).then_inc(s["x_mid"], 1)
            dve.wait_ge(s["x_mid"], 4)
            modulate(1, N_FFN)
            dve.wait_ge(s["scored"], STREAMS)
            for st in range(STREAMS):
                last = tt(biased[:, st, :], scores[:, st, :], rbias[:], ALU.add)
            link(last)
            for st in range(STREAMS):
                for g in range(GROUPS):
                    last = nc.vector.max(top[:, st, g, :], biased[:, st, PER_GROUP * g:PER_GROUP * (g + 1)])
            link(last)
            link(tt(grp, top[:, :, :, 0], top[:, :, :, 1], ALU.add))
            for st in range(STREAMS):
                other = grp[:, st, :].unsqueeze(1).broadcast_to([P, GROUPS, GROUPS])
                own = grp[:, st, :].unsqueeze(2).broadcast_to([P, GROUPS, GROUPS])
                link(tt(beats[:, 0], other, own, ALU.is_equal))
                link(tt(beats[:, 0], beats[:, 0], tri8[:], ALU.mult))
                link(tt(beats[:, 1], other, own, ALU.is_gt))
                link(tt(beats[:, 0], beats[:, 0], beats[:, 1], ALU.add))
                link(nc.vector.tensor_reduce(rank, beats[:, 0], AX.X, ALU.add))
                link(ts(rank, rank, TOP_GROUPS - 0.5, NEVER, ALU.is_gt, ALU.mult))
                bs = biased[:, st, :].rearrange("p (g n) -> p g n", n=PER_GROUP)
                link(tt(bs, bs, rank.unsqueeze(2).broadcast_to([P, GROUPS, PER_GROUP]), ALU.add))
                link(nc.vector.max(best, biased[:, st, :]))
                link(nc.vector.match_replace(out=chosen[:, st, :], in_to_replace=best, in_values=biased[:, st, :],
                                             imm_value=3 * NEVER))
                link(ts(chosen[:, st, :], chosen[:, st, :], 2 * NEVER, None, ALU.is_lt))
                link(tt(chosen[:, st, :], chosen[:, st, :], scores[:, st, :], ALU.mult))
                link(nc.vector.tensor_reduce(tot, chosen[:, st, :], AX.X, ALU.add))
                link(nc.vector.reciprocal(tot, tot))
                link(ts(gate[:, st, 1:], chosen[:, st, :], tot, ROUTED_SCALE, ALU.mult, ALU.mult))

            def act_step(b, k):
                stt(out=acts[:, b, :], in0=silu[:, b, :], scalar=gate[:, b, k], in1=bank(4 + b, FF, 2 * FF),
                    op0=ALU.mult, op1=ALU.mult).then_inc(s["act_done"], 1)

            for st in range(STREAMS):
                dve.wait_ge(s["silu_done"], st + 1)
                act_step(st, slice(0, 1))
            with dve.Fori(0, EXPERTS // SLOTS) as i:
                for q in range(STEPS):
                    dve.wait_ge(s["silu_done"], i * STEPS + q + 3)
                    dve.wait_ge(s["actT_shown"], i * STEPS + q + 1)
                    act_step(q % 2, bass.ds(i * SLOTS + (q // 2 + 1), 1))
            dve.wait_ge(s["down_done"], 2 * EXPERTS + 3)
            for st in range(STREAMS):
                link(tt(tmflat, two(2 * st), g2[:, st, :], ALU.mult))
                link(tt(x[:, st, :], x[:, st, :], tmflat, ALU.add))

        @block.gpsimd
        def _(pool):
            pool.wait_ge(s["attn_in"], 16 * N_ATTN)
            nc.gpsimd.tensor_tensor(biasr, biasr, maskr[:].unsqueeze(1).broadcast_to([P, HEADS, P]), ALU.add)\
              .then_inc(s["bias_ready"], 1)
            pool.wait_ge(s["small_in"], 16 * N_SMALL)
            pool.wait_ge(s["nq_ready"], 1)
            nc.gpsimd.tensor_tensor(kco.rearrange("p (h d) -> p h d", h=HEADS),
                                    nq[:, 0, 256:512].rearrange("p (h d) -> p h d", h=HEADS),
                                    gk[:].unsqueeze(1).broadcast_to([P, HEADS, DK]), ALU.mult).then_inc(s["kco_ready"], 1)
            pool.wait_ge(s["kco_ready"], 1)
            dma_in(pool, A["new_cache_na_k"][0, layer].rearrange("h t d -> t h d"),
                   kco.rearrange("p (h d) -> p h d", h=HEADS), s["stored"])
            dma_in(pool, A["new_cache_na_v"][0, layer].rearrange("h t d -> t h d"),
                   nax[:, 0, 512:768].rearrange("p (h d) -> p h d", h=HEADS), s["stored"])
            pool.wait_ge(s["st_kept"], 1)
            for dr in range(2):
                dma_in(pool, A["new_state_gla"][0, layer, dr].rearrange("h d v -> d h v"),
                       hflat[0:DK, 512 * dr:512 * (dr + 1)].rearrange("p (h v) -> p h v", h=HEADS), s["stored"])
            pool.wait_ge(s["stored"], layer * (16 * STORES) + 16 * STORES)

    with nc.Block() as block:
        @block.gpsimd
        def _(pool):
            for name in SIGNALS:
                if name not in ("stored", "const_step", "x_loaded", "c_sig", "c_step", "y_out"):
                    pool.sem_clear(s[name])
    layers.__exit__(None, None, None)

    with nc.Block() as block:
        @block.sync
        def _(sp):
            sp.dma_start(A["y_prompt"][0], x[:, 0, :]).then_inc(s["y_out"], 16)
            sp.dma_start(A["y_sample"][0], x[:, 1, :]).then_inc(s["y_out"], 16)
            sp.wait_ge(s["y_out"], 32)


_INS = ["x_prompt", "x_sample", "state_gla", "cache_na_k", "cache_na_v", "c", "c_ctx", "w_ada", "b_ada", "norm_mix",
        "norm_ffn", "w_in", "gla_w_gate", "gla_b_gate", "gla_out_norm", "conv_dw", "conv_dw_b", "conv_ln_g",
        "conv_ln_b", "conv_pw", "na_q_norm", "na_k_norm", "na_rpb", "w_out", "router_w", "router_bias", "exp_w_gate",
        "exp_w_up", "exp_w_down", "sh_w_gate", "sh_w_up", "sh_w_down"]
_OUTS = [("y_prompt", (1, 128, 1024)), ("y_sample", (1, 128, 1024)), ("new_state_gla", (1, 2, 2, 4, 64, 128)),
         ("new_cache_na_k", (1, 2, 4, 128, 64)), ("new_cache_na_v", (1, 2, 4, 128, 64))]


def kernel(**inputs):
    import numpy as _np
    import concourse.bacc as _bacc
    from concourse.bass_utils import run_bass_kernel_spmd as _run

    nc = _bacc.Bacc("TRN2", target_bir_lowering=False, num_devices=1)
    arrays, tensors = {}, {}
    for name in _INS:
        a = _np.ascontiguousarray(inputs[name])
        arrays[f"in_{name}"] = a
        tensors[name] = nc.dram_tensor(f"in_{name}", a.shape, F32, kind="ExternalInput").ap()
    for name, shape in _OUTS:
        tensors[name] = nc.dram_tensor(f"out_{name}", shape, F32, kind="ExternalOutput").ap()
    build(nc, tensors)
    r = _run(nc, [arrays], core_ids=[0])
    return tuple(r.results[0][f"out_{name}"] for name, _ in _OUTS)
```

```python
import concourse.bass as bass
from concourse import mybir

F32 = mybir.dt.float32
BF16 = mybir.dt.bfloat16
ALU = mybir.AluOpType
ACT = mybir.ActivationFunctionType
AX = mybir.AxisListType

P = 128
D = 1024
KT = D // P
DEPTH = 2
STREAMS = 2
HEADS = 4
DK = 64
DV = 128
PAIRS = HEADS // 2
RANK = 16
CONV_CH = 256
TAPS = 31
HALO = TAPS // 2
GRID_W = 64
WIN_ROWS = 8
WIN_COLS = 16
RPB_COLS = 2 * WIN_COLS - 1
RPB_HEAD = (2 * WIN_ROWS - 1) * RPB_COLS
IN_WIDTH = 2848
EXPERTS = 64
GROUPS = 8
PER_GROUP = EXPERTS // GROUPS
TOP_K = 8
TOP_GROUPS = 4
FF = 256
ROUTED_SCALE = 2.5
EPS = 1e-6
LEVELS = 7
NEVER = -1e30

SLOTS = 4
SLOT = 3 * KT * FF
ADA_CHUNKS = 12
IN_CHUNKS = [(1536, 544), (0, 512), (512, 512), (2080, 768), (1024, 512)]
OUT_CHUNKS = 2
PRE = ADA_CHUNKS + len(IN_CHUNKS) + OUT_CHUNKS + 1
PRE_SLOTS = 3

C_IN = ADA_CHUNKS
C_OUT = C_IN + len(IN_CHUNKS)
C_SH = PRE - 1

UNITS_IN = [(0, 0, 2 * RANK, True, None)] + [(0, 2 * RANK + P * j, P, True, None) for j in range(4)]
UNITS_IN += [(1, P * j, P, True, None) for j in range(4)]
UNITS_IN += [(2, 0, 512, False, st) for st in range(STREAMS)]
UNITS_IN += [(3, c0, w, False, st) for st in range(STREAMS) for c0, w in ((0, 512), (512, 256))]
UNITS_IN += [(4, 0, 512, False, st) for st in range(STREAMS)]
LAST_UNIT = [max(u for u, unit in enumerate(UNITS_IN) if unit[0] == c) for c in range(len(IN_CHUNKS))]
PROJ_BANKS = (2, 3, 6, 7)
STORES = 4
CAP = (96, 32)
FIRST = (0, CAP[0])
TILES = ((0, 64, 0), (64, 32, 0), (96, 32, 1))
SKEW = CAP[0] // CAP[1]
PASSES = STREAMS * P // CAP[1]
EPAIRS = EXPERTS // 2
TURN = SLOTS // 2

R_DW, R_DWB, R_LNG, R_LNB, R_ON, R_QN, R_KN, R_END = 0, 31, 32, 33, 34, 35, 36, 37


SIGNALS = """x_loaded const_step c_sig c_step small_in vec_in norm_in attn_in shared_in chunk_in0 chunk_in1 chunk_in2
expert_in0 expert_in1 expert_in2 expert_in3 act_step dve_step ada_done ada_kept bias_in square_done var_ready
root_ready mod_shown h_ready hT_shown hT_ready vec_shown vec_ready proj_done proj_kept z_shown la_log la_ready
conv_sig tap conv_ready convT_shown ctok_ready convB_shown conv_neg cact_ready pw_shown cat_conv nq_ready
kco_ready nT_shown nT_ready bias_ready scores_shown max_ready p_exp p_ready pT_shown pT_ready pv_shown cat_na
gg_sig decay_shown E_ready X_ready pair_shown masked att_ready o_shown go_ready goT_shown cat_gla st_pre
st_exp kd_ready st_shown st_kept mix_shown x_mid logits_shown scored g2_shown g2_kept stored y_out hs1 hs2 hs3 ordered tables_shown
tables_kept sorted_shown order_ready over_want
rest1 rest2 chosen_ready counted places sh_gu sh_silu sh_act sh_turned sh_kept sh_done moe_zero G_ready
S_ready X_shown X_kept gu_done gu_free silu_done act_done turned turn_kept Y_shown Y_kept scattered over_G over_GS over_Xs
over_Xk over_gu over_silu over_act over_turned over_kept over_Ys over_Yk over_done over_left""".split()


def rpb_window(rpb, layer, head, half):
    flat = rpb.rearrange("l h r c -> l (h r c)")
    first = head * RPB_HEAD + (WIN_ROWS - 2 + half) * RPB_COLS + (WIN_COLS - 1) - (GRID_W - 1)
    row = flat[layer, first:first + 1]
    ap = [list(d) for d in row.ap]
    return bass.AP(row.tensor, row.offset, [[1, GRID_W], [RPB_COLS, 2], [1, GRID_W]])


def expert_slot(e):
    return (e + 2) % SLOTS


def build(nc, A):
    def sb(name, shape, dt=F32):
        return nc.alloc_sbuf_tensor(name, shape, dt)

    s = {name: nc.alloc_semaphore(name) for name in SIGNALS}

    ring = sb("ring", [P, SLOTS, SLOT])
    x = sb("x", [P, STREAMS, D])
    ada = sb("ada", [P, ADA_CHUNKS, P])
    h = sb("h", [P, STREAMS, D])
    gbc = sb("gbc", [P, D])
    hT = sb("hT", [P, KT, STREAMS * P])
    mid = sb("mid", [P, 5120])
    qT = mid[:, 0:512].rearrange("p (a n) -> p a n", a=PAIRS)
    kT = mid[:, 512:1024].rearrange("p (a n) -> p a n", a=PAIRS)
    v = mid[:, 1024:2048].rearrange("p (s n) -> p s n", s=STREAMS)
    gg = mid[:, 2048:3072].rearrange("p (s n) -> p s n", s=STREAMS)
    la = mid[:, 3072:4096].rearrange("p (s a n) -> p s a n", s=STREAMS, a=2)
    ci = mid[:, 4096:5120].rearrange("p (a n) -> p a n", a=4)
    lrT = sb("lrT", [33, STREAMS * P])
    nax = sb("nax", [P, STREAMS, 3 * HEADS * DK])
    cat = sb("cat", [P, KT, STREAMS * P])
    sm = sb("sm", [P, 256])
    ident = sb("ident", [P, P])
    flip = sb("flip", [P, P])
    pick = sb("pick", [P, 4, STREAMS, P])
    mf = sb("mf", [P, LEVELS + 1, P])
    mb = sb("mb", [P, LEVELS + 1, P])
    suf = sb("suf", [P, 2, P])
    maskf = sb("maskf", [P, LEVELS + 1, P], BF16)
    maskb = sb("maskb", [P, LEVELS, P], BF16)
    maskr = sb("maskr", [P, P])
    tri8 = sb("tri8", [P, GROUPS, GROUPS])
    zero = sb("zero", [P, P])
    cs = sb("cs", [P, KT, 32])
    craw = sb("craw", [P, 3, 2, KT])
    vec = sb("vec", [R_END, CONV_CH])
    vecT = sb("vecT", [P, 2, R_END])
    wg = sb("wg", [33, 2 * HEADS * DK])
    s0 = sb("s0", [P, 2, HEADS, DV])
    gk = sb("gk", [P, DK])
    wpw = sb("wpw", [P, 2, CONV_CH])
    wr = sb("wr", [P, KT, EXPERTS])
    rbias = sb("rbias", [P, EXPERTS])
    hpad = sb("hpad", [P, 2, STREAMS, P + 2 * HALO])
    gate = sb("gate", [P, STREAMS, EXPERTS + 4])
    ones = sb("ones", [P, P])
    wanted = sb("wanted", [P, 2, P])
    want = sb("want", [P, P])
    rank_at = sb("rank_at", [P, EXPERTS])
    expert_no = sb("expert_no", [P, EXPERTS])

    class Scratch:
        def __init__(self, base):
            self.base, self.at = base, 0

        def take(self, n):
            self.at += n
            return self.base[:, self.at - n:self.at]

    arena = Scratch(ring[:, 3, :])
    cacc = arena.take(512).rearrange("p (c s t) -> p c s t", c=2, s=2)
    csig = arena.take(512).rearrange("p (c n) -> p c n", c=2)
    biasr = arena.take(512).rearrange("p (h k) -> p h k", h=HEADS)
    kvc = arena.take(512).rearrange("p (a n) -> p a n", a=2)
    kcT = arena.take(256).rearrange("p (a n) -> p a n", a=PAIRS)
    qnT = arena.take(512).rearrange("p (a n) -> p a n", a=PAIRS)
    knT = arena.take(512).rearrange("p (a n) -> p a n", a=PAIRS)
    p0 = arena.take(512).rearrange("p (h k) -> p h k", h=HEADS)
    p1 = arena.take(1024).rearrange("p (h k) -> p h k", h=HEADS)
    kd = arena.take(512).rearrange("p (a n) -> p a n", a=2)
    kco = arena.take(HEADS * DK)
    att = p0.rearrange("p (b e) i -> p b e i", b=2)
    att2 = p1[:, 0, :]
    qd = p1[:, 2:4, :].rearrange("p b (r i) -> p b r i", r=2)
    assert arena.at <= SLOT
    sq = h[:, :, :].rearrange("p s n -> p (s n)")[:, 0:1024].rearrange("p (s n) -> p s n", s=2)
    nq = h[:, :, :].rearrange("p s n -> p (s n)")[:, 1024:2048].rearrange("p (s n) -> p s n", s=2)
    pT = hT[:, :, :].rearrange("p k n -> p (k n)")[:, 0:12 * P].rearrange("p (b n) -> p b n", n=P)
    E = h[:, :, :].rearrange("p s (l n) -> p s l n", n=P)
    X = hT[:, :, :].rearrange("p k n -> p (k n)").rearrange("p (b l n) -> p b l n", b=2, n=P)
    tm = sb("tm", [P, LEVELS + 1, P])
    hflat = h[:, :, :].rearrange("p s n -> p (s n)")
    cTok = tm[:, 0:4, :].rearrange("p (s a) n -> p s (a n)", s=2)
    cSq = tm[:, 4:8, :].rearrange("p (s a) n -> p s (a n)", s=2)
    g2 = cat[:, :, :].rearrange("p k n -> p (k n)").rearrange("p (s n) -> p s n", s=2)
    silu = qT[:, :, :]
    acts = kT[:, :, :]
    turn = v[:, 0, :]
    turn_over = v[:, 1, :]
    sh_actT = v[:, :, 0:FF]
    hs = mid[:, 2048:5120].bitcast(BF16).rearrange("p (c s k n) -> p c s k n", c=3, s=STREAMS, k=KT)
    X_e = h[:, :, :].rearrange("p s (k n) -> p s k n", k=KT)
    hTf = hT[:, :, :].rearrange("p k n -> p (k n)")
    Y, Y_over = hTf[:, 0:D], hTf[:, D:2 * D]
    tmf = tm[:].rearrange("p l n -> p (l n)")
    G = [tmf[:, 128 * b:128 * (b + 1)].bitcast(BF16).rearrange("p (s n) -> p s n", s=STREAMS)
         for b in range(3)]
    S = [tmf[:, 384 + 256 * b:384 + 256 * (b + 1)].rearrange("p (s n) -> p s n", s=STREAMS)
         for b in range(2)]
    tables = tmf[0:EXPERTS, 0:4 * P].rearrange("p (a n) -> p a n", a=4)
    naf = nax[:].rearrange("p s n -> p (s n)")
    scores = naf[:, 0:128].rearrange("p (s n) -> p s n", s=2)
    biased = naf[:, 128:256].rearrange("p (s n) -> p s n", s=2)
    chosen = naf[:, 256:384].rearrange("p (s n) -> p s n", s=2)
    top = naf[:, 384:512].rearrange("p (s g n) -> p s g n", s=2, n=8)
    beats = naf[:, 512:640].rearrange("p (b g n) -> p b g n", b=2, n=8)
    grp = naf[:, 640:656].rearrange("p (s g) -> p s g", s=2)
    place = naf[:, 700:836].rearrange("p (s e) -> p s e", s=2)
    load = naf[0:EXPERTS, 836:900]
    most = naf[0:EXPERTS, 900:932]
    most_i = naf[0:EXPERTS, 932:964].bitcast(mybir.dt.int32)
    own_load = naf[0:EXPERTS, 1092:1156]
    own_key = naf[0:EXPERTS, 1156:1220]
    keys = naf[0:EXPERTS, 1220:1284]
    order = naf[0:EXPERTS, 1284:1348]
    order_i = naf[0:EXPERTS, 1348:1412].bitcast(mybir.dt.int32)
    load_rank = naf[0:EXPERTS, 1412:1413]
    sel = naf[:, 964:1092].rearrange("p (s e) -> p s e", s=2)
    rank, best, tot = naf[:, 656:664], naf[:, 664:672], naf[:, 672:673]
    ps = nc.alloc_psum_tensor("ps", [P, 8, 512], F32)

    def bank(b, lo=0, hi=512):
        return ps[:, b, lo:hi]

    with nc.Block() as block:
        @block.gpsimd
        def _(pool):
            count = [0]

            def link(ins):
                count[0] += 1
                ins.then_inc(s["const_step"], 1)
                pool.wait_ge(s["const_step"], count[0])

            def keep(view, cond, fill, base, pattern, mult):
                link(nc.gpsimd.affine_select(out=view, in_=view, compare_op=cond, fill=fill, base=base,
                                             pattern=pattern, channel_multiplier=mult))

            for t, val in ((ident, 0.0), (flip, 0.0), (pick, 0.0), (mf, 1.0), (mb, 1.0), (suf, 1.0), (maskf, 1.0),
                           (maskb, 1.0), (maskr, 0.0), (tri8, 1.0), (zero, 0.0), (cs, 0.0), (s0, 0.0), (wg, 0.0),
                           (lrT, 1.0), (hpad, 0.0), (gate, 0.0), (ones, 1.0)):
                link(nc.gpsimd.memset(t[:], val))
            for first, cap in zip(FIRST, CAP):
                link(nc.gpsimd.iota(wanted[:, 0, first:first + cap], [[1, cap]], base=0, channel_multiplier=0,
                                    allow_small_or_imprecise_dtypes=True))
                link(nc.gpsimd.memset(wanted[:, 1, first:first + cap], float(cap)))
            link(nc.gpsimd.iota(rank_at[:, 0::2], [[1, EPAIRS]], base=0, channel_multiplier=0,
                                allow_small_or_imprecise_dtypes=True))
            link(nc.gpsimd.iota(rank_at[:, 1::2], [[-1, EPAIRS]], base=EXPERTS - 1, channel_multiplier=0,
                                allow_small_or_imprecise_dtypes=True))
            link(nc.gpsimd.iota(expert_no[:], [[0, EXPERTS]], base=0, channel_multiplier=1,
                                allow_small_or_imprecise_dtypes=True))
            keep(ident[:], ALU.not_equal, 1.0, 0, [[-1, P]], 1)
            keep(flip[:], ALU.not_equal, 1.0, -(P - 1), [[1, P]], 1)
            for c in range(4):
                for st in range(STREAMS):
                    keep(pick[:, c, st, :], ALU.not_equal, 1.0, -(32 * c + st), [[0, P]], 1)
                    keep(pick[:, c, st, :], ALU.not_equal, 1.0, -(32 * c + 2), [[0, P]], 1)
            for lv in range(LEVELS):
                w = P >> (lv + 1)
                nb = P // (2 * w)
                early = [t[:, lv, :].rearrange("p (b a r) -> p b a r", a=2, r=w)[:, :, 0, :] for t in (mf, mb, maskf, maskb)]
                late = [t[:, lv, :].rearrange("p (b a r) -> p b a r", a=2, r=w)[:, :, 1, :] for t in (mf, mb, maskf, maskb)]
                blocks = [[-2 * w, nb], [0, w]]
                blocks_up = [[2 * w, nb], [0, w]]
                tok = [[-2 * w, nb], [-1, w]]
                tok_up = [[2 * w, nb], [1, w]]
                keep(late[0], ALU.is_ge, 0.0, -w, blocks, 1)
                keep(late[0], ALU.is_ge, 0.0, w, tok_up, -1)
                keep(early[0], ALU.is_ge, 0.0, -1, tok, 1)
                keep(early[0], ALU.is_ge, 0.0, w - 1, blocks_up, -1)
                keep(early[1], ALU.is_ge, 0.0, 0, tok, 1)
                keep(early[1], ALU.is_ge, 0.0, w - 1, blocks_up, -1)
                keep(late[1], ALU.is_ge, 0.0, -w, blocks, 1)
                keep(late[1], ALU.is_ge, 0.0, w - 1, tok_up, -1)
                keep(late[2], ALU.is_ge, 0.0, 0, blocks, 1)
                keep(late[2], ALU.is_ge, 0.0, w - 1, blocks_up, -1)
                link(nc.gpsimd.memset(early[2], 0.0))
                keep(early[3], ALU.is_ge, 0.0, -w, blocks, 1)
                keep(early[3], ALU.is_ge, 0.0, 2 * w - 1, blocks_up, -1)
                link(nc.gpsimd.memset(late[3], 0.0))
            keep(mf[:, LEVELS, :], ALU.is_ge, 0.0, 0, [[1, P]], -1)
            keep(mb[:, LEVELS, :], ALU.is_ge, 0.0, 0, [[-1, P]], 1)
            keep(suf[:, 0, :], ALU.is_ge, 0.0, -1, [[-1, P]], 1)
            keep(suf[:, 1, :], ALU.is_ge, 0.0, -1, [[1, P]], -1)
            link(nc.gpsimd.memset(maskf[:, LEVELS, :], 0.0))
            keep(maskf[:, LEVELS, :], ALU.not_equal, 2.0, 0, [[-1, P]], 1)
            for half in range(2):
                rows = maskr[64 * half:64 * half + 64, :].rearrange("p (r k) -> p r k", k=GRID_W)
                link(nc.gpsimd.affine_select(out=rows[:, :, 0:48], in_=rows[:, :, 0:48], compare_op=ALU.is_ge,
                                             fill=NEVER, base=-(GRID_W - 1 - 8), pattern=[[0, 2], [1, 48]],
                                             channel_multiplier=1))
                link(nc.gpsimd.affine_select(out=rows[:, :, 16:64], in_=rows[:, :, 16:64], compare_op=ALU.is_ge,
                                             fill=NEVER, base=GRID_W - 1 + 7 - 16, pattern=[[0, 2], [-1, 48]],
                                             channel_multiplier=-1))
            keep(tri8[:], ALU.is_ge, 0.0, -1, [[1, GROUPS], [-1, GROUPS]], 0)

        @block.sync
        def _(sp):
            for st, name in ((0, "x_prompt"), (1, "x_sample")):
                sp.dma_start(x[:, st, :], A[name][0]).then_inc(s["x_loaded"], 16)
            sp.dma_start(craw[:, 0, 0, :], A["c_ctx"].rearrange("(p k) -> p k", k=KT)).then_inc(s["x_loaded"], 16)
            sp.dma_start(craw[:, 0, 1, :], A["c"][0].rearrange("(p k) -> p k", k=KT)).then_inc(s["x_loaded"], 16)
            sp.wait_ge(s["x_loaded"], 64)

        @block.scalar
        def _(act):
            act.wait_ge(s["x_loaded"], 64)
            nc.scalar.activation(craw[:, 1], craw[:, 0], ACT.Sigmoid).then_inc(s["c_sig"], 1)

        @block.vector
        def _(dve):
            dve.wait_ge(s["c_sig"], 1)
            dve.wait_ge(s["const_step"], 18)
            nc.vector.tensor_tensor(cs[:, :, 0:2].rearrange("p k s -> p s k"), craw[:, 0], craw[:, 1],
                                    ALU.mult).then_inc(s["c_step"], 1)

    def dma_in(eng, out, in_, sem):
        eng.dma_start(out, in_).then_inc(sem, 16)

    def pre_slot(n):
        return n % PRE_SLOTS

    def pre_loaded(eng, n):
        eng.wait_ge(chunk_in[pre_slot(n)], 16 * (n // PRE_SLOTS + 1))

    def load_gate_up(eng, slot, weights, sem):
        for j, w in enumerate(weights):
            dma_in(eng, slot[:, KT * FF * j:KT * FF * (j + 1)].rearrange("p (k n) -> p k n", k=KT),
                   w.rearrange("(p k) n -> p k n", k=KT), sem)

    def load_down(eng, slot, w, sem):
        dma_in(eng, slot[:, 2 * KT * FF:SLOT].rearrange("p (j n) -> p j n", j=2),
               w.rearrange("(p j) n -> p j n", j=2), sem)

    def gate_up(slot, k):
        return slot[:, 0:2 * KT * FF].rearrange("p (a k n) -> p a k n", a=2, k=KT)[:, :, k, :]

    def down(slot, j, half):
        return slot[:, 2 * KT * FF:SLOT].rearrange("p (j n) -> p j n", j=2)[:, j, 512 * half:512 * (half + 1)]

    def chunk_used(eng, n):
        if n < C_IN:
            eng.wait_ge(s["ada_done"], n + 1)
        elif n < C_OUT:
            eng.wait_ge(s["proj_done"], LAST_UNIT[n - C_IN] + 1)
        elif n < C_SH:
            eng.wait_ge(s["mix_shown"], 2 * (n - C_OUT + 1))
        else:
            eng.wait_ge(s["sh_done"], STREAMS)

    chunk_in = [s["chunk_in0"], s["chunk_in1"], s["chunk_in2"]]
    expert_in = [s["expert_in0"], s["expert_in1"], s["expert_in2"], s["expert_in3"]]
    N_SMALL, N_VEC, N_ATTN = 18, 8, 2 * HEADS + 2

    layers = nc.Fori(0, DEPTH)
    layer = layers.__enter__()
    with nc.Block() as block:
        @block.sync
        def _(sp):
            for r0, r1, name in ((R_DW, R_DWB, "conv_dw"),):
                dma_in(sp, vec[r0:r1, :], A[name][layer], s["small_in"])
            for r, name in ((R_DWB, "conv_dw_b"), (R_LNG, "conv_ln_g"), (R_LNB, "conv_ln_b")):
                dma_in(sp, vec[r:r + 1, :], A[name][bass.ds(layer, 1), :], s["small_in"])
            dma_in(sp, vec[R_ON:R_ON + 1, 0:DV], A["gla_out_norm"][bass.ds(layer, 1), :], s["small_in"])
            dma_in(sp, vec[R_ON:R_ON + 1, DV:2 * DV], A["gla_out_norm"][bass.ds(layer, 1), :], s["small_in"])
            for r, name in ((R_QN, "na_q_norm"), (R_KN, "na_k_norm")):
                for j in range(CONV_CH // DK):
                    dma_in(sp, vec[r:r + 1, DK * j:DK * (j + 1)], A[name][bass.ds(layer, 1), :], s["vec_in"])
            dma_in(sp, gbc[:], A["norm_mix"][bass.ds(layer, 1), :].partition_broadcast(P)[:, 0, :], s["norm_in"])
            dma_in(sp, gk[:], A["na_k_norm"][bass.ds(layer, 1), :].partition_broadcast(P)[:, 0, :], s["small_in"])
            for dr in range(2):
                dma_in(sp, wg[RANK * dr:RANK * (dr + 1), 256 * dr:256 * (dr + 1)],
                       A["gla_w_gate"][layer, dr], s["small_in"])
                dma_in(sp, wg[32:33, 256 * dr:256 * (dr + 1)],
                       A["gla_b_gate"][layer, dr:dr + 1, :], s["small_in"])
                for e in range(2):
                    dma_in(sp, s0[DK * e:DK * (e + 1), dr, e::2, :],
                           A["state_gla"][0, layer, dr, e::2].rearrange("h d v -> d h v"), s["small_in"])
            dma_in(sp, wpw[:], A["conv_pw"][layer].rearrange("(c p) n -> p c n", p=P), s["small_in"])
            dma_in(sp, wr[:], A["router_w"][layer].rearrange("(p k) n -> p k n", k=KT), s["small_in"])
            dma_in(sp, rbias[:], A["router_bias"][bass.ds(layer, 1), :].partition_broadcast(P)[:, 0, :], s["small_in"])
            for n in range(PRE):
                if n >= PRE_SLOTS:
                    chunk_used(sp, n - PRE_SLOTS)
                slot = ring[:, pre_slot(n), :]
                sem = chunk_in[pre_slot(n)]
                if n < C_IN:
                    dma_in(sp, slot[:, 0:KT * 512].rearrange("p (k n) -> p k n", k=KT),
                           A["w_ada"][layer, :, 512 * n:512 * (n + 1)].rearrange("(p k) n -> p k n", k=KT), sem)
                elif n < C_OUT:
                    c0, cw = IN_CHUNKS[n - C_IN]
                    dma_in(sp, slot[:, 0:KT * cw].rearrange("p (k n) -> p k n", k=KT),
                           A["w_in"][layer, :, c0:c0 + cw].rearrange("(p k) n -> p k n", k=KT), sem)
                elif n < C_SH:
                    c0 = 512 * (n - C_OUT)
                    dma_in(sp, slot[:, 0:KT * 512].rearrange("p (k n) -> p k n", k=KT),
                           A["w_out"][layer, :, c0:c0 + 512].rearrange("(k p) n -> p k n", p=P), sem)
                else:
                    load_gate_up(sp, slot, [A[w][layer] for w in ("sh_w_gate", "sh_w_up")], s["shared_in"])
                    load_down(sp, slot, A["sh_w_down"][layer], s["shared_in"])
                if n == C_IN + PRE_SLOTS:
                    sp.wait_ge(s["h_ready"], STREAMS)
                    dma_in(sp, gbc[:], A["norm_ffn"][bass.ds(layer, 1), :].partition_broadcast(P)[:, 0, :], s["norm_in"])
                if n == PRE_SLOTS + 1:
                    for half in range(2):
                        for hh in range(HEADS):
                            sp.dma_start(
                                biasr[64 * half:64 * (half + 1), hh, :].rearrange("p (r k) -> p r k", k=GRID_W),
                                rpb_window(A["na_rpb"], layer, hh, half)).then_inc(s["attn_in"], 16)
                    for a, name in enumerate(("cache_na_k", "cache_na_v")):
                        dma_in(sp, kvc[:, a, :].rearrange("p (h d) -> p h d", h=HEADS),
                               A[name][0, layer].rearrange("h t d -> t h d"), s["attn_in"])
            sp.wait_ge(s["order_ready"], 1)
            firsts = [sp.value_load(order_i[0:1, k:k + 1], min_val=0, max_val=EXPERTS - 1) for k in range(SLOTS)]
            for k in range(SLOTS):
                slot = expert_slot(k)
                if slot < PRE_SLOTS:
                    last = max(n for n in range(PRE) if pre_slot(n) == slot)
                    chunk_used(sp, last)
                else:
                    sp.wait_ge(s["st_kept"], 1)
                    sp.wait_ge(s["go_ready"], STREAMS)
                    sp.wait_ge(s["stored"], 16 * STORES * (layer + 1))
                e = firsts[k]
                load_gate_up(sp, ring[:, slot, :],
                             [A[w][layer, bass.ds(e, 1)][0] for w in ("exp_w_gate", "exp_w_up")], expert_in[slot])
                load_down(sp, ring[:, slot, :], A["exp_w_down"][layer, bass.ds(e, 1)][0], expert_in[slot])
            with sp.Fori(1, EXPERTS // SLOTS) as i:
                for pair in range(TURN):
                    e = [sp.value_load(order_i[0:1, bass.ds(i * SLOTS + q, 1)], min_val=0, max_val=EXPERTS - 1)
                         for q in (2 * pair, 2 * pair + 1)]
                    sp.wait_ge(s["gu_free"], i * TURN + pair - TURN + 1)
                    for q in (2 * pair, 2 * pair + 1):
                        load_gate_up(sp, ring[:, expert_slot(q), :],
                                     [A[w][layer, bass.ds(e[q % 2], 1)][0] for w in ("exp_w_gate", "exp_w_up")],
                                     expert_in[expert_slot(q)])
                    sp.wait_ge(s["Y_shown"], i * (2 * TURN) + 2 * (pair - 1))
                    sp.wait_ge(s["over_done"], i * (TURN * (PASSES - 1)) + (PASSES - 1) * (pair - 1))
                    for q in (2 * pair, 2 * pair + 1):
                        load_down(sp, ring[:, expert_slot(q), :],
                                  A["exp_w_down"][layer, bass.ds(e[q % 2], 1)][0], expert_in[expert_slot(q)])

        def rsqrt_dve(dve, link, k, ss, v, r0, t, r, scale):
            nc.vector.tensor_scalar(v, ss, scale, EPS, ALU.mult, ALU.add).then_inc(s["var_ready"], 1)
            dve.wait_ge(s["root_ready"], k + 1)
            link(nc.vector.tensor_tensor(t, r0, r0, ALU.mult))
            link(nc.vector.tensor_tensor(t, t, v, ALU.mult))
            link(nc.vector.tensor_scalar(t, t, -0.5, 1.5, ALU.mult, ALU.add))
            link(nc.vector.tensor_tensor(r, r0, t, ALU.mult))

        def rsqrt_act(act, link, k, v, r0):
            act.wait_ge(s["var_ready"], k + 1)
            link(nc.scalar.activation(r0, v, ACT.Ln))
            nc.scalar.activation(r0, r0, ACT.Exp, scale=-0.5).then_inc(s["root_ready"], 1)

        def numbers(k, part):
            at, n = ((0, 2), (10, 2), (20, 16), (100, 4), (120, 4), (140, 2))[k]
            return sm[:, at + n * part:at + n * (part + 1)]

        N_IN, N_CONV, N_QK, N_GLA, N_FFN = 0, 1, 2, 3, 5
        conv_mean = sm[:, 150:152]
        mx = sm[:, 152:160]
        p_sum = sm[:, 160:168]
        p_inv = sm[:, 168:176]

        @block.tensor
        def _(pe):
            mm = nc.tensor.matmul

            def show(n, st, b):
                for c in range(4):
                    last = mm(bank(b, P * c, P * (c + 1)), pick[:, c, st, :], ada[:, n, :], start=True, stop=True)
                return last

            def modulation(k):
                for st in range(STREAMS):
                    for half in range(2):
                        show(6 * k + 2 + half, st, 4 * st + half)
                    for half in range(2):
                        last = show(6 * k + half, st, 4 * st + 2 + half)
                    last.then_inc(s["mod_shown"], 1)

            def turn_h(k):
                for st in range(STREAMS):
                    pe.wait_ge(s["h_ready"], STREAMS * k + st + 1)
                    ht = h[:, st, :].rearrange("t (p k) -> t k p", k=KT)
                    for kt in range(KT):
                        last = nc.tensor.transpose(bank(4 * st + kt // 4, P * (kt % 4), P * (kt % 4 + 1)),
                                                   ht[:, kt, :], ident[:])
                    last.then_inc(s["hT_shown"], 1)

            for n in range(ADA_CHUNKS):
                pre_loaded(pe, n)
                if n >= 2:
                    pe.wait_ge(s["ada_kept"], n - 1)
                w = ring[:, pre_slot(n), 0:KT * 512].rearrange("p (k n) -> p k n", k=KT)
                for kt in range(KT):
                    for c in range(4):
                        last = mm(ps[32 * c:32 * (c + 1), n % 2, 0:P], cs[:, kt, :], w[:, kt, P * c:P * (c + 1)],
                                  start=(kt == 0), stop=(kt == KT - 1))
                last.then_inc(s["ada_done"], 1)
            pe.wait_ge(s["bias_in"], 64)
            modulation(0)
            turn_h(0)
            pe.wait_ge(s["small_in"], 16 * N_SMALL)
            pe.wait_ge(s["vec_in"], 16 * N_VEC)
            pe.wait_ge(s["hT_ready"], STREAMS)
            for c in range(2):
                last = nc.tensor.transpose(bank(5, 64 * c, 64 * c + R_END), vec[:, P * c:P * (c + 1)],
                                           ident[0:R_END, 0:R_END])
            last.then_inc(s["vec_shown"], 1)
            for u, (c, c0, w, by_channel, st) in enumerate(UNITS_IN):
                if u == 0 or UNITS_IN[u - 1][0] != c:
                    pre_loaded(pe, C_IN + c)
                if u >= len(PROJ_BANKS):
                    pe.wait_ge(s["proj_kept"], u - len(PROJ_BANKS) + 1)
                cw = IN_CHUNKS[c][1]
                wt = ring[:, pre_slot(C_IN + c), 0:KT * cw].rearrange("p (k n) -> p k n", k=KT)[:, :, c0:c0 + w]
                b = PROJ_BANKS[u % len(PROJ_BANKS)]
                for kt in range(KT):
                    if by_channel:
                        last = mm(ps[0:w, b, 0:STREAMS * P], wt[:, kt, :], hT[:, kt, :],
                                  start=(kt == 0), stop=(kt == KT - 1))
                    else:
                        last = mm(bank(b, 0, w), hT[:, kt, P * st:P * (st + 1)], wt[:, kt, :],
                                  start=(kt == 0), stop=(kt == KT - 1))
                last.then_inc(s["proj_done"], 1)
                if u == 4:
                    pe.wait_ge(s["proj_kept"], 1)
                    for st2 in range(STREAMS):
                        mm(bank(st2), lrT[:, P * st2:P * (st2 + 1)], wg[:], start=True,
                           stop=True).then_inc(s["z_shown"], 1)
            pe.wait_ge(s["vec_ready"], 1)
            pe.wait_ge(s["conv_ready"], 1)
            for st in range(STREAMS):
                for c in range(2):
                    at = 256 * st + P * c
                    last = nc.tensor.transpose(bank(4, at, at + P), cacc[:, c, st, :], ident[:])
            last.then_inc(s["convT_shown"], 1)
            pe.wait_ge(s["ctok_ready"], 1)
            for c in range(2):
                for st in range(STREAMS):
                    at = 256 * c + P * st
                    last = nc.tensor.transpose(bank(5, at, at + P), cTok[:, st, P * c:P * (c + 1)], ident[:])
            last.then_inc(s["convB_shown"], 1)
            pe.wait_ge(s["cact_ready"], 1)
            for o in range(2):
                for c in range(2):
                    last = mm(bank(4, 256 * o, 256 * (o + 1)), wpw[:, c, P * o:P * (o + 1)],
                              cacc[:, c, :, :].rearrange("p s t -> p (s t)"), start=(c == 0), stop=(c == 1))
            last.then_inc(s["pw_shown"], 1)
            pe.wait_ge(s["nq_ready"], 1)
            pe.wait_ge(s["proj_kept"], len(UNITS_IN))
            pe.wait_ge(s["attn_in"], 16 * N_ATTN)
            for b, c0 in ((2, 0), (3, 256)):
                for a in range(PAIRS):
                    for st in range(STREAMS):
                        at = 256 * a + P * st
                        nc.tensor.transpose(bank(b, at, at + P), nq[:, st, c0 + P * a:c0 + P * (a + 1)], ident[:])
            for a in range(PAIRS):
                last = nc.tensor.transpose(bank(6, P * a, P * (a + 1)), kvc[:, 0, P * a:P * (a + 1)], ident[:])
            last.then_inc(s["nT_shown"], 1)
            pe.wait_ge(s["nT_ready"], 1)
            pe.wait_ge(s["bias_ready"], 1)
            for e in range(2):
                r = slice(DK * e, DK * (e + 1))
                for a in range(PAIRS):
                    last = mm(bank(2 + e, P * a, P * (a + 1)), qnT[r, a, 0:P], knT[r, a, 0:P], start=True, stop=True)
            last.then_inc(s["scores_shown"], 1)
            for e in range(2):
                r = slice(DK * e, DK * (e + 1))
                for a in range(PAIRS):
                    local = bank(6 + e, 256 * a, 256 * a + P)
                    mm(local, qnT[r, a, P:2 * P], knT[r, a, P:2 * P], start=True, stop=False)
                    mm(local, flip[:], biasr[:, 2 * a + e, :], start=False, stop=True)
                    last = mm(bank(6 + e, 256 * a + P, 256 * (a + 1)), qnT[r, a, P:2 * P], kcT[r, a, :],
                              start=True, stop=True)
            last.then_inc(s["scores_shown"], 1)
            pe.wait_ge(s["p_ready"], 1)
            pe.wait_ge(s["la_ready"], STREAMS)
            blocks = [(p0[:, i, :]) for i in range(HEADS)]
            blocks += [p1[:, i, P * j:P * (j + 1)] for i in range(HEADS) for j in range(2)]
            for i, block_in in enumerate(blocks):
                last = nc.tensor.transpose(bank(i // 4, P * (i % 4), P * (i % 4 + 1)), block_in, ident[:])
            last.then_inc(s["pT_shown"], 1)
            pe.wait_ge(s["pT_ready"], 1)
            for e in range(2):
                for a in range(PAIRS):
                    hh, i = 2 * a + e, 2 * e + a
                    c0 = 2 * HEADS * DK + DK * hh
                    out = ps[DK * e:DK * (e + 1), 3, :]
                    mm(out[:, 256 * a:256 * a + P], nax[:, 0, c0:c0 + DK], pT[:, i, :], start=True, stop=True)
                    out1 = out[:, 256 * a + P:256 * (a + 1)]
                    mm(out1, nax[:, 1, c0:c0 + DK], pT[:, HEADS + 2 * i, :], start=True, stop=False)
                    last = mm(out1, kvc[:, 1, DK * hh:DK * (hh + 1)], pT[:, HEADS + 2 * i + 1, :],
                              start=False, stop=True)
            last.then_inc(s["pv_shown"], 1)

            def decays(g):
                st, a, dr = g // 4, g // 2 % 2, g % 2
                if g:
                    pe.wait_ge(s["E_ready"], g)
                m = (mf, mb)[dr]
                for b in range(2):
                    last = mm(bank(b), la[:, st, dr, P * a:P * (a + 1)],
                              m[:, 4 * b:4 * (b + 1), :].rearrange("p l n -> p (l n)"), start=True, stop=True)
                last.then_inc(s["decay_shown"], 1)

            def pairs(g):
                st, a, dr = g // 4, g // 2 % 2, g % 2
                pe.wait_ge(s["X_ready"], g + 1)
                for e in range(2):
                    if g:
                        pe.wait_ge(s["masked"], 2 * (g - 1) + e + 1)
                    r = slice(DK * e, DK * (e + 1))
                    for lv in range(LEVELS + (dr == 0)):
                        out = bank((2, 6)[e] + lv // 4, P * (lv % 4), P * (lv % 4 + 1))
                        if lv < LEVELS:
                            last = mm(out, X[r, dr, lv, :], X[r, dr, lv, :], start=True, stop=True)
                        else:
                            last = mm(out, kT[r, a, P * st:P * (st + 1)], qT[r, a, P * st:P * (st + 1)],
                                      start=True, stop=True)
                    last.then_inc(s["pair_shown"], 1)

            def outputs(g):
                st, a = g // 4, g // 2 % 2
                for e in range(2):
                    pe.wait_ge(s["att_ready"], 2 * (g // 2) + e + 1)
                    hh = 2 * a + e
                    out = bank(4 + st, DV * hh, DV * (hh + 1))
                    last = mm(out, att[:, a, e, :], v[:, st, DV * hh:DV * (hh + 1)], start=True, stop=(st == 0))
                    if st == 1:
                        for dr in range(2):
                            last = mm(out, qd[:, a, dr, :], s0[:, dr, hh, :], start=False, stop=(dr == 1))
                    last.then_inc(s["o_shown"], 1)

            pe.wait_ge(s["cat_na"], 1)
            pe.wait_ge(s["cat_conv"], 1)
            decays(0)
            for g in range(8):
                if g + 1 < 8:
                    decays(g + 1)
                pairs(g)
                if g % 2:
                    outputs(g)
            pe.wait_ge(s["masked"], 16)
            for a in range(PAIRS):
                nc.tensor.transpose(bank(2, P * a, P * (a + 1)), kT[:, a, 0:P], ident[:])
            for dr in range(2):
                last = mm(bank(3, 256 * dr, 256 * (dr + 1)), suf[:, dr, :], la[:, 0, dr, :], start=True, stop=True)
            last.then_inc(s["st_pre"], 1)
            pe.wait_ge(s["kd_ready"], 1)
            for dr in range(2):
                for hh in range(HEADS):
                    last = mm(ps[0:DK, 6 + dr, DV * hh:DV * (hh + 1)], kd[:, dr, DK * hh:DK * (hh + 1)],
                              v[:, 0, DV * hh:DV * (hh + 1)], start=True, stop=True)
            last.then_inc(s["st_shown"], 1)
            for st in range(STREAMS):
                pe.wait_ge(s["go_ready"], st + 1)
                for hh in range(HEADS):
                    last = nc.tensor.transpose(bank(st, P * hh, P * (hh + 1)), gg[:, st, P * hh:P * (hh + 1)], ident[:])
                last.then_inc(s["goT_shown"], 1)
            pe.wait_ge(s["cat_gla"], STREAMS)
            pe.wait_ge(s["st_kept"], 1)
            for half in range(2):
                pre_loaded(pe, C_OUT + half)
                w = ring[:, pre_slot(C_OUT + half), 0:KT * 512].rearrange("p (k n) -> p k n", k=KT)
                for st in range(STREAMS):
                    show(4 + half, st, (4, 5, 0, 1)[2 * half + st])
                    for kt in range(KT):
                        last = mm(bank(PROJ_BANKS[2 * half + st]), cat[:, kt, P * st:P * (st + 1)], w[:, kt, :],
                                  start=(kt == 0), stop=(kt == KT - 1))
                    last.then_inc(s["mix_shown"], 1)
            pe.wait_ge(s["x_mid"], 4)
            modulation(1)
            turn_h(1)
            pe.wait_ge(s["hT_ready"], 2 * STREAMS)
            for st in range(STREAMS):
                for kt in range(KT):
                    last = mm(bank(2 + 4 * st, 0, EXPERTS), hT[:, kt, P * st:P * (st + 1)], wr[:, kt, :],
                              start=(kt == 0), stop=(kt == KT - 1))
                last.then_inc(s["logits_shown"], 1)
            for st in range(STREAMS):
                for half in range(2):
                    last = show(10 + half, st, 4 * st + half)
            last.then_inc(s["g2_shown"], 1)

            pe.wait_ge(s["chosen_ready"], 1)
            pe.wait_ge(s["scored"], STREAMS)
            mm(bank(2, 0, EXPERTS), suf[:, 1, :], sel[:, 0, :], start=True, stop=True)
            mm(bank(2, 64, 64 + EXPERTS), suf[:, 1, :], sel[:, 1, :], start=True, stop=False)
            mm(bank(2, 64, 64 + EXPERTS), ones[:], sel[:, 0, :], start=False, stop=True)
            mm(bank(2, 128, 128 + EXPERTS), ones[:], sel[:, 0, :], start=True, stop=False)
            mm(bank(2, 128, 128 + EXPERTS), ones[:], sel[:, 1, :], start=False, stop=True)
            for st in range(STREAMS):
                last = mm(ps[0:EXPERTS, 2, 192:192 + EXPERTS], sel[:, st, :], ones[:, 0:EXPERTS], start=(st == 0),
                          stop=(st == STREAMS - 1))
            last.then_inc(s["counted"], 1)

            shared = ring[:, pre_slot(C_SH), :]
            pe.wait_ge(s["shared_in"], 48)
            pe.wait_ge(s["g2_kept"], 1)
            for st in range(STREAMS):
                for kt in range(KT):
                    last = mm(bank(4 + st), hT[:, kt, P * st:P * (st + 1)], gate_up(shared, kt),
                              start=(kt == 0), stop=(kt == KT - 1))
                last.then_inc(s["sh_gu"], 1)
                if st == 0:
                    pe.wait_ge(s["ordered"], 1)
                    for st2 in range(STREAMS):
                        nc.tensor.transpose(ps[0:EXPERTS, 6, P * st2:P * (st2 + 1)], place[:, st2, 0:EXPERTS], ident[:])
                        last = nc.tensor.transpose(ps[0:EXPERTS, 6, P * (2 + st2):P * (3 + st2)],
                                                   gate[:, st2, 0:EXPERTS], ident[:])
                    last.then_inc(s["tables_shown"], 1)
                    mm(ps[0:EXPERTS, 7, 256:256 + EXPERTS], expert_no[0:EXPERTS, :], order, start=True, stop=True)
                    mm(ps[0:EXPERTS, 7, 320:320 + EXPERTS], own_load, order, start=True, stop=True)
                    pe.wait_ge(s["tables_kept"], 1)
                    for a in range(4):
                        last = mm(bank(7, EXPERTS * a, EXPERTS * (a + 1)), tables[:, a, :], order, start=True, stop=True)
                    last.then_inc(s["sorted_shown"], 1)
            pe.wait_ge(s["places"], 1)
            for b in range(4):
                mm(bank(b), zero[:], mf[:, 0:4, :].rearrange("p l n -> p (l n)"), start=True, stop=False,
                   skip_group_check=True)

            def gather(X_bank, onehot, half):
                for k in range(KT // 2):
                    for st in range(STREAMS):
                        for part in range(3):
                            last = mm(bank(X_bank, P * k, P * (k + 1)), hs[:, part, st, KT // 2 * half + k, :],
                                      onehot[:, st],
                                      start=(st == 0 and part == 0), stop=(st == STREAMS - 1 and part == 2))
                return last

            def gate_up_pair(b, slots):
                for kt in range(KT):
                    for first, n, c in TILES:
                        last = mm(ps[first:first + n, 4, :], X_e[:, b, kt, first:first + n],
                                  gate_up(ring[:, slots[c], :], kt), start=(kt == 0), stop=(kt == KT - 1))
                return last

            def turn_pair(weights):
                for st in range(STREAMS):
                    nc.tensor.transpose(bank(5, FF + P * st, FF + P * (st + 1)),
                                        weights[:, st], ident[:])

            def turn_acts(b):
                a_in = acts[:, b, :].rearrange("t (p j) -> t j p", j=2)
                for j in range(2):
                    last = nc.tensor.transpose(bank(5, P * j, P * (j + 1)), a_in[:, j, :], ident[:])
                return last

            def down_pair(turned, slots, half):
                for j in range(2):
                    for first, n, c in TILES:
                        last = mm(ps[first:first + n, 7, :], turned[:, P * j + first:P * j + first + n],
                                  down(ring[:, slots[c], :], j, half), start=(j == 0), stop=(j == 1))
                return last

            def scatter(turned, y):
                for st in range(STREAMS):
                    for half in range(2):
                        last = mm(bank(2 * st + half), turned[:, FF + P * st:FF + P * (st + 1)],
                                  y[:, 512 * half:512 * (half + 1)], start=False, stop=False, skip_group_check=True)
                return last

            pe.wait_ge(s["G_ready"], 1)
            pe.wait_ge(s["hs3"], STREAMS)
            gather(6, G[0], 0).then_inc(s["X_shown"], 1)
            for st in range(STREAMS):
                pe.wait_ge(s["sh_act"], st + 1)
                a_in = acts[:, st, :].rearrange("t (p j) -> t j p", j=2)
                for j in range(2):
                    last = nc.tensor.transpose(bank(4 + st, P * j, P * (j + 1)), a_in[:, j, :], ident[:])
                last.then_inc(s["sh_turned"], 1)
            pe.wait_ge(s["X_kept"], 1)
            gather(6, G[0], 1).then_inc(s["X_shown"], 1)
            for st in range(STREAMS):
                pe.wait_ge(s["sh_kept"], st + 1)
                for half in range(2):
                    for j in range(2):
                        last = mm(bank(2 * st + half), sh_actT[:, st, P * j:P * (j + 1)], down(shared, j, half),
                                  start=False, stop=False, skip_group_check=True)
                last.then_inc(s["sh_done"], 1)
            pe.wait_ge(s["moe_zero"], 2)
            with pe.Fori(0, EPAIRS // TURN) as i:
                for q in range(TURN):
                    slots = (expert_slot(2 * q), expert_slot(2 * q + 1))
                    tokens = pe.value_load(most_i[0:1, bass.ds(i * TURN + q, 1)], min_val=0, max_val=SKEW * STREAMS * P)
                    for c in range(2):
                        pe.wait_ge(expert_in[slots[c]], i * 48 + 48)
                    pe.wait_ge(s["X_kept"], i * (2 * TURN) + 2 * q + 2)
                    gate_up_pair(q, slots).then_inc(s["gu_done"], 1)
                    pe.wait_ge(s["Y_kept"], i * (2 * TURN) + 2 * q + 2)
                    scatter(turn, Y).then_inc(s["scattered"], 1)
                    pe.wait_ge(s["S_ready"], i * TURN + q + 1)
                    turn_pair(S[0])
                    pe.wait_ge(s["act_done"], i * TURN + q + 1)
                    turn_acts(0).then_inc(s["turned"], 1)
                    with pe.If(tokens < CAP[0] + 1):
                        pe.wait_ge(s["gu_done"], i * TURN + q + 1)
                        pe.sem_inc(s["gu_free"], 1)
                    pe.wait_ge(s["G_ready"], i * TURN + q + 2)
                    gather(6, G[1 - q], 0).then_inc(s["X_shown"], 1)
                    pe.wait_ge(s["turn_kept"], i * TURN + q + 1)
                    down_pair(turn, slots, 0).then_inc(s["Y_shown"], 1)
                    pe.wait_ge(s["X_kept"], i * (2 * TURN) + 2 * q + 3)
                    gather(6, G[1 - q], 1).then_inc(s["X_shown"], 1)
                    pe.wait_ge(s["Y_kept"], i * (2 * TURN) + 2 * q + 3)
                    down_pair(turn, slots, 1).then_inc(s["Y_shown"], 1)
                    with pe.If(tokens > CAP[0]):
                        with pe.Fori(1, PASSES) as r:
                            m = (i * TURN + q) * (PASSES - 1) + r
                            with pe.If(tokens > r * CAP[0]):
                                pe.wait_ge(s["X_kept"], i * (2 * TURN) + 2 * q + 4)
                                pe.wait_ge(s["Y_kept"], i * (2 * TURN) + 2 * q + 4)
                                pe.wait_ge(s["over_GS"], m)
                                gather(6, G[2], 0).then_inc(s["over_Xs"], 1)
                                pe.wait_ge(s["over_Xk"], m * 2 - 1)
                                gather(6, G[2], 1).then_inc(s["over_Xs"], 1)
                                turn_pair(S[1])
                                pe.wait_ge(s["over_Xk"], m * 2)
                                gate_up_pair(q, slots).then_inc(s["over_gu"], 1)
                                pe.wait_ge(s["over_act"], m)
                                turn_acts(1).then_inc(s["over_turned"], 1)
                                pe.wait_ge(s["over_kept"], m)
                                down_pair(turn_over, slots, 0).then_inc(s["over_Ys"], 1)
                                pe.wait_ge(s["over_Yk"], m * 2 - 1)
                                down_pair(turn_over, slots, 1).then_inc(s["over_Ys"], 1)
                                pe.wait_ge(s["over_Yk"], m * 2)
                                scatter(turn_over, Y_over).then_inc(s["over_done"], 1)
                                pe.wait_ge(s["over_done"], m)
                                pe.sem_inc(s["over_left"], 1)
                            with pe.Else():
                                for name, k in (("over_Xs", 2), ("over_gu", 1), ("over_turned", 1), ("over_Ys", 2),
                                                ("over_done", 1)):
                                    pe.sem_inc(s[name], k)
                        pe.sem_inc(s["gu_free"], 1)
                    with pe.Else():
                        for name, k in (("over_Xs", 2), ("over_gu", 1), ("over_turned", 1), ("over_Ys", 2),
                                        ("over_done", 1)):
                            pe.sem_inc(s[name], k * (PASSES - 1))
            pe.wait_ge(s["Y_kept"], 2 * EPAIRS + 2)
            scatter(turn, Y).then_inc(s["scattered"], 1)

        @block.scalar
        def _(act):
            count = [0]

            def link(ins):
                count[0] += 1
                ins.then_inc(s["act_step"], 1)
                act.wait_ge(s["act_step"], count[0])

            def two(b):
                return ps[:, b:b + 2, :].rearrange("p b n -> p (b n)")

            def squares(k):
                for st in range(STREAMS):
                    last = nc.scalar.activation(h[:, st, :], x[:, st, :], ACT.Square,
                                                accum_out=numbers(k, 0)[:, st:st + 1])
                last.then_inc(s["square_done"], 1)

            def keep_hT(k):
                for st in range(STREAMS):
                    act.wait_ge(s["hT_shown"], STREAMS * k + st + 1)
                    nc.scalar.copy(hT[:, :, P * st:P * (st + 1)], two(4 * st).rearrange("p (k n) -> p k n", n=P))\
                      .then_inc(s["hT_ready"], 1)

            squares(0)
            rsqrt_act(act, link, N_IN, numbers(N_IN, 1), numbers(N_IN, 2))
            for n in range(ADA_CHUNKS):
                act.wait_ge(s["ada_done"], n + 1)
                nc.scalar.copy(ada[:, n, :], bank(n % 2, 0, P)).then_inc(s["ada_kept"], 1)
            act.wait_ge(s["ada_kept"], ADA_CHUNKS)
            for c in range(4):
                dma_in(act, ada[32 * c + 2:32 * c + 3, :, :],
                       A["b_ada"][bass.ds(layer, 1), :].rearrange("l (n c m) -> l n c m", c=4, m=P)[:, :, c, :],
                       s["bias_in"])
            keep_hT(0)
            act.wait_ge(s["vec_shown"], 1)
            nc.scalar.copy(vecT[:], bank(5, 0, 2 * 64).rearrange("p (c r) -> p c r", c=2)[:, :, 0:R_END])\
              .then_inc(s["vec_ready"], 1)
            for u, (c, c0, w, by_channel, st) in enumerate(UNITS_IN):
                act.wait_ge(s["proj_done"], u + 1)
                b = PROJ_BANKS[u % len(PROJ_BANKS)]
                wide = bank(b, 0, STREAMS * P)
                if u == 0:
                    last = nc.scalar.copy(lrT[0:2 * RANK, :], ps[0:2 * RANK, b, 0:STREAMS * P])
                elif c == 0:
                    last = nc.scalar.copy(ci[:, u - 1, :], wide)
                elif c == 1 and u < 7:
                    last = nc.scalar.mul(qT[:, u - 5, :], wide, float(DK) ** -0.5)
                elif c == 1:
                    last = nc.scalar.copy(kT[:, u - 7, :], wide)
                else:
                    last = nc.scalar.copy(((v, nax, gg)[c - 2])[:, st, c0:c0 + w], bank(b, 0, w))
                last.then_inc(s["proj_kept"], 1)
                if u == 4:
                    for st2 in range(STREAMS):
                        act.wait_ge(s["z_shown"], st2 + 1)
                        z = la[:, st2, :, :].rearrange("p a n -> p (a n)")
                        link(nc.scalar.activation(z, bank(st2), ACT.Abs))
                        link(nc.scalar.activation(z, z, ACT.Exp, scale=-1.0))
                        nc.scalar.activation(z, z, ACT.Ln, bias=1.0).then_inc(s["la_log"], 1)
                    act.wait_ge(s["proj_kept"], 5)
                    nc.scalar.activation(csig, ci[:, 2:4, :], ACT.Sigmoid).then_inc(s["conv_sig"], 1)
            rsqrt_act(act, link, N_CONV, numbers(N_CONV, 1), numbers(N_CONV, 2))
            act.wait_ge(s["convB_shown"], 1)
            for c in range(2):
                y = cacc[:, c, :, :].rearrange("p s t -> p (s t)")
                nc.scalar.activation(y, bank(5, 256 * c, 256 * (c + 1)), ACT.Identity,
                                     scale=vecT[:, c, R_LNG:R_LNG + 1], bias=vecT[:, c, R_LNB:R_LNB + 1])\
                  .then_inc(s["conv_neg"], 1)
            act.wait_ge(s["conv_neg"], 2)
            nc.scalar.activation(csig, cacc[:].rearrange("p c s t -> p c (s t)"), ACT.Sigmoid)\
              .then_inc(s["conv_sig"], 1)
            act.wait_ge(s["pw_shown"], 1)
            nc.scalar.copy(cat[:, 4:6, :], bank(4).rearrange("p (o n) -> p o n", o=2)).then_inc(s["cat_conv"], 1)
            rsqrt_act(act, link, N_QK, numbers(N_QK, 1), numbers(N_QK, 2))
            act.wait_ge(s["nT_shown"], 1)
            nc.scalar.mul(qnT, bank(2).rearrange("p (a n) -> p a n", a=2), vecT[:, 0, R_QN:R_QN + 1])
            nc.scalar.mul(knT, bank(3).rearrange("p (a n) -> p a n", a=2), vecT[:, 0, R_KN:R_KN + 1])
            nc.scalar.copy(kcT, bank(6, 0, 256).rearrange("p (a n) -> p a n", a=2)).then_inc(s["nT_ready"], 1)
            for st in range(STREAMS):
                act.wait_ge(s["max_ready"], st + 1)
                pr = (p0, p1)[st]
                w = (P, 2 * P)[st]
                for e in range(2):
                    for a in range(PAIRS):
                        i = 2 * e + a
                        last = nc.scalar.activation(pr[:, i, :], bank((2, 6)[st] + e, w * a, w * (a + 1)), ACT.Exp,
                                                    bias=mx[:, 4 * st + i:4 * st + i + 1],
                                                    accum_out=p_sum[:, 4 * st + i:4 * st + i + 1])
                last.then_inc(s["p_exp"], 1)
            act.wait_ge(s["pT_shown"], 1)
            nc.scalar.copy(pT, ps[:, 0:3, :].rearrange("p b (i n) -> p (b i) n", n=P)).then_inc(s["pT_ready"], 1)
            act.wait_ge(s["pv_shown"], 1)
            nc.scalar.copy(cat[:, 6:8, :], bank(3).rearrange("p (a n) -> p a n", a=2)).then_inc(s["cat_na"], 1)
            nc.scalar.activation(tm[:].rearrange("p l n -> p (l n)"), gg[:].rearrange("p s n -> p (s n)"),
                                 ACT.Sigmoid).then_inc(s["gg_sig"], 1)
            for g in range(8):
                act.wait_ge(s["decay_shown"], g + 1)
                if g == 1:
                    act.wait_ge(s["kco_ready"], 1)
                if g >= 2:
                    act.wait_ge(s["X_ready"], g - 1)
                nc.scalar.activation(E[:, g % 2, :, :], two(0).rearrange("p (l n) -> p l n", n=P), ACT.Exp)\
                  .then_inc(s["E_ready"], 1)
            act.wait_ge(s["st_pre"], 1)
            nc.scalar.activation(kd.rearrange("p a n -> p (a n)"), bank(3), ACT.Exp).then_inc(s["st_exp"], 1)
            act.wait_ge(s["st_shown"], 1)
            act.wait_ge(s["X_ready"], 8)
            nc.scalar.copy(hflat[0:DK, 0:1024], ps[0:DK, 6:8, :].rearrange("p b n -> p (b n)")).then_inc(s["st_kept"], 1)
            for st in range(STREAMS):
                rsqrt_act(act, link, N_GLA + st, numbers(N_GLA + st, 1), numbers(N_GLA + st, 2))
            for st in range(STREAMS):
                act.wait_ge(s["goT_shown"], st + 1)
                nc.scalar.mul(cat[:, 0:4, P * st:P * (st + 1)], bank(st).rearrange("p (k n) -> p k n", n=P),
                              vecT[:, 0, R_ON:R_ON + 1]).then_inc(s["cat_gla"], 1)
            act.wait_ge(s["x_mid"], 4)
            act.wait_ge(s["stored"], layer * (16 * STORES) + 16 * STORES)
            squares(N_FFN)
            rsqrt_act(act, link, N_FFN, numbers(N_FFN, 1), numbers(N_FFN, 2))
            keep_hT(1)
            for st in range(STREAMS):
                by_tile = h[:, st, :].rearrange("t (n k) -> t k n", k=KT)
                if st == 0:
                    act.wait_ge(s["logits_shown"], STREAMS)
                nc.scalar.copy(hs[:, 0, st], by_tile).then_inc(s["hs1"], 1)
                nc.scalar.activation(scores[:, st, :], bank(2 + 4 * st, 0, EXPERTS), ACT.Sigmoid)\
                  .then_inc(s["scored"], 1)
            act.wait_ge(s["g2_shown"], 1)
            for st in range(STREAMS):
                last = nc.scalar.copy(g2[:, st, :], two(4 * st))
            last.then_inc(s["g2_kept"], 1)

            for part, left, done in ((1, "rest1", "hs2"), (2, "rest2", "hs3")):
                for st in range(STREAMS):
                    act.wait_ge(s[left], st + 1)
                    nc.scalar.copy(hs[:, part, st], h[:, st, :].rearrange("t (n k) -> t k n", k=KT))\
                      .then_inc(s[done], 1)
            for st in range(STREAMS):
                if st == 1:
                    act.wait_ge(s["tables_shown"], 1)
                    nc.scalar.copy(tables, ps[0:EXPERTS, 6, :].rearrange("p (a n) -> p a n", a=4))\
                      .then_inc(s["tables_kept"], 1)
                act.wait_ge(s["sh_gu"], st + 1)
                nc.scalar.activation(silu[:, st, :], bank(4 + st, 0, FF), ACT.Silu).then_inc(s["sh_silu"], 1)

            def keep_X(b, half):
                return nc.scalar.copy(X_e[:, b, KT // 2 * half:KT // 2 * (half + 1), :],
                                      bank(6).rearrange("p (k n) -> p k n", n=P))

            act.wait_ge(s["X_shown"], 1)
            keep_X(0, 0).then_inc(s["X_kept"], 1)
            for st in range(STREAMS):
                act.wait_ge(s["sh_turned"], st + 1)
                nc.scalar.copy(sh_actT[:, st, :], bank(4 + st, 0, FF)).then_inc(s["sh_kept"], 1)
            act.wait_ge(s["X_shown"], 2)
            keep_X(0, 1).then_inc(s["X_kept"], 1)
            act.wait_ge(s["moe_zero"], 2)
            with act.Fori(0, EPAIRS // TURN) as i:
                for q in range(TURN):
                    act.wait_ge(s["gu_done"], i * TURN + q + 1)
                    act.wait_ge(s["sh_act"], STREAMS)
                    nc.scalar.activation(silu[:, 0, :], bank(4, 0, FF), ACT.Silu).then_inc(s["silu_done"], 1)
                    act.wait_ge(s["turned"], i * TURN + q + 1)
                    nc.scalar.copy(turn, bank(5)).then_inc(s["turn_kept"], 1)
                    for half in range(2):
                        act.wait_ge(s["X_shown"], i * (2 * TURN) + 2 * q + 3 + half)
                        keep_X(1 - q, half).then_inc(s["X_kept"], 1)
                    tokens = act.value_load(most_i[0:1, bass.ds(i * TURN + q, 1)], min_val=0, max_val=SKEW * STREAMS * P)
                    with act.If(tokens > CAP[0]):
                        with act.Fori(1, PASSES) as r:
                            m = (i * TURN + q) * (PASSES - 1) + r
                            with act.If(tokens > r * CAP[0]):
                                for half in range(2):
                                    act.wait_ge(s["over_Xs"], m * 2 - 1 + half)
                                    keep_X(q, half).then_inc(s["over_Xk"], 1)
                                act.wait_ge(s["over_gu"], m)
                                nc.scalar.activation(silu[:, 1, :], bank(4, 0, FF), ACT.Silu)\
                                  .then_inc(s["over_silu"], 1)
                                act.wait_ge(s["over_turned"], m)
                                nc.scalar.copy(turn_over, bank(5)).then_inc(s["over_kept"], 1)
                                act.wait_ge(s["over_done"], m)
                                act.sem_inc(s["over_left"], 1)
                            with act.Else():
                                for name, k in (("over_Xk", 2), ("over_silu", 1), ("over_kept", 1)):
                                    act.sem_inc(s[name], k)
                    with act.Else():
                        for name, k in (("over_Xk", 2), ("over_silu", 1), ("over_kept", 1)):
                            act.sem_inc(s[name], k * (PASSES - 1))

        @block.vector
        def _(dve):
            count = [0]

            def link(ins):
                count[0] += 1
                ins.then_inc(s["dve_step"], 1)
                dve.wait_ge(s["dve_step"], count[0])

            tt, ts, stt = nc.vector.tensor_tensor, nc.vector.tensor_scalar, nc.vector.scalar_tensor_tensor

            def two(b):
                return ps[:, b:b + 2, :].rearrange("p b n -> p (b n)")

            tmflat = tm[:].rearrange("p l n -> p (l n)")

            def modulate(k, norm):
                dve.wait_ge(s["square_done"], k + 1)
                rsqrt_dve(dve, link, norm, *[numbers(norm, j) for j in range(5)], 1.0 / D)
                dve.wait_ge(s["norm_in"], 16 * (k + 1))
                for st in range(STREAMS):
                    dve.wait_ge(s["mod_shown"], STREAMS * k + st + 1)
                    link(stt(out=tmflat, in0=two(4 * st), scalar=1.0, in1=gbc[:], op0=ALU.add, op1=ALU.mult))
                    link(stt(out=h[:, st, :], in0=x[:, st, :], scalar=numbers(norm, 4)[:, st:st + 1], in1=tmflat,
                             op0=ALU.mult, op1=ALU.mult))
                    tt(h[:, st, :], h[:, st, :], two(4 * st + 2), ALU.add).then_inc(s["h_ready"], 1)

            modulate(0, N_IN)
            for st in range(STREAMS):
                dve.wait_ge(s["la_log"], st + 1)
                z = la[:, st, :, :].rearrange("p a n -> p (a n)")
                link(stt(out=z, in0=bank(st), scalar=0.0, in1=z, op0=ALU.min, op1=ALU.subtract))
                ts(z, z, 1.0 / 16.0, None, ALU.mult).then_inc(s["la_ready"], 1)
            dve.wait_ge(s["conv_sig"], 1)
            for c in range(2):
                link(tt(hpad[:, c, :, HALO:HALO + P], ci[:, c, :].rearrange("p (s t) -> p s t", s=2),
                        csig[:, c, :].rearrange("p (s t) -> p s t", s=2), ALU.mult))
            dve.wait_ge(s["vec_ready"], 1)
            for t in range(TAPS):
                for c in range(2):
                    k = 2 * t + c
                    shifted = hpad[:, c, :, t:t + P]
                    wt = vecT[:, c, R_DW + t:R_DW + t + 1]
                    if t == 0:
                        ins = ts(cacc[:, c, :, :], shifted, wt, vecT[:, c, R_DWB:R_DWB + 1], ALU.mult, ALU.add)
                    else:
                        dve.wait_ge(s["tap"], k - 1)
                        ins = stt(out=cacc[:, c, :, :], in0=shifted, scalar=wt, in1=cacc[:, c, :, :],
                                  op0=ALU.mult, op1=ALU.add)
                    ins.then_inc(s["tap"], 1)
            dve.wait_ge(s["tap"], 2 * TAPS)
            nc.vector.memset(sm[:, 176:177], 0.0).then_inc(s["conv_ready"], 1)
            dve.wait_ge(s["convT_shown"], 1)
            tok = bank(4).rearrange("p (s n) -> p s n", s=2)
            link(nc.vector.tensor_reduce(conv_mean, tok, AX.X, ALU.add))
            link(ts(conv_mean, conv_mean, -1.0 / CONV_CH, None, ALU.mult))
            for st in range(STREAMS):
                link(ts(cTok[:, st, :], tok[:, st, :], conv_mean[:, st:st + 1], None, ALU.add))
            link(tt(cSq, cTok, cTok, ALU.mult))
            link(nc.vector.tensor_reduce(numbers(N_CONV, 0), cSq, AX.X, ALU.add))
            rsqrt_dve(dve, link, N_CONV, *[numbers(N_CONV, j) for j in range(5)], 1.0 / CONV_CH)
            for st in range(STREAMS):
                last = ts(cTok[:, st, :], cTok[:, st, :], numbers(N_CONV, 4)[:, st:st + 1], None, ALU.mult)
            last.then_inc(s["ctok_ready"], 1)
            dve.wait_ge(s["conv_sig"], 2)
            y = cacc[:].rearrange("p c s t -> p c (s t)")
            tt(y, y, csig, ALU.mult).then_inc(s["cact_ready"], 1)
            dve.wait_ge(s["proj_kept"], LAST_UNIT[3] + 1)
            dve.wait_ge(s["hT_ready"], STREAMS)
            link(tt(sq, nax[:, :, 0:512], nax[:, :, 0:512], ALU.mult))
            link(nc.vector.tensor_reduce(numbers(N_QK, 0), sq.rearrange("p s (g d) -> p (s g) d", d=DK), AX.X, ALU.add))
            rsqrt_dve(dve, link, N_QK, *[numbers(N_QK, j) for j in range(5)], 1.0 / DK)
            r = numbers(N_QK, 4)
            link(ts(r.rearrange("p (s g) -> p s g", s=2)[:, :, 0:HEADS], r.rearrange("p (s g) -> p s g", s=2)[:, :, 0:HEADS],
                    float(DK) ** -0.5, None, ALU.mult))
            for st in range(STREAMS):
                last = tt(nq[:, st, :].rearrange("p (g d) -> p g d", d=DK),
                          nax[:, st, 0:512].rearrange("p (g d) -> p g d", d=DK),
                          r[:, 8 * st:8 * (st + 1)].unsqueeze(2).broadcast_to([P, 8, DK]), ALU.mult)
            last.then_inc(s["nq_ready"], 1)
            for st in range(STREAMS):
                dve.wait_ge(s["scores_shown"], st + 1)
                sc = ps[:, 2:4, 0:256] if st == 0 else ps[:, 6:8, :]
                link(nc.vector.tensor_reduce(mx[:, 4 * st:4 * st + 4].rearrange("p (e a) -> p e a", e=2),
                                             sc.rearrange("p e (a k) -> p e a k", a=2), AX.X, ALU.max))
                ts(mx[:, 4 * st:4 * st + 4], mx[:, 4 * st:4 * st + 4], -1.0, None, ALU.mult).then_inc(s["max_ready"], 1)
            dve.wait_ge(s["p_exp"], STREAMS)
            link(nc.vector.reciprocal(p_inv, p_sum))
            tt(p0, p0, p_inv[:, 0:4].unsqueeze(2).broadcast_to([P, 4, P]), ALU.mult)
            tt(p1, p1, p_inv[:, 4:8].unsqueeze(2).broadcast_to([P, 4, 2 * P]), ALU.mult).then_inc(s["p_ready"], 1)
            dve.wait_ge(s["gg_sig"], 1)
            ggf = gg[:].rearrange("p s n -> p (s n)")
            link(tt(ggf, ggf, tmflat, ALU.mult))

            def decayed(g):
                st, a, dr = g // 4, g // 2 % 2, g % 2
                dve.wait_ge(s["E_ready"], g + 1)
                if g >= 2:
                    dve.wait_ge(s["pair_shown"], 2 * (g - 1))
                q_, k_ = (t[:, a, P * st:P * (st + 1)] for t in (qT, kT))
                for lv in range(LEVELS):
                    w = P >> (lv + 1)
                    for part, src in ((0, (k_, q_)[dr]), (1, (q_, k_)[dr])):
                        views = [t.rearrange("p (b a r) -> p b a r", a=2, r=w)[:, :, part, :]
                                 for t in (X[:, dr, lv, :], E[:, dr, lv, :], src)]
                        last = tt(*views, ALU.mult)
                if st == 1:
                    last = tt(qd[:, a, dr, :], E[:, dr, LEVELS, :], q_, ALU.mult)
                last.then_inc(s["X_ready"], 1)

            def combine(g):
                st, a, dr = g // 4, g // 2 % 2, g % 2
                n = LEVELS + (dr == 0)
                for e in range(2):
                    dve.wait_ge(s["pair_shown"], 2 * g + e + 1)
                    if st == 1 and dr == 0:
                        dve.wait_ge(s["o_shown"], 2 * a + e + 1)
                    b = (2, 6)[e]
                    tt(tm[:, 0:n, :], two(b).rearrange("p (l n) -> p l n", n=P)[:, 0:n, :],
                       (maskf, maskb)[dr][:, 0:n, :], ALU.mult).then_inc(s["masked"], 1)
                    dve.wait_ge(s["masked"], 2 * g + e + 1)
                    levels = tm[:, 0:n, :].rearrange("p l n -> p n l")
                    if dr == 0:
                        link(nc.vector.tensor_reduce(att[:, a, e, :], levels, AX.X, ALU.add))
                    else:
                        link(nc.vector.tensor_reduce(att2[:, 0:P], levels, AX.X, ALU.add))
                        tt(att[:, a, e, :], att[:, a, e, :], att2[:, 0:P], ALU.add).then_inc(s["att_ready"], 1)
                        dve.wait_ge(s["att_ready"], 2 * (g // 2) + e + 1)

            dve.wait_ge(s["pv_shown"], 1)
            decayed(0)
            for g in range(8):
                if g + 1 < 8:
                    decayed(g + 1)
                combine(g)
            dve.wait_ge(s["st_exp"], 1)
            for dr in range(2):
                last = tt(kd[:, dr, :], kd[:, dr, :], bank(2, 0, 256), ALU.mult)
            last.then_inc(s["kd_ready"], 1)
            for st in range(STREAMS):
                dve.wait_ge(s["o_shown"], 4 * (st + 1))
                o = bank(4 + st).rearrange("p (h n) -> p h n", n=DV)
                t4 = tm[:, 4 * st:4 * (st + 1), :]
                o_copy = hflat[:, 1024 + 512 * st:1536 + 512 * st].rearrange("p (h n) -> p h n", n=DV)
                link(nc.vector.tensor_copy(o_copy, o))
                link(tt(t4, o_copy, o_copy, ALU.mult))
                link(nc.vector.tensor_reduce(numbers(N_GLA + st, 0), t4, AX.X, ALU.add))
                rsqrt_dve(dve, link, N_GLA + st, *[numbers(N_GLA + st, j) for j in range(5)], 1.0 / DV)
                link(tt(t4, o_copy, numbers(N_GLA + st, 4).unsqueeze(2).broadcast_to([P, HEADS, DV]), ALU.mult))
                g4 = gg[:, st, :].rearrange("p (h n) -> p h n", n=DV)
                tt(g4, g4, t4, ALU.mult).then_inc(s["go_ready"], 1)
            dve.wait_ge(s["go_ready"], STREAMS)
            for half in range(2):
                for st in range(STREAMS):
                    u = 2 * half + st
                    dve.wait_ge(s["mix_shown"], u + 1)
                    t = tmflat[:, 512 * (u % 2):512 * (u % 2 + 1)]
                    nc.vector.tensor_copy(t, bank((4, 5, 0, 1)[u])).then_inc(s["dve_step"], 1)
                    count[0] += 1
                    dve.wait_ge(s["dve_step"], count[0])
                    link(tt(t, t, bank(PROJ_BANKS[u]), ALU.mult))
                    xs = x[:, st, 512 * half:512 * (half + 1)]
                    tt(xs, xs, t, ALU.add).then_inc(s["x_mid"], 1)
            dve.wait_ge(s["x_mid"], 4)
            modulate(1, N_FFN)
            dve.wait_ge(s["scored"], STREAMS)
            for st in range(STREAMS):
                last = tt(biased[:, st, :], scores[:, st, :], rbias[:], ALU.add)
            link(last)
            for st in range(STREAMS):
                for g in range(GROUPS):
                    last = nc.vector.max(top[:, st, g, :], biased[:, st, PER_GROUP * g:PER_GROUP * (g + 1)])
            link(last)
            link(tt(grp, top[:, :, :, 0], top[:, :, :, 1], ALU.add))
            for st in range(STREAMS):
                other = grp[:, st, :].unsqueeze(1).broadcast_to([P, GROUPS, GROUPS])
                own = grp[:, st, :].unsqueeze(2).broadcast_to([P, GROUPS, GROUPS])
                link(tt(beats[:, 0], other, own, ALU.is_equal))
                link(tt(beats[:, 0], beats[:, 0], tri8[:], ALU.mult))
                link(tt(beats[:, 1], other, own, ALU.is_gt))
                link(tt(beats[:, 0], beats[:, 0], beats[:, 1], ALU.add))
                link(nc.vector.tensor_reduce(rank, beats[:, 0], AX.X, ALU.add))
                link(ts(rank, rank, TOP_GROUPS - 0.5, NEVER, ALU.is_gt, ALU.mult))
                bs = biased[:, st, :].rearrange("p (g n) -> p g n", n=PER_GROUP)
                link(tt(bs, bs, rank.unsqueeze(2).broadcast_to([P, GROUPS, PER_GROUP]), ALU.add))
                link(nc.vector.max(best, biased[:, st, :]))
                link(nc.vector.match_replace(out=chosen[:, st, :], in_to_replace=best, in_values=biased[:, st, :],
                                             imm_value=3 * NEVER))
                link(ts(sel[:, st, :], chosen[:, st, :], 2 * NEVER, None, ALU.is_lt))
                link(tt(chosen[:, st, :], sel[:, st, :], scores[:, st, :], ALU.mult))
                link(nc.vector.tensor_reduce(tot, chosen[:, st, :], AX.X, ALU.add))
                link(nc.vector.reciprocal(tot, tot))
                link(ts(gate[:, st, 0:EXPERTS], chosen[:, st, :], tot, ROUTED_SCALE, ALU.mult, ALU.mult))

            nc.vector.memset(place[:, :, EXPERTS:], -1.0).then_inc(s["chosen_ready"], 1)
            dve.wait_ge(s["counted"], 1)
            for st in range(STREAMS):
                link(stt(out=place[:, st, 0:EXPERTS], in0=bank(2, 64 * st, 64 * (st + 1)), scalar=1.0,
                         in1=sel[:, st, :], op0=ALU.add, op1=ALU.mult))
                link(ts(place[:, st, 0:EXPERTS], place[:, st, 0:EXPERTS], -1.0, None, ALU.add))
            link(nc.vector.tensor_copy(own_load, ps[0:EXPERTS, 2, 192:192 + EXPERTS]))
            link(stt(out=own_key, in0=own_load, scalar=-float(EXPERTS), in1=expert_no[0:EXPERTS, :], op0=ALU.mult,
                     op1=ALU.add))
            link(ts(keys, ps[0:EXPERTS, 2, 128:128 + EXPERTS], -float(EXPERTS), None, ALU.mult))
            link(tt(keys, keys, wanted[0:EXPERTS, 0, 0:EXPERTS], ALU.add))
            link(tt(keys, own_key, keys, ALU.is_gt))
            link(nc.vector.tensor_reduce(load_rank, keys, AX.X, ALU.add))
            ts(order, rank_at[0:EXPERTS, :], load_rank, None, ALU.is_equal).then_inc(s["ordered"], 1)
            dve.wait_ge(s["sorted_shown"], 1)
            nc.vector.tensor_copy(order_i, ps[0:EXPERTS, 7, 256:256 + EXPERTS]).then_inc(s["order_ready"], 1)
            link(nc.vector.tensor_copy(load, ps[0:EXPERTS, 7, 320:320 + EXPERTS]))
            link(stt(out=most, in0=load[:, 1::2], scalar=float(SKEW), in1=load[:, 0::2], op0=ALU.mult, op1=ALU.max))
            nc.vector.tensor_copy(most_i, most)
            nc.vector.tensor_copy(place[:, :, 0:EXPERTS], bank(7, 0, 128).rearrange("p (s e) -> p s e", s=STREAMS))
            nc.vector.tensor_copy(gate[:, :, 0:EXPERTS], bank(7, 128, 256).rearrange("p (s e) -> p s e", s=STREAMS))\
              .then_inc(s["places"], 1)

            def onehot(out, pair, places):
                for c, (first, cap) in enumerate(zip(FIRST, CAP)):
                    last = tt(out[:, :, first:first + cap],
                              places[:, first:first + cap].unsqueeze(1).broadcast_to([P, STREAMS, cap]),
                              place[:, :, bass.ds(pair * 2 + c, 1)].broadcast_to([P, STREAMS, cap]), ALU.is_equal)
                return last

            def weigh(out, places, pair):
                for c, (first, cap) in enumerate(zip(FIRST, CAP)):
                    last = tt(out[:, :, first:first + cap], places[:, :, first:first + cap],
                              gate[:, :, bass.ds(pair * 2 + c, 1)].broadcast_to([P, STREAMS, cap]), ALU.mult)
                return last

            dve.wait_ge(s["places"], 1)
            onehot(G[0], 0, wanted[:, 0, :]).then_inc(s["G_ready"], 1)
            onehot(G[1], 1, wanted[:, 0, :]).then_inc(s["G_ready"], 1)
            dve.wait_ge(s["G_ready"], 1)
            weigh(S[0], G[0], 0).then_inc(s["S_ready"], 1)
            for st in range(STREAMS):
                dve.wait_ge(s["sh_silu"], st + 1)
                tt(acts[:, st, :], silu[:, st, :], bank(4 + st, FF, 2 * FF), ALU.mult).then_inc(s["sh_act"], 1)
            dve.wait_ge(s["sh_gu"], STREAMS)
            nc.vector.memset(Y[:, 0:512], 0.0).then_inc(s["Y_kept"], 1)
            nc.vector.memset(Y[:, 512:1024], 0.0).then_inc(s["Y_kept"], 1)
            dve.wait_ge(s["sh_done"], STREAMS)
            nc.vector.memset(turn, 0.0).then_inc(s["moe_zero"], 1)
            nc.vector.memset(turn_over, 0.0).then_inc(s["moe_zero"], 1)
            dve.wait_ge(s["sh_turned"], STREAMS)
            with dve.Fori(0, EPAIRS // TURN) as i:
                for q in range(TURN):
                    pair = i * TURN + q
                    dve.wait_ge(s["silu_done"], i * TURN + q + 1)
                    tt(acts[:, 0, :], silu[:, 0, :], bank(4, FF, 2 * FF), ALU.mult).then_inc(s["act_done"], 1)
                    dve.wait_ge(s["Y_shown"], i * (2 * TURN) + 2 * q + 1)
                    nc.vector.tensor_copy(Y[:, 0:512], bank(7)).then_inc(s["Y_kept"], 1)
                    dve.wait_ge(s["G_ready"], i * TURN + q + 2)
                    weigh(S[0], G[1 - q], pair + 1).then_inc(s["S_ready"], 1)
                    dve.wait_ge(s["S_ready"], i * TURN + q + 1)
                    onehot(G[q], pair + 2, wanted[:, 0, :]).then_inc(s["G_ready"], 1)
                    dve.wait_ge(s["Y_shown"], i * (2 * TURN) + 2 * q + 2)
                    nc.vector.tensor_copy(Y[:, 512:1024], bank(7)).then_inc(s["Y_kept"], 1)
                    tokens = dve.value_load(most_i[0:1, bass.ds(i * TURN + q, 1)], min_val=0, max_val=SKEW * STREAMS * P)
                    with dve.If(tokens > CAP[0]):
                        nc.vector.tensor_copy(want[:], wanted[:, 0, :]).then_inc(s["over_want"], 1)
                        with dve.Fori(1, PASSES) as r:
                            m = (i * TURN + q) * (PASSES - 1) + r
                            with dve.If(tokens > r * CAP[0]):
                                steps = pair * PASSES + r
                                dve.wait_ge(s["over_want"], steps)
                                tt(want[:], want[:], wanted[:, 1, :], ALU.add).then_inc(s["over_want"], 1)
                                dve.wait_ge(s["over_want"], steps + 1)
                                onehot(G[2], pair, want).then_inc(s["over_G"], 1)
                                dve.wait_ge(s["over_G"], m)
                                weigh(S[1], G[2], pair).then_inc(s["over_GS"], 1)
                                dve.wait_ge(s["over_silu"], m)
                                tt(acts[:, 1, :], silu[:, 1, :], bank(4, FF, 2 * FF), ALU.mult)\
                                  .then_inc(s["over_act"], 1)
                                for half in range(2):
                                    dve.wait_ge(s["over_Ys"], m * 2 - 1 + half)
                                    nc.vector.tensor_copy(Y_over[:, 512 * half:512 * (half + 1)], bank(7))\
                                      .then_inc(s["over_Yk"], 1)
                                dve.wait_ge(s["over_done"], m)
                                dve.sem_inc(s["over_left"], 1)
                            with dve.Else():
                                for name, k in (("over_want", 1), ("over_G", 1), ("over_GS", 1), ("over_act", 1),
                                                ("over_Yk", 2)):
                                    dve.sem_inc(s[name], k)
                    with dve.Else():
                        dve.sem_inc(s["over_want"], PASSES)
                        for name, k in (("over_G", 1), ("over_GS", 1), ("over_act", 1), ("over_Yk", 2)):
                            dve.sem_inc(s[name], k * (PASSES - 1))
            dve.wait_ge(s["scattered"], EPAIRS + 1)
            for st in range(STREAMS):
                link(tt(tmflat, two(2 * st), g2[:, st, :], ALU.mult))
                link(tt(x[:, st, :], x[:, st, :], tmflat, ALU.add))

        @block.gpsimd
        def _(pool):
            pool.wait_ge(s["attn_in"], 16 * N_ATTN)
            nc.gpsimd.tensor_tensor(biasr, biasr, maskr[:].unsqueeze(1).broadcast_to([P, HEADS, P]), ALU.add)\
              .then_inc(s["bias_ready"], 1)
            pool.wait_ge(s["small_in"], 16 * N_SMALL)
            pool.wait_ge(s["nq_ready"], 1)
            nc.gpsimd.tensor_tensor(kco.rearrange("p (h d) -> p h d", h=HEADS),
                                    nq[:, 0, 256:512].rearrange("p (h d) -> p h d", h=HEADS),
                                    gk[:].unsqueeze(1).broadcast_to([P, HEADS, DK]), ALU.mult).then_inc(s["kco_ready"], 1)
            pool.wait_ge(s["kco_ready"], 1)
            dma_in(pool, A["new_cache_na_k"][0, layer].rearrange("h t d -> t h d"),
                   kco.rearrange("p (h d) -> p h d", h=HEADS), s["stored"])
            dma_in(pool, A["new_cache_na_v"][0, layer].rearrange("h t d -> t h d"),
                   nax[:, 0, 512:768].rearrange("p (h d) -> p h d", h=HEADS), s["stored"])
            pool.wait_ge(s["st_kept"], 1)
            for dr in range(2):
                dma_in(pool, A["new_state_gla"][0, layer, dr].rearrange("h d v -> d h v"),
                       hflat[0:DK, 512 * dr:512 * (dr + 1)].rearrange("p (h v) -> p h v", h=HEADS), s["stored"])
            pool.wait_ge(s["stored"], layer * (16 * STORES) + 16 * STORES)
            pool.wait_ge(s["hT_shown"], 2 * STREAMS)
            for part, kept, left in ((0, "hs1", "rest1"), (1, "hs2", "rest2")):
                for st in range(STREAMS):
                    pool.wait_ge(s[kept], st + 1)
                    nc.gpsimd.tensor_tensor(h[:, st, :].rearrange("t (n k) -> t k n", k=KT),
                                            h[:, st, :].rearrange("t (n k) -> t k n", k=KT), hs[:, part, st],
                                            ALU.subtract).then_inc(s[left], 1)

    with nc.Block() as block:
        @block.gpsimd
        def _(pool):
            for name in SIGNALS:
                if name not in ("stored", "const_step", "x_loaded", "c_sig", "c_step", "y_out"):
                    pool.sem_clear(s[name])
    layers.__exit__(None, None, None)

    with nc.Block() as block:
        @block.sync
        def _(sp):
            sp.dma_start(A["y_prompt"][0], x[:, 0, :]).then_inc(s["y_out"], 16)
            sp.dma_start(A["y_sample"][0], x[:, 1, :]).then_inc(s["y_out"], 16)
            sp.wait_ge(s["y_out"], 32)


_INS = ["x_prompt", "x_sample", "state_gla", "cache_na_k", "cache_na_v", "c", "c_ctx", "w_ada", "b_ada", "norm_mix",
        "norm_ffn", "w_in", "gla_w_gate", "gla_b_gate", "gla_out_norm", "conv_dw", "conv_dw_b", "conv_ln_g",
        "conv_ln_b", "conv_pw", "na_q_norm", "na_k_norm", "na_rpb", "w_out", "router_w", "router_bias", "exp_w_gate",
        "exp_w_up", "exp_w_down", "sh_w_gate", "sh_w_up", "sh_w_down"]
_OUTS = [("y_prompt", (1, 128, 1024)), ("y_sample", (1, 128, 1024)), ("new_state_gla", (1, 2, 2, 4, 64, 128)),
         ("new_cache_na_k", (1, 2, 4, 128, 64)), ("new_cache_na_v", (1, 2, 4, 128, 64))]


def kernel(**inputs):
    import numpy as _np
    import concourse.bacc as _bacc
    from concourse.bass_utils import run_bass_kernel_spmd as _run

    nc = _bacc.Bacc("TRN2", target_bir_lowering=False, num_devices=1)
    arrays, tensors = {}, {}
    for name in _INS:
        a = _np.ascontiguousarray(inputs[name])
        arrays[f"in_{name}"] = a
        tensors[name] = nc.dram_tensor(f"in_{name}", a.shape, F32, kind="ExternalInput").ap()
    for name, shape in _OUTS:
        tensors[name] = nc.dram_tensor(f"out_{name}", shape, F32, kind="ExternalOutput").ap()
    build(nc, tensors)
    r = _run(nc, [arrays], core_ids=[0])
    return tuple(r.results[0][f"out_{name}"] for name, _ in _OUTS)
```

```python
import concourse.bass as bass
from concourse import mybir

F32 = mybir.dt.float32
BF16 = mybir.dt.bfloat16
ALU = mybir.AluOpType
ACT = mybir.ActivationFunctionType
AX = mybir.AxisListType

P = 128
D = 1024
KT = D // P
DEPTH = 2
STREAMS = 2
HEADS = 4
DK = 64
DV = 128
PAIRS = HEADS // 2
RANK = 16
CONV_CH = 256
TAPS = 31
HALO = TAPS // 2
GRID_W = 64
WIN_ROWS = 8
WIN_COLS = 16
RPB_COLS = 2 * WIN_COLS - 1
RPB_HEAD = (2 * WIN_ROWS - 1) * RPB_COLS
IN_WIDTH = 2848
EXPERTS = 64
GROUPS = 8
PER_GROUP = EXPERTS // GROUPS
TOP_K = 8
TOP_GROUPS = 4
FF = 256
ROUTED_SCALE = 2.5
EPS = 1e-6
LEVELS = 7
NEVER = -1e30

SLOTS = 4
SLOT = 3 * KT * FF
ADA_CHUNKS = 12
ADA_FIRST = 4
IN_CHUNKS = [(1536, 544), (0, 512), (512, 512), (2080, 768), (1024, 512)]
OUT_CHUNKS = 2
PRE_SLOTS = 3
C_ADA = len(IN_CHUNKS)
C_OUT = C_ADA + ADA_CHUNKS
C_SH = C_OUT + OUT_CHUNKS
PRE = C_SH + 1
ADA_LATER = ADA_CHUNKS - ADA_FIRST
ADA_EARLY = 5
ADA_GLA = 9

UNITS_IN = [(0, 0, 2 * RANK, True, None)] + [(0, 2 * RANK + P * j, P, True, None) for j in range(4)]
UNITS_IN += [(1, P * j, P, True, None) for j in range(4)]
UNITS_IN += [(2, 0, 512, False, st) for st in range(STREAMS)]
UNITS_IN += [(3, c0, w, False, st) for st in range(STREAMS) for c0, w in ((0, 512), (512, 256))]
UNITS_IN += [(4, 0, 512, False, st) for st in range(STREAMS)]
LAST_UNIT = [max(u for u, unit in enumerate(UNITS_IN) if unit[0] == c) for c in range(len(IN_CHUNKS))]
PROJ_BANKS = (2, 3, 6, 7)
STORES = 4
CAP = (96, 32)
FIRST = (0, CAP[0])
TILES = ((0, 64, 0), (64, 32, 0), (96, 32, 1))
SKEW = CAP[0] // CAP[1]
PASSES = STREAMS * P // CAP[1]
EPAIRS = EXPERTS // 2
TURN = SLOTS // 2

R_DW, R_DWB, R_LNG, R_LNB, R_ON, R_QN, R_KN, R_END = 0, 31, 32, 33, 34, 35, 36, 37


SIGNALS = """x_loaded c_loaded const_set const_step matrices c_sig c_step first_in0 first_in1
first_in2 first_in3 first_done first_kept first_bias bias_next small_in vec_in norm_in attn_in shared_in chunk_in0 chunk_in1 chunk_in2
expert_in0 expert_in1 expert_in2 expert_in3 act_step dve_step ada_done ada_kept bias_in square_done var_ready
root_ready mod_shown h_ready hT_shown hT_ready vec_shown vec_ready proj_done proj_kept z_shown la_log la_ready
conv_sig tap conv_ready convT_shown ctok_ready convB_shown conv_neg cact_ready pw_shown cat_conv nq_ready
kco_ready nT_shown nT_ready bias_ready scores_shown max_ready p_exp p_ready pT_shown pT_ready pv_shown cat_na
gg_sig decay_shown E_ready X_ready pair_shown masked att_ready o_shown go_ready goT_shown cat_gla st_pre
st_exp kd_ready st_shown st_kept mix_shown x_mid logits_shown scored g2_shown g2_kept stored y_out hs1 hs2 hs3 ordered tables_shown
tables_kept sorted_shown order_ready over_want
rest1 rest2 chosen_ready counted places sh_gu sh_silu sh_act sh_turned sh_kept sh_done G_ready
S_ready X_shown X_kept gu_done gu_free silu_done act_done turned turn_kept Y_shown Y_kept scattered over_G over_GS over_Xs
over_Xk over_gu over_silu over_act over_turned over_kept over_Ys over_Yk over_done over_left""".split()


def rpb_window(rpb, layer, head, half):
    flat = rpb.rearrange("l h r c -> l (h r c)")
    first = head * RPB_HEAD + (WIN_ROWS - 2 + half) * RPB_COLS + (WIN_COLS - 1) - (GRID_W - 1)
    row = flat[layer, first:first + 1]
    ap = [list(d) for d in row.ap]
    return bass.AP(row.tensor, row.offset, [[1, GRID_W], [RPB_COLS, 2], [1, GRID_W]])


def expert_slot(e):
    return (e + 2) % SLOTS


def build(nc, A):
    def sb(name, shape, dt=F32):
        return nc.alloc_sbuf_tensor(name, shape, dt)

    s = {name: nc.alloc_semaphore(name) for name in SIGNALS}

    ring = sb("ring", [P, SLOTS, SLOT])
    x = sb("x", [P, STREAMS, D])
    ada = sb("ada", [P, ADA_CHUNKS, P])
    h = sb("h", [P, STREAMS, D])
    gbc = sb("gbc", [P, D])
    hT = sb("hT", [P, KT, STREAMS * P])
    mid = sb("mid", [P, 5120])
    qT = mid[:, 0:512].rearrange("p (a n) -> p a n", a=PAIRS)
    kT = mid[:, 512:1024].rearrange("p (a n) -> p a n", a=PAIRS)
    v = mid[:, 1024:2048].rearrange("p (s n) -> p s n", s=STREAMS)
    gg = mid[:, 2048:3072].rearrange("p (s n) -> p s n", s=STREAMS)
    la = mid[:, 3072:4096].rearrange("p (s a n) -> p s a n", s=STREAMS, a=2)
    ci = mid[:, 4096:5120].rearrange("p (a n) -> p a n", a=4)
    lrT = sb("lrT", [33, STREAMS * P])
    nax = sb("nax", [P, STREAMS, 3 * HEADS * DK])
    cat = sb("cat", [P, KT, STREAMS * P])
    sm = sb("sm", [P, 256])
    ident = sb("ident", [P, P])
    flip = sb("flip", [P, P])
    pick = sb("pick", [P, 4, STREAMS, P])
    mf = sb("mf", [P, LEVELS + 1, P])
    mb = sb("mb", [P, LEVELS + 1, P])
    suf = sb("suf", [P, 2, P])
    maskf = sb("maskf", [P, LEVELS + 1, P], BF16)
    maskb = sb("maskb", [P, LEVELS, P], BF16)
    maskr = sb("maskr", [P, P])
    tri8 = sb("tri8", [P, GROUPS, GROUPS])
    zero = sb("zero", [P, P])
    cs = sb("cs", [P, KT, 32])
    craw = sb("craw", [P, 3, 2, KT])
    vec = sb("vec", [R_END, CONV_CH])
    vecT = sb("vecT", [P, 2, R_END])
    wg = sb("wg", [33, 2 * HEADS * DK])
    s0 = sb("s0", [P, 2, HEADS, DV])
    gk = sb("gk", [P, DK])
    wpw = sb("wpw", [P, 2, CONV_CH])
    wr = sb("wr", [P, KT, EXPERTS])
    rbias = sb("rbias", [P, EXPERTS])
    hpad = sb("hpad", [P, 2, STREAMS, P + 2 * HALO])
    gate = sb("gate", [P, STREAMS, EXPERTS + 4])
    ones = sb("ones", [P, P])
    wanted = sb("wanted", [P, 2, P])
    want = sb("want", [P, P])
    rank_at = sb("rank_at", [P, EXPERTS])
    expert_no = sb("expert_no", [P, EXPERTS])

    class Scratch:
        def __init__(self, base):
            self.base, self.at = base, 0

        def take(self, n):
            self.at += n
            return self.base[:, self.at - n:self.at]

    arena = Scratch(ring[:, 3, :])
    cacc = arena.take(512).rearrange("p (c s t) -> p c s t", c=2, s=2)
    csig = arena.take(512).rearrange("p (c n) -> p c n", c=2)
    biasr = arena.take(512).rearrange("p (h k) -> p h k", h=HEADS)
    kvc = arena.take(512).rearrange("p (a n) -> p a n", a=2)
    kcT = arena.take(256).rearrange("p (a n) -> p a n", a=PAIRS)
    qnT = arena.take(512).rearrange("p (a n) -> p a n", a=PAIRS)
    knT = arena.take(512).rearrange("p (a n) -> p a n", a=PAIRS)
    p0 = arena.take(512).rearrange("p (h k) -> p h k", h=HEADS)
    p1 = arena.take(1024).rearrange("p (h k) -> p h k", h=HEADS)
    kd = arena.take(512).rearrange("p (a n) -> p a n", a=2)
    kco = arena.take(HEADS * DK)
    att = p0.rearrange("p (b e) i -> p b e i", b=2)
    att2 = p1[:, 0, :]
    qd = p1[:, 2:4, :].rearrange("p b (r i) -> p b r i", r=2)
    assert arena.at <= SLOT
    sq = h[:, :, :].rearrange("p s n -> p (s n)")[:, 0:1024].rearrange("p (s n) -> p s n", s=2)
    nq = h[:, :, :].rearrange("p s n -> p (s n)")[:, 1024:2048].rearrange("p (s n) -> p s n", s=2)
    pT = hT[:, :, :].rearrange("p k n -> p (k n)")[:, 0:12 * P].rearrange("p (b n) -> p b n", n=P)
    E = h[:, :, :].rearrange("p s (l n) -> p s l n", n=P)
    X = hT[:, :, :].rearrange("p k n -> p (k n)").rearrange("p (b l n) -> p b l n", b=2, n=P)
    tm = sb("tm", [P, LEVELS + 1, P])
    hflat = h[:, :, :].rearrange("p s n -> p (s n)")
    cTok = tm[:, 0:4, :].rearrange("p (s a) n -> p s (a n)", s=2)
    cSq = tm[:, 4:8, :].rearrange("p (s a) n -> p s (a n)", s=2)
    g2 = cat[:, :, :].rearrange("p k n -> p (k n)").rearrange("p (s n) -> p s n", s=2)
    silu = qT[:, :, :]
    acts = kT[:, :, :]
    turn = v[:, 0, :]
    turn_over = v[:, 1, :]
    sh_actT = v[:, :, 0:FF]
    hs = mid[:, 2048:5120].bitcast(BF16).rearrange("p (c s k n) -> p c s k n", c=3, s=STREAMS, k=KT)
    X_e = h[:, :, :].rearrange("p s (k n) -> p s k n", k=KT)
    hTf = hT[:, :, :].rearrange("p k n -> p (k n)")
    Y, Y_over = hTf[:, 0:D], hTf[:, D:2 * D]
    tmf = tm[:].rearrange("p l n -> p (l n)")
    G = [tmf[:, 128 * b:128 * (b + 1)].bitcast(BF16).rearrange("p (s n) -> p s n", s=STREAMS)
         for b in range(3)]
    S = [tmf[:, 384 + 256 * b:384 + 256 * (b + 1)].rearrange("p (s n) -> p s n", s=STREAMS)
         for b in range(2)]
    tables = tmf[0:EXPERTS, 0:4 * P].rearrange("p (a n) -> p a n", a=4)
    naf = nax[:].rearrange("p s n -> p (s n)")
    scores = naf[:, 0:128].rearrange("p (s n) -> p s n", s=2)
    biased = naf[:, 128:256].rearrange("p (s n) -> p s n", s=2)
    chosen = naf[:, 256:384].rearrange("p (s n) -> p s n", s=2)
    top = naf[:, 384:512].rearrange("p (s g n) -> p s g n", s=2, n=8)
    ties = naf[:, 1092:1220].rearrange("p (s g n) -> p s g n", s=2, n=8)
    beats = naf[:, 1220:1348].rearrange("p (s g n) -> p s g n", s=2, n=8)
    grp = naf[:, 640:656].rearrange("p (s g) -> p s g", s=2)
    place = naf[:, 700:836].rearrange("p (s e) -> p s e", s=2)
    load = naf[0:EXPERTS, 836:900]
    most = naf[0:EXPERTS, 900:932]
    most_i = naf[0:EXPERTS, 932:964].bitcast(mybir.dt.int32)
    own_load = naf[0:EXPERTS, 1092:1156]
    own_key = naf[0:EXPERTS, 1156:1220]
    keys = naf[0:EXPERTS, 1220:1284]
    order = naf[0:EXPERTS, 1284:1348]
    order_i = naf[0:EXPERTS, 1348:1412].bitcast(mybir.dt.int32)
    load_rank = naf[0:EXPERTS, 1412:1413]
    sel = naf[:, 964:1092].rearrange("p (s e) -> p s e", s=2)
    rank, best = (naf[:, at:at + 16].rearrange("p (s n) -> p s n", s=2) for at in (656, 672))
    tot = naf[:, 688:690]
    ps = nc.alloc_psum_tensor("ps", [P, 8, 512], F32)

    def bank(b, lo=0, hi=512):
        return ps[:, b, lo:hi]

    const_steps = [0]

    def step(ins):
        const_steps[0] += 1
        ins.then_inc(s["const_step"], 1)

    def steps_done(eng):
        eng.wait_ge(s["const_step"], const_steps[0])

    def keep(view, cond, fill, base, pattern, mult):
        step(nc.gpsimd.affine_select(out=view, in_=view, compare_op=cond, fill=fill, base=base,
                                     pattern=pattern, channel_multiplier=mult))

    def number(view, pattern, base=0, mult=0):
        step(nc.gpsimd.iota(view, pattern, base=base, channel_multiplier=mult,
                            allow_small_or_imprecise_dtypes=True))

    def halves(lv):
        w = P >> (lv + 1)
        return ([t[:, lv, :].rearrange("p (b a r) -> p b a r", a=2, r=w)[:, :, a, :]
                 for t in (mf, mb, maskf, maskb)] for a in range(2))

    def ada_product(w, out):
        for kt in range(KT):
            for c in range(4):
                last = nc.tensor.matmul(out[32 * c:32 * (c + 1), :], cs[:, kt, :], w[:, kt, P * c:P * (c + 1)],
                                        start=(kt == 0), stop=(kt == KT - 1))
        return last

    def ada_weights(slot):
        return ring[:, slot, 0:KT * 512].rearrange("p (k n) -> p k n", k=KT)

    def ada_columns(which, n):
        return A["w_ada"][which, :, 512 * n:512 * (n + 1)].rearrange("(p k) n -> p k n", k=KT)

    def load_bias(eng, which, lo, hi, sem):
        for c in range(4):
            eng.dma_start(ada[32 * c + 2:32 * c + 3, lo:hi, :],
                          A["b_ada"][bass.ds(which, 1), :].rearrange("l (n c m) -> l n c m", c=4, m=P)[:, lo:hi, c, :])\
               .then_inc(sem, 16)

    CONSTANTS = ((cs, 0.0), (ident, 0.0), (flip, 0.0), (pick, 0.0), (mf, 1.0), (mb, 1.0), (suf, 1.0), (maskf, 1.0),
                 (maskb, 1.0), (maskr, 0.0), (tri8, 1.0), (zero, 0.0), (s0, 0.0), (wg, 0.0), (lrT, 1.0), (hpad, 0.0),
                 (gate, 0.0), (ones, 1.0), (wanted[:, 1, 0:CAP[0]], float(CAP[0])), (wanted[:, 1, CAP[0]:], float(CAP[1])))
    first_in = [s["first_in0"], s["first_in1"], s["first_in2"], s["first_in3"]]
    with nc.Block() as block:
        @block.gpsimd
        def _(pool):
            for first, cap in zip(FIRST, CAP):
                number(wanted[:, 0, first:first + cap], [[1, cap]])
            number(rank_at[:, 0::2], [[1, EPAIRS]])
            number(rank_at[:, 1::2], [[-1, EPAIRS]], base=EXPERTS - 1)
            number(expert_no[:], [[0, EXPERTS]], mult=1)

            pool.wait_ge(s["const_set"], len(CONSTANTS))
            keep(ident[:], ALU.not_equal, 1.0, 0, [[-1, P]], 1)
            keep(flip[:], ALU.not_equal, 1.0, -(P - 1), [[1, P]], 1)
            for c in range(4):
                for st in range(STREAMS):
                    keep(pick[:, c, st, :], ALU.not_equal, 1.0, -(32 * c + st), [[0, P]], 1)
            keep(mf[:, LEVELS, :], ALU.is_ge, 0.0, 0, [[1, P]], -1)
            keep(mb[:, LEVELS, :], ALU.is_ge, 0.0, 0, [[-1, P]], 1)
            keep(suf[:, 0, :], ALU.is_ge, 0.0, -1, [[-1, P]], 1)
            keep(suf[:, 1, :], ALU.is_ge, 0.0, -1, [[1, P]], -1)
            step(nc.gpsimd.memset(maskf[:, LEVELS, :], 0.0))
            rows = [maskr[64 * half:64 * half + 64, :].rearrange("p (r k) -> p r k", k=GRID_W) for half in range(2)]
            for half in range(2):
                steps_done(pool)
                keep(rows[half][:, :, 0:48], ALU.is_ge, NEVER, -(GRID_W - 1 - 8), [[0, 2], [1, 48]], 1)
            steps_done(pool)
            keep(tri8[:], ALU.is_ge, 0.0, -1, [[1, GROUPS], [-1, GROUPS]], 0)
            steps_done(pool)
            for c in range(4):
                for st in range(STREAMS):
                    keep(pick[:, c, st, :], ALU.not_equal, 1.0, -(32 * c + 2), [[0, P]], 1)
            keep(maskf[:, LEVELS, :], ALU.not_equal, 2.0, 0, [[-1, P]], 1)
            for half in range(2):
                steps_done(pool)
                keep(rows[half][:, :, 16:64], ALU.is_ge, NEVER, GRID_W - 1 + 7 - 16, [[0, 2], [-1, 48]], -1)
            steps_done(pool)

        @block.sync
        def _(sp):
            sp.dma_start(craw[:, 0, 0, :], A["c_ctx"].rearrange("(p k) -> p k", k=KT)).then_inc(s["c_loaded"], 16)
            sp.dma_start(craw[:, 0, 1, :], A["c"][0].rearrange("(p k) -> p k", k=KT)).then_inc(s["c_loaded"], 16)
            for n in range(ADA_FIRST):
                sp.dma_start(ada_weights(n), ada_columns(0, n)).then_inc(first_in[n], 16)
            for st, name in ((0, "x_prompt"), (1, "x_sample")):
                sp.dma_start(x[:, st, :], A[name][0]).then_inc(s["x_loaded"], 16)
            sp.wait_ge(s["x_loaded"], 32)

        @block.tensor
        def _(pe):
            pe.wait_ge(s["c_step"], 1)
            for n in range(ADA_FIRST):
                pe.wait_ge(first_in[n], 16)
                ada_product(ada_weights(n), ps[:, n, 0:P]).then_inc(s["first_done"], 1)

        @block.scalar
        def _(act):
            act.wait_ge(s["c_loaded"], 32)
            nc.scalar.activation(craw[:, 1], craw[:, 0], ACT.Sigmoid).then_inc(s["c_sig"], 1)
            for n in range(ADA_FIRST):
                act.wait_ge(s["first_done"], n + 1)
                nc.scalar.copy(ada[:, n, :], ps[:, n, 0:P]).then_inc(s["first_kept"], 1)
            act.wait_ge(s["first_kept"], ADA_FIRST)
            load_bias(act, 0, 0, ADA_FIRST, s["first_bias"])
            act.wait_ge(s["first_bias"], 64)

        @block.vector
        def _(dve):
            for t, val in CONSTANTS:
                nc.vector.memset(t[:], val).then_inc(s["const_set"], 1)
            dve.wait_ge(s["c_sig"], 1)
            dve.wait_ge(s["const_set"], 1)
            nc.vector.tensor_tensor(cs[:, :, 0:2].rearrange("p k s -> p s k"), craw[:, 0], craw[:, 1],
                                    ALU.mult).then_inc(s["c_step"], 1)

    def dma_in(eng, out, in_, sem):
        eng.dma_start(out, in_).then_inc(sem, 16)

    def pre_slot(n):
        return n % PRE_SLOTS

    def pre_loaded(eng, n):
        eng.wait_ge(chunk_in[pre_slot(n)], 16 * (n // PRE_SLOTS + 1))

    def load_gate_up(eng, slot, weights, sem):
        for j, w in enumerate(weights):
            dma_in(eng, slot[:, KT * FF * j:KT * FF * (j + 1)].rearrange("p (k n) -> p k n", k=KT),
                   w.rearrange("(p k) n -> p k n", k=KT), sem)

    def load_down(eng, slot, w, sem):
        dma_in(eng, slot[:, 2 * KT * FF:SLOT].rearrange("p (j n) -> p j n", j=2),
               w.rearrange("(p j) n -> p j n", j=2), sem)

    def gate_up(slot, k):
        return slot[:, 0:2 * KT * FF].rearrange("p (a k n) -> p a k n", a=2, k=KT)[:, :, k, :]

    def down(slot, j, half):
        return slot[:, 2 * KT * FF:SLOT].rearrange("p (j n) -> p j n", j=2)[:, j, 512 * half:512 * (half + 1)]

    def chunk_used(eng, n):
        if n < C_ADA:
            eng.wait_ge(s["proj_done"], LAST_UNIT[n] + 1)
        elif n < C_OUT:
            eng.wait_ge(s["ada_done"], n - C_ADA + 1)
        elif n < C_SH:
            eng.wait_ge(s["mix_shown"], 2 * (n - C_OUT + 1))
        else:
            eng.wait_ge(s["sh_done"], STREAMS)

    chunk_in = [s["chunk_in0"], s["chunk_in1"], s["chunk_in2"]]
    expert_in = [s["expert_in0"], s["expert_in1"], s["expert_in2"], s["expert_in3"]]
    N_SMALL, N_VEC, N_ATTN = 18, 8, 2 * HEADS + 2

    layers = nc.Fori(0, DEPTH)
    layer = layers.__enter__()
    following = (layer + 1) % DEPTH
    with nc.Block() as block:
        @block.sync
        def _(sp):
            dma_in(sp, gbc[:], A["norm_mix"][bass.ds(layer, 1), :].partition_broadcast(P)[:, 0, :], s["norm_in"])
            for n in range(PRE):
                if n >= PRE_SLOTS:
                    chunk_used(sp, n - PRE_SLOTS)
                slot = ring[:, pre_slot(n), :]
                sem = chunk_in[pre_slot(n)]
                if C_ADA <= n < C_OUT:
                    m = n - C_ADA
                    dma_in(sp, ada_weights(pre_slot(n)), ada_columns(layer, ADA_FIRST + m) if m < ADA_LATER else
                           ada_columns(following, m - ADA_LATER), sem)
                elif n < C_ADA:
                    c0, cw = IN_CHUNKS[n]
                    dma_in(sp, slot[:, 0:KT * cw].rearrange("p (k n) -> p k n", k=KT),
                           A["w_in"][layer, :, c0:c0 + cw].rearrange("(p k) n -> p k n", k=KT), sem)
                elif n < C_SH:
                    c0 = 512 * (n - C_OUT)
                    dma_in(sp, slot[:, 0:KT * 512].rearrange("p (k n) -> p k n", k=KT),
                           A["w_out"][layer, :, c0:c0 + 512].rearrange("(k p) n -> p k n", p=P), sem)
                else:
                    load_gate_up(sp, slot, [A[w][layer] for w in ("sh_w_gate", "sh_w_up")], s["shared_in"])
                    load_down(sp, slot, A["sh_w_down"][layer], s["shared_in"])
                if n == 1:
                    for r0, r1, name in ((R_DW, R_DWB, "conv_dw"),):
                        dma_in(sp, vec[r0:r1, :], A[name][layer], s["small_in"])
                    for r, name in ((R_DWB, "conv_dw_b"), (R_LNG, "conv_ln_g"), (R_LNB, "conv_ln_b")):
                        dma_in(sp, vec[r:r + 1, :], A[name][bass.ds(layer, 1), :], s["small_in"])
                    dma_in(sp, vec[R_ON:R_ON + 1, 0:DV], A["gla_out_norm"][bass.ds(layer, 1), :], s["small_in"])
                    dma_in(sp, vec[R_ON:R_ON + 1, DV:2 * DV], A["gla_out_norm"][bass.ds(layer, 1), :], s["small_in"])
                    for r, name in ((R_QN, "na_q_norm"), (R_KN, "na_k_norm")):
                        for j in range(CONV_CH // DK):
                            dma_in(sp, vec[r:r + 1, DK * j:DK * (j + 1)], A[name][bass.ds(layer, 1), :], s["vec_in"])
                    dma_in(sp, gk[:], A["na_k_norm"][bass.ds(layer, 1), :].partition_broadcast(P)[:, 0, :], s["small_in"])
                    for dr in range(2):
                        dma_in(sp, wg[RANK * dr:RANK * (dr + 1), 256 * dr:256 * (dr + 1)],
                               A["gla_w_gate"][layer, dr], s["small_in"])
                        dma_in(sp, wg[32:33, 256 * dr:256 * (dr + 1)],
                               A["gla_b_gate"][layer, dr:dr + 1, :], s["small_in"])
                        for e in range(2):
                            dma_in(sp, s0[DK * e:DK * (e + 1), dr, e::2, :],
                                   A["state_gla"][0, layer, dr, e::2].rearrange("h d v -> d h v"), s["small_in"])
                    dma_in(sp, wpw[:], A["conv_pw"][layer].rearrange("(c p) n -> p c n", p=P), s["small_in"])
                    dma_in(sp, wr[:], A["router_w"][layer].rearrange("(p k) n -> p k n", k=KT), s["small_in"])
                    dma_in(sp, rbias[:], A["router_bias"][bass.ds(layer, 1), :].partition_broadcast(P)[:, 0, :], s["small_in"])
                if n == C_ADA - 1:
                    sp.wait_ge(s["h_ready"], STREAMS)
                    dma_in(sp, gbc[:], A["norm_ffn"][bass.ds(layer, 1), :].partition_broadcast(P)[:, 0, :], s["norm_in"])
                if n == PRE_SLOTS:
                    for half in range(2):
                        for hh in range(HEADS):
                            sp.dma_start(
                                biasr[64 * half:64 * (half + 1), hh, :].rearrange("p (r k) -> p r k", k=GRID_W),
                                rpb_window(A["na_rpb"], layer, hh, half)).then_inc(s["attn_in"], 16)
                    for a, name in enumerate(("cache_na_k", "cache_na_v")):
                        dma_in(sp, kvc[:, a, :].rearrange("p (h d) -> p h d", h=HEADS),
                               A[name][0, layer].rearrange("h t d -> t h d"), s["attn_in"])
            sp.wait_ge(s["order_ready"], 1)
            firsts = [sp.value_load(order_i[0:1, k:k + 1], min_val=0, max_val=EXPERTS - 1) for k in range(SLOTS)]
            for k in range(SLOTS):
                slot = expert_slot(k)
                if slot < PRE_SLOTS:
                    last = max(n for n in range(PRE) if pre_slot(n) == slot)
                    chunk_used(sp, last)
                else:
                    sp.wait_ge(s["st_kept"], 1)
                    sp.wait_ge(s["go_ready"], STREAMS)
                    sp.wait_ge(s["stored"], 16 * STORES * (layer + 1))
                e = firsts[k]
                load_gate_up(sp, ring[:, slot, :],
                             [A[w][layer, bass.ds(e, 1)][0] for w in ("exp_w_gate", "exp_w_up")], expert_in[slot])
                load_down(sp, ring[:, slot, :], A["exp_w_down"][layer, bass.ds(e, 1)][0], expert_in[slot])
            with sp.Fori(1, EXPERTS // SLOTS) as i:
                for pair in range(TURN):
                    e = [sp.value_load(order_i[0:1, bass.ds(i * SLOTS + q, 1)], min_val=0, max_val=EXPERTS - 1)
                         for q in (2 * pair, 2 * pair + 1)]
                    sp.wait_ge(s["gu_free"], i * TURN + pair - TURN + 1)
                    for q in (2 * pair, 2 * pair + 1):
                        load_gate_up(sp, ring[:, expert_slot(q), :],
                                     [A[w][layer, bass.ds(e[q % 2], 1)][0] for w in ("exp_w_gate", "exp_w_up")],
                                     expert_in[expert_slot(q)])
                    sp.wait_ge(s["Y_shown"], i * (2 * TURN) + 2 * (pair - 1))
                    sp.wait_ge(s["over_done"], i * (TURN * (PASSES - 1)) + (PASSES - 1) * (pair - 1))
                    for q in (2 * pair, 2 * pair + 1):
                        load_down(sp, ring[:, expert_slot(q), :],
                                  A["exp_w_down"][layer, bass.ds(e[q % 2], 1)][0], expert_in[expert_slot(q)])

        def rsqrt_dve(dve, link, k, ss, v, r0, t, r, scale):
            nc.vector.tensor_scalar(v, ss, scale, EPS, ALU.mult, ALU.add).then_inc(s["var_ready"], 1)
            dve.wait_ge(s["root_ready"], k + 1)
            link(nc.vector.tensor_tensor(t, r0, r0, ALU.mult))
            link(nc.vector.tensor_tensor(t, t, v, ALU.mult))
            link(nc.vector.tensor_scalar(t, t, -0.5, 1.5, ALU.mult, ALU.add))
            link(nc.vector.tensor_tensor(r, r0, t, ALU.mult))

        def rsqrt_act(act, link, k, v, r0):
            act.wait_ge(s["var_ready"], k + 1)
            link(nc.scalar.activation(r0, v, ACT.Ln))
            nc.scalar.activation(r0, r0, ACT.Exp, scale=-0.5).then_inc(s["root_ready"], 1)

        def numbers(k, part):
            at, n = ((0, 2), (20, 16), (10, 2), (100, 4), (120, 4), (140, 2))[k]
            return sm[:, at + n * part:at + n * (part + 1)]

        N_IN, N_QK, N_CONV, N_GLA, N_FFN = 0, 1, 2, 3, 5
        conv_mean = sm[:, 150:152]
        mx = sm[:, 152:160]
        p_sum = sm[:, 160:168]
        p_inv = sm[:, 168:176]

        def decayed(eng, tt, g):
            st, a, dr = g // 4, g // 2 % 2, g % 2
            eng.wait_ge(s["E_ready"], g + 1)
            if g >= 2:
                eng.wait_ge(s["pair_shown"], 2 * (g - 1))
            q_, k_ = (t[:, a, P * st:P * (st + 1)] for t in (qT, kT))
            for lv in range(LEVELS):
                w = P >> (lv + 1)
                for part, src in ((0, (k_, q_)[dr]), (1, (q_, k_)[dr])):
                    views = [t.rearrange("p (b a r) -> p b a r", a=2, r=w)[:, :, part, :]
                             for t in (X[:, dr, lv, :], E[:, dr, lv, :], src)]
                    last = tt(*views, ALU.mult)
            if st == 1:
                last = tt(qd[:, a, dr, :], E[:, dr, LEVELS, :], q_, ALU.mult)
            last.then_inc(s["X_ready"], 1)

        def ada_bank(m):
            return bank(m % 2 if m < ADA_EARLY else 4 + m % 2 if m < ADA_GLA else 5, 0, P)

        @block.tensor
        def _(pe):
            mm = nc.tensor.matmul

            def show(n, st, b):
                for c in range(4):
                    last = mm(bank(b, P * c, P * (c + 1)), pick[:, c, st, :], ada[:, n, :], start=True, stop=True)
                return last

            def modulation(k):
                for st in range(STREAMS):
                    for half in range(2):
                        show(6 * k + 2 + half, st, 4 * st + half)
                    for half in range(2):
                        last = show(6 * k + half, st, 4 * st + 2 + half)
                    last.then_inc(s["mod_shown"], 1)

            def turn_h(k):
                for st in range(STREAMS):
                    pe.wait_ge(s["h_ready"], STREAMS * k + st + 1)
                    ht = h[:, st, :].rearrange("t (p k) -> t k p", k=KT)
                    for kt in range(KT):
                        last = nc.tensor.transpose(bank(4 * st + kt // 4, P * (kt % 4), P * (kt % 4 + 1)),
                                                   ht[:, kt, :], ident[:])
                    last.then_inc(s["hT_shown"], 1)

            def ada_step(m):
                pre_loaded(pe, C_ADA + m)
                if m == 0:
                    pe.wait_ge(s["la_ready"], STREAMS)
                elif m == ADA_EARLY + 1:
                    pe.wait_ge(s["cat_conv"], 1)
                elif m > ADA_GLA:
                    pe.wait_ge(s["ada_kept"], m)
                elif m != ADA_EARLY and m > 1:
                    pe.wait_ge(s["ada_kept"], m - 1)
                ada_product(ada_weights(pre_slot(C_ADA + m)), ada_bank(m)).then_inc(s["ada_done"], 1)

            modulation(0)
            turn_h(0)
            pe.wait_ge(s["hT_ready"], STREAMS)
            for u, (c, c0, w, by_channel, st) in enumerate(UNITS_IN):
                if u == 0 or UNITS_IN[u - 1][0] != c:
                    pre_loaded(pe, c)
                if u >= len(PROJ_BANKS):
                    pe.wait_ge(s["proj_kept"], u - len(PROJ_BANKS) + 1)
                cw = IN_CHUNKS[c][1]
                wt = ring[:, pre_slot(c), 0:KT * cw].rearrange("p (k n) -> p k n", k=KT)[:, :, c0:c0 + w]
                b = PROJ_BANKS[u % len(PROJ_BANKS)]
                for kt in range(KT):
                    if by_channel:
                        last = mm(ps[0:w, b, 0:STREAMS * P], wt[:, kt, :], hT[:, kt, :],
                                  start=(kt == 0), stop=(kt == KT - 1))
                    else:
                        last = mm(bank(b, 0, w), hT[:, kt, P * st:P * (st + 1)], wt[:, kt, :],
                                  start=(kt == 0), stop=(kt == KT - 1))
                last.then_inc(s["proj_done"], 1)
                if u == 3:
                    pe.wait_ge(s["small_in"], 16 * N_SMALL)
                    pe.wait_ge(s["vec_in"], 16 * N_VEC)
                    for c in range(2):
                        last = nc.tensor.transpose(bank(5, 64 * c, 64 * c + R_END), vec[:, P * c:P * (c + 1)],
                                                   ident[0:R_END, 0:R_END])
                    last.then_inc(s["vec_shown"], 1)
                if u == 4:
                    pe.wait_ge(s["proj_kept"], 1)
                    for st2 in range(STREAMS):
                        mm(bank(st2), lrT[:, P * st2:P * (st2 + 1)], wg[:], start=True,
                           stop=True).then_inc(s["z_shown"], 1)
            pe.wait_ge(s["vec_ready"], 1)
            pe.wait_ge(s["conv_ready"], 1)
            for st in range(STREAMS):
                for c in range(2):
                    at = 256 * st + P * c
                    last = nc.tensor.transpose(bank(4, at, at + P), cacc[:, c, st, :], ident[:])
            last.then_inc(s["convT_shown"], 1)
            for m in range(3):
                ada_step(m)
            pe.wait_ge(s["ctok_ready"], 1)
            for c in range(2):
                for st in range(STREAMS):
                    at = 256 * c + P * st
                    last = nc.tensor.transpose(bank(5, at, at + P), cTok[:, st, P * c:P * (c + 1)], ident[:])
            last.then_inc(s["convB_shown"], 1)
            ada_step(3)
            ada_step(4)
            pe.wait_ge(s["cact_ready"], 1)
            for o in range(2):
                for c in range(2):
                    last = mm(bank(4, 256 * o, 256 * (o + 1)), wpw[:, c, P * o:P * (o + 1)],
                              cacc[:, c, :, :].rearrange("p s t -> p (s t)"), start=(c == 0), stop=(c == 1))
            last.then_inc(s["pw_shown"], 1)
            pe.wait_ge(s["nq_ready"], 1)
            pe.wait_ge(s["proj_kept"], len(UNITS_IN))
            pe.wait_ge(s["attn_in"], 16 * N_ATTN)
            for b, c0 in ((2, 0), (3, 256)):
                for a in range(PAIRS):
                    for st in range(STREAMS):
                        at = 256 * a + P * st
                        nc.tensor.transpose(bank(b, at, at + P), nq[:, st, c0 + P * a:c0 + P * (a + 1)], ident[:])
            for a in range(PAIRS):
                last = nc.tensor.transpose(bank(6, P * a, P * (a + 1)), kvc[:, 0, P * a:P * (a + 1)], ident[:])
            last.then_inc(s["nT_shown"], 1)
            ada_step(5)
            pe.wait_ge(s["nT_ready"], 1)
            pe.wait_ge(s["bias_ready"], 1)
            for e in range(2):
                r = slice(DK * e, DK * (e + 1))
                for a in range(PAIRS):
                    last = mm(bank(2 + e, P * a, P * (a + 1)), qnT[r, a, 0:P], knT[r, a, 0:P], start=True, stop=True)
            last.then_inc(s["scores_shown"], 1)
            for e in range(2):
                r = slice(DK * e, DK * (e + 1))
                for a in range(PAIRS):
                    local = bank(6 + e, 256 * a, 256 * a + P)
                    mm(local, qnT[r, a, P:2 * P], knT[r, a, P:2 * P], start=True, stop=False)
                    mm(local, flip[:], biasr[:, 2 * a + e, :], start=False, stop=True)
                    last = mm(bank(6 + e, 256 * a + P, 256 * (a + 1)), qnT[r, a, P:2 * P], kcT[r, a, :],
                              start=True, stop=True)
            last.then_inc(s["scores_shown"], 1)
            ada_step(6)
            ada_step(7)
            pe.wait_ge(s["p_ready"], 1)
            pe.wait_ge(s["ada_kept"], ADA_EARLY)
            blocks = [(p0[:, i, :]) for i in range(HEADS)]
            blocks += [p1[:, i, P * j:P * (j + 1)] for i in range(HEADS) for j in range(2)]
            for i, block_in in enumerate(blocks):
                last = nc.tensor.transpose(bank(i // 4, P * (i % 4), P * (i % 4 + 1)), block_in, ident[:])
            last.then_inc(s["pT_shown"], 1)
            ada_step(8)
            pe.wait_ge(s["pT_ready"], 1)
            for e in range(2):
                for a in range(PAIRS):
                    hh, i = 2 * a + e, 2 * e + a
                    c0 = 2 * HEADS * DK + DK * hh
                    out = ps[DK * e:DK * (e + 1), 3, :]
                    mm(out[:, 256 * a:256 * a + P], nax[:, 0, c0:c0 + DK], pT[:, i, :], start=True, stop=True)
                    out1 = out[:, 256 * a + P:256 * (a + 1)]
                    mm(out1, nax[:, 1, c0:c0 + DK], pT[:, HEADS + 2 * i, :], start=True, stop=False)
                    last = mm(out1, kvc[:, 1, DK * hh:DK * (hh + 1)], pT[:, HEADS + 2 * i + 1, :],
                              start=False, stop=True)
            last.then_inc(s["pv_shown"], 1)

            def decays(g):
                st, a, dr = g // 4, g // 2 % 2, g % 2
                if g:
                    pe.wait_ge(s["E_ready"], g)
                m = (mf, mb)[dr]
                for b in range(2):
                    last = mm(bank(b), la[:, st, dr, P * a:P * (a + 1)],
                              m[:, 4 * b:4 * (b + 1), :].rearrange("p l n -> p (l n)"), start=True, stop=True)
                last.then_inc(s["decay_shown"], 1)

            def pairs(g):
                st, a, dr = g // 4, g // 2 % 2, g % 2
                pe.wait_ge(s["X_ready"], g + 1)
                for e in range(2):
                    if g:
                        pe.wait_ge(s["masked"], 2 * (g - 1) + e + 1)
                    r = slice(DK * e, DK * (e + 1))
                    for lv in range(LEVELS + (dr == 0)):
                        out = bank((2, 6)[e] + lv // 4, P * (lv % 4), P * (lv % 4 + 1))
                        if lv < LEVELS:
                            last = mm(out, X[r, dr, lv, :], X[r, dr, lv, :], start=True, stop=True)
                        else:
                            last = mm(out, kT[r, a, P * st:P * (st + 1)], qT[r, a, P * st:P * (st + 1)],
                                      start=True, stop=True)
                    last.then_inc(s["pair_shown"], 1)

            def outputs(g):
                st, a = g // 4, g // 2 % 2
                if a == 0:
                    pe.wait_ge(s["ada_kept"], (ADA_GLA, ADA_CHUNKS)[st])
                for e in range(2):
                    pe.wait_ge(s["att_ready"], 2 * (g // 2) + e + 1)
                    hh = 2 * a + e
                    out = bank(4 + st, DV * hh, DV * (hh + 1))
                    last = mm(out, att[:, a, e, :], v[:, st, DV * hh:DV * (hh + 1)], start=True, stop=(st == 0))
                    if st == 1:
                        for dr in range(2):
                            last = mm(out, qd[:, a, dr, :], s0[:, dr, hh, :], start=False, stop=(dr == 1))
                    last.then_inc(s["o_shown"], 1)

            pe.wait_ge(s["matrices"], 1)
            decays(0)
            decays(1)
            pe.wait_ge(s["cat_na"], 1)
            pe.wait_ge(s["cat_conv"], 1)
            for g in range(8):
                pairs(g)
                if ADA_GLA + g < ADA_CHUNKS:
                    ada_step(ADA_GLA + g)
                if g + 2 < 8:
                    decays(g + 2)
                if g % 2 == 0 and g:
                    outputs(g - 1)
            outputs(7)
            pe.wait_ge(s["masked"], 16)
            for a in range(PAIRS):
                nc.tensor.transpose(bank(2, P * a, P * (a + 1)), kT[:, a, 0:P], ident[:])
            for dr in range(2):
                last = mm(bank(3, 256 * dr, 256 * (dr + 1)), suf[:, dr, :], la[:, 0, dr, :], start=True, stop=True)
            last.then_inc(s["st_pre"], 1)
            pe.wait_ge(s["kd_ready"], 1)
            for dr in range(2):
                for hh in range(HEADS):
                    last = mm(ps[0:DK, 6 + dr, DV * hh:DV * (hh + 1)], kd[:, dr, DK * hh:DK * (hh + 1)],
                              v[:, 0, DV * hh:DV * (hh + 1)], start=True, stop=True)
            last.then_inc(s["st_shown"], 1)

            def mix(half, st, tiles):
                w = ada_weights(pre_slot(C_OUT + half))
                for kt in tiles:
                    last = mm(bank(PROJ_BANKS[2 * half + st]), cat[:, kt, P * st:P * (st + 1)], w[:, kt, :],
                              start=(kt == HEADS), stop=(kt == HEADS - 1))
                return last

            for half in range(2):
                pre_loaded(pe, C_OUT + half)
                if half == 1:
                    pe.wait_ge(s["st_kept"], 1)
                for st in range(STREAMS):
                    mix(half, st, range(HEADS, KT))
            for st in range(STREAMS):
                pe.wait_ge(s["go_ready"], st + 1)
                for hh in range(HEADS):
                    last = nc.tensor.transpose(bank(st, P * hh, P * (hh + 1)), gg[:, st, P * hh:P * (hh + 1)], ident[:])
                last.then_inc(s["goT_shown"], 1)
            pe.wait_ge(s["bias_in"], 64)
            pe.wait_ge(s["cat_gla"], STREAMS)
            for half in range(2):
                for st in range(STREAMS):
                    show(4 + half, st, (4, 5, 0, 1)[2 * half + st])
                    mix(half, st, range(HEADS)).then_inc(s["mix_shown"], 1)
            pe.wait_ge(s["x_mid"], 4)
            modulation(1)
            turn_h(1)
            pe.wait_ge(s["hT_ready"], 2 * STREAMS)
            for st in range(STREAMS):
                for kt in range(KT):
                    last = mm(bank(2 + 4 * st, 0, EXPERTS), hT[:, kt, P * st:P * (st + 1)], wr[:, kt, :],
                              start=(kt == 0), stop=(kt == KT - 1))
                last.then_inc(s["logits_shown"], 1)
            for st in range(STREAMS):
                for half in range(2):
                    last = show(10 + half, st, 4 * st + half)
            last.then_inc(s["g2_shown"], 1)

            pe.wait_ge(s["chosen_ready"], 1)
            pe.wait_ge(s["scored"], STREAMS)
            mm(bank(2, 0, EXPERTS), suf[:, 1, :], sel[:, 0, :], start=True, stop=True)
            mm(bank(2, 64, 64 + EXPERTS), suf[:, 1, :], sel[:, 1, :], start=True, stop=False)
            mm(bank(2, 64, 64 + EXPERTS), ones[:], sel[:, 0, :], start=False, stop=True)
            mm(bank(2, 128, 128 + EXPERTS), ones[:], sel[:, 0, :], start=True, stop=False)
            mm(bank(2, 128, 128 + EXPERTS), ones[:], sel[:, 1, :], start=False, stop=True)
            for st in range(STREAMS):
                last = mm(ps[0:EXPERTS, 2, 192:192 + EXPERTS], sel[:, st, :], ones[:, 0:EXPERTS], start=(st == 0),
                          stop=(st == STREAMS - 1))
            last.then_inc(s["counted"], 1)

            shared = ring[:, pre_slot(C_SH), :]
            pe.wait_ge(s["shared_in"], 48)
            pe.wait_ge(s["g2_kept"], 1)
            for st in range(STREAMS):
                for kt in range(KT):
                    last = mm(bank(4 + st), hT[:, kt, P * st:P * (st + 1)], gate_up(shared, kt),
                              start=(kt == 0), stop=(kt == KT - 1))
                last.then_inc(s["sh_gu"], 1)
                if st == 0:
                    pe.wait_ge(s["ordered"], 1)
                    for st2 in range(STREAMS):
                        nc.tensor.transpose(ps[0:EXPERTS, 6, P * st2:P * (st2 + 1)], place[:, st2, 0:EXPERTS], ident[:])
                        last = nc.tensor.transpose(ps[0:EXPERTS, 6, P * (2 + st2):P * (3 + st2)],
                                                   gate[:, st2, 0:EXPERTS], ident[:])
                    last.then_inc(s["tables_shown"], 1)
                    mm(ps[0:EXPERTS, 7, 256:256 + EXPERTS], expert_no[0:EXPERTS, :], order, start=True, stop=True)
                    mm(ps[0:EXPERTS, 7, 320:320 + EXPERTS], own_load, order, start=True, stop=True)
                    pe.wait_ge(s["tables_kept"], 1)
                    for a in range(4):
                        last = mm(bank(7, EXPERTS * a, EXPERTS * (a + 1)), tables[:, a, :], order, start=True, stop=True)
                    last.then_inc(s["sorted_shown"], 1)
            pe.wait_ge(s["places"], 1)
            for b in range(4):
                mm(bank(b), zero[:], mf[:, 0:4, :].rearrange("p l n -> p (l n)"), start=True, stop=False,
                   skip_group_check=True)

            def gather(X_bank, onehot, half):
                for k in range(KT // 2):
                    for st in range(STREAMS):
                        for part in range(3):
                            last = mm(bank(X_bank, P * k, P * (k + 1)), hs[:, part, st, KT // 2 * half + k, :],
                                      onehot[:, st],
                                      start=(st == 0 and part == 0), stop=(st == STREAMS - 1 and part == 2))
                return last

            def gate_up_pair(b, slots):
                for kt in range(KT):
                    for first, n, c in TILES:
                        last = mm(ps[first:first + n, 4, :], X_e[:, b, kt, first:first + n],
                                  gate_up(ring[:, slots[c], :], kt), start=(kt == 0), stop=(kt == KT - 1))
                return last

            def turn_pair(weights):
                for st in range(STREAMS):
                    nc.tensor.transpose(bank(5, FF + P * st, FF + P * (st + 1)),
                                        weights[:, st], ident[:])

            def turn_acts(b):
                a_in = acts[:, b, :].rearrange("t (p j) -> t j p", j=2)
                for j in range(2):
                    last = nc.tensor.transpose(bank(5, P * j, P * (j + 1)), a_in[:, j, :], ident[:])
                return last

            def down_pair(turned, slots, half):
                for j in range(2):
                    for first, n, c in TILES:
                        last = mm(ps[first:first + n, 7, :], turned[:, P * j + first:P * j + first + n],
                                  down(ring[:, slots[c], :], j, half), start=(j == 0), stop=(j == 1))
                return last

            def scatter(turned, y):
                for st in range(STREAMS):
                    for half in range(2):
                        last = mm(bank(2 * st + half), turned[:, FF + P * st:FF + P * (st + 1)],
                                  y[:, 512 * half:512 * (half + 1)], start=False, stop=False, skip_group_check=True)
                return last

            pe.wait_ge(s["G_ready"], 1)
            pe.wait_ge(s["hs3"], STREAMS)
            gather(6, G[0], 0).then_inc(s["X_shown"], 1)
            for st in range(STREAMS):
                pe.wait_ge(s["sh_act"], st + 1)
                a_in = acts[:, st, :].rearrange("t (p j) -> t j p", j=2)
                for j in range(2):
                    last = nc.tensor.transpose(bank(4 + st, P * j, P * (j + 1)), a_in[:, j, :], ident[:])
                last.then_inc(s["sh_turned"], 1)
            pe.wait_ge(s["X_kept"], 1)
            gather(6, G[0], 1).then_inc(s["X_shown"], 1)
            for st in range(STREAMS):
                pe.wait_ge(s["sh_kept"], st + 1)
                for half in range(2):
                    for j in range(2):
                        last = mm(bank(2 * st + half), sh_actT[:, st, P * j:P * (j + 1)], down(shared, j, half),
                                  start=False, stop=False, skip_group_check=True)
                last.then_inc(s["sh_done"], 1)
            with pe.Fori(0, EPAIRS // TURN) as i:
                for q in range(TURN):
                    slots = (expert_slot(2 * q), expert_slot(2 * q + 1))
                    tokens = pe.value_load(most_i[0:1, bass.ds(i * TURN + q, 1)], min_val=0, max_val=SKEW * STREAMS * P)
                    for c in range(2):
                        pe.wait_ge(expert_in[slots[c]], i * 48 + 48)
                    pe.wait_ge(s["X_kept"], i * (2 * TURN) + 2 * q + 2)
                    gate_up_pair(q, slots).then_inc(s["gu_done"], 1)
                    pe.wait_ge(s["Y_kept"], i * (2 * TURN) + 2 * q + 2)
                    scatter(turn, Y).then_inc(s["scattered"], 1)
                    pe.wait_ge(s["S_ready"], i * TURN + q + 1)
                    turn_pair(S[0])
                    pe.wait_ge(s["act_done"], i * TURN + q + 1)
                    turn_acts(0).then_inc(s["turned"], 1)
                    with pe.If(tokens < CAP[0] + 1):
                        pe.wait_ge(s["gu_done"], i * TURN + q + 1)
                        pe.sem_inc(s["gu_free"], 1)
                    pe.wait_ge(s["G_ready"], i * TURN + q + 2)
                    gather(6, G[1 - q], 0).then_inc(s["X_shown"], 1)
                    pe.wait_ge(s["turn_kept"], i * TURN + q + 1)
                    down_pair(turn, slots, 0).then_inc(s["Y_shown"], 1)
                    pe.wait_ge(s["X_kept"], i * (2 * TURN) + 2 * q + 3)
                    gather(6, G[1 - q], 1).then_inc(s["X_shown"], 1)
                    pe.wait_ge(s["Y_kept"], i * (2 * TURN) + 2 * q + 3)
                    down_pair(turn, slots, 1).then_inc(s["Y_shown"], 1)
                    def further(r):
                        m = (i * TURN + q) * (PASSES - 1) + r
                        pe.wait_ge(s["X_kept"], i * (2 * TURN) + 2 * q + 4)
                        pe.wait_ge(s["Y_kept"], i * (2 * TURN) + 2 * q + 4)
                        pe.wait_ge(s["over_GS"], m)
                        gather(6, G[2], 0).then_inc(s["over_Xs"], 1)
                        pe.wait_ge(s["over_Xk"], m * 2 - 1)
                        gather(6, G[2], 1).then_inc(s["over_Xs"], 1)
                        turn_pair(S[1])
                        pe.wait_ge(s["over_Xk"], m * 2)
                        gate_up_pair(q, slots).then_inc(s["over_gu"], 1)
                        pe.wait_ge(s["over_act"], m)
                        turn_acts(1).then_inc(s["over_turned"], 1)
                        pe.wait_ge(s["over_kept"], m)
                        down_pair(turn_over, slots, 0).then_inc(s["over_Ys"], 1)
                        pe.wait_ge(s["over_Yk"], m * 2 - 1)
                        down_pair(turn_over, slots, 1).then_inc(s["over_Ys"], 1)
                        pe.wait_ge(s["over_Yk"], m * 2)
                        scatter(turn_over, Y_over).then_inc(s["over_done"], 1)
                        pe.wait_ge(s["over_done"], m)
                        pe.sem_inc(s["over_left"], 1)

                    def skipped(k):
                        for name, n in (("over_Xs", 2), ("over_gu", 1), ("over_turned", 1), ("over_Ys", 2),
                                        ("over_done", 1)):
                            pe.sem_inc(s[name], n * k)

                    with pe.If(tokens > CAP[0]):
                        further(1)
                        with pe.If(tokens > 2 * CAP[0]):
                            with pe.Fori(2, PASSES) as r:
                                with pe.If(tokens > r * CAP[0]):
                                    further(r)
                                with pe.Else():
                                    skipped(1)
                        with pe.Else():
                            skipped(PASSES - 2)
                        pe.sem_inc(s["gu_free"], 1)
                    with pe.Else():
                        skipped(PASSES - 1)
            pe.wait_ge(s["Y_kept"], 2 * EPAIRS + 2)
            scatter(turn, Y).then_inc(s["scattered"], 1)

        @block.scalar
        def _(act):
            count = [0]

            def link(ins):
                count[0] += 1
                ins.then_inc(s["act_step"], 1)
                act.wait_ge(s["act_step"], count[0])

            def two(b):
                return ps[:, b:b + 2, :].rearrange("p b n -> p (b n)")

            def squares(k):
                for st in range(STREAMS):
                    if k == N_FFN:
                        act.wait_ge(s["x_mid"], 3 + st)
                    last = nc.scalar.activation(h[:, st, :], x[:, st, :], ACT.Square,
                                                accum_out=numbers(k, 0)[:, st:st + 1])
                last.then_inc(s["square_done"], 1)

            def keep_hT(k):
                for st in range(STREAMS):
                    act.wait_ge(s["hT_shown"], STREAMS * k + st + 1)
                    nc.scalar.copy(hT[:, :, P * st:P * (st + 1)], two(4 * st).rearrange("p (k n) -> p k n", n=P))\
                      .then_inc(s["hT_ready"], 1)

            squares(0)
            rsqrt_act(act, link, N_IN, numbers(N_IN, 1), numbers(N_IN, 2))

            def keep_ada(m):
                act.wait_ge(s["ada_done"], m + 1)
                nc.scalar.copy(ada[:, (ADA_FIRST + m) % ADA_CHUNKS, :], ada_bank(m)).then_inc(s["ada_kept"], 1)

            keep_hT(0)
            for u, (c, c0, w, by_channel, st) in enumerate(UNITS_IN):
                act.wait_ge(s["proj_done"], u + 1)
                b = PROJ_BANKS[u % len(PROJ_BANKS)]
                wide = bank(b, 0, STREAMS * P)
                if u == 0:
                    last = nc.scalar.copy(lrT[0:2 * RANK, :], ps[0:2 * RANK, b, 0:STREAMS * P])
                elif c == 0:
                    last = nc.scalar.copy(ci[:, u - 1, :], wide)
                elif c == 1 and u < 7:
                    last = nc.scalar.mul(qT[:, u - 5, :], wide, float(DK) ** -0.5)
                elif c == 1:
                    last = nc.scalar.copy(kT[:, u - 7, :], wide)
                else:
                    last = nc.scalar.copy(((v, nax, gg)[c - 2])[:, st, c0:c0 + w], bank(b, 0, w))
                last.then_inc(s["proj_kept"], 1)
                if u == LAST_UNIT[3]:
                    rsqrt_act(act, link, N_QK, numbers(N_QK, 1), numbers(N_QK, 2))
                if u == 3:
                    act.wait_ge(s["vec_shown"], 1)
                    nc.scalar.copy(vecT[:], bank(5, 0, 2 * 64).rearrange("p (c r) -> p c r", c=2)[:, :, 0:R_END])\
                      .then_inc(s["vec_ready"], 1)
                if u == 4:
                    for st2 in range(STREAMS):
                        act.wait_ge(s["z_shown"], st2 + 1)
                        z = la[:, st2, :, :].rearrange("p a n -> p (a n)")
                        link(nc.scalar.activation(z, bank(st2), ACT.Abs))
                        link(nc.scalar.activation(z, z, ACT.Exp, scale=-1.0))
                        nc.scalar.activation(z, z, ACT.Ln, bias=1.0).then_inc(s["la_log"], 1)
                    act.wait_ge(s["proj_kept"], 5)
                    nc.scalar.activation(csig, ci[:, 2:4, :], ACT.Sigmoid).then_inc(s["conv_sig"], 1)
            rsqrt_act(act, link, N_CONV, numbers(N_CONV, 1), numbers(N_CONV, 2))
            for m in range(3):
                keep_ada(m)
            act.wait_ge(s["convB_shown"], 1)
            for c in range(2):
                y = cacc[:, c, :, :].rearrange("p s t -> p (s t)")
                nc.scalar.activation(y, bank(5, 256 * c, 256 * (c + 1)), ACT.Identity,
                                     scale=vecT[:, c, R_LNG:R_LNG + 1], bias=vecT[:, c, R_LNB:R_LNB + 1])\
                  .then_inc(s["conv_neg"], 1)
            act.wait_ge(s["conv_neg"], 2)
            nc.scalar.activation(csig, cacc[:].rearrange("p c s t -> p c (s t)"), ACT.Sigmoid)\
              .then_inc(s["conv_sig"], 1)
            nc.scalar.activation(tm[:].rearrange("p l n -> p (l n)"), gg[:].rearrange("p s n -> p (s n)"),
                                 ACT.Sigmoid).then_inc(s["gg_sig"], 1)
            keep_ada(3)
            keep_ada(4)
            act.wait_ge(s["pw_shown"], 1)
            nc.scalar.copy(cat[:, 4:6, :], bank(4).rearrange("p (o n) -> p o n", o=2)).then_inc(s["cat_conv"], 1)
            act.wait_ge(s["nT_shown"], 1)
            nc.scalar.mul(qnT, bank(2).rearrange("p (a n) -> p a n", a=2), vecT[:, 0, R_QN:R_QN + 1])
            nc.scalar.mul(knT, bank(3).rearrange("p (a n) -> p a n", a=2), vecT[:, 0, R_KN:R_KN + 1])
            nc.scalar.copy(kcT, bank(6, 0, 256).rearrange("p (a n) -> p a n", a=2)).then_inc(s["nT_ready"], 1)
            keep_ada(5)
            for st in range(STREAMS):
                act.wait_ge(s["max_ready"], st + 1)
                pr = (p0, p1)[st]
                w = (P, 2 * P)[st]
                for e in range(2):
                    for a in range(PAIRS):
                        i = 2 * e + a
                        last = nc.scalar.activation(pr[:, i, :], bank((2, 6)[st] + e, w * a, w * (a + 1)), ACT.Exp,
                                                    bias=mx[:, 4 * st + i:4 * st + i + 1],
                                                    accum_out=p_sum[:, 4 * st + i:4 * st + i + 1])
                last.then_inc(s["p_exp"], 1)
            keep_ada(6)
            keep_ada(7)
            act.wait_ge(s["pT_shown"], 1)
            nc.scalar.copy(pT, ps[:, 0:3, :].rearrange("p b (i n) -> p (b i) n", n=P)).then_inc(s["pT_ready"], 1)
            keep_ada(8)
            act.wait_ge(s["ada_kept"], ADA_LATER)
            load_bias(act, layer, ADA_FIRST, ADA_CHUNKS, s["bias_in"])
            act.wait_ge(s["pv_shown"], 1)
            nc.scalar.copy(cat[:, 6:8, :], bank(3).rearrange("p (a n) -> p a n", a=2)).then_inc(s["cat_na"], 1)
            for g in range(8):
                act.wait_ge(s["decay_shown"], g + 1)
                if g == 1:
                    act.wait_ge(s["kco_ready"], 1)
                if g >= 2:
                    act.wait_ge(s["X_ready"], g - 1)
                nc.scalar.activation(E[:, g % 2, :, :], two(0).rearrange("p (l n) -> p l n", n=P), ACT.Exp)\
                  .then_inc(s["E_ready"], 1)
                if 1 <= g <= ADA_CHUNKS - ADA_GLA:
                    keep_ada(ADA_GLA - 1 + g)
            act.wait_ge(s["ada_kept"], ADA_CHUNKS)
            load_bias(act, following, 0, ADA_FIRST, s["bias_next"])
            act.wait_ge(s["st_pre"], 1)
            nc.scalar.activation(kd.rearrange("p a n -> p (a n)"), bank(3), ACT.Exp).then_inc(s["st_exp"], 1)
            act.wait_ge(s["st_shown"], 1)
            act.wait_ge(s["X_ready"], 8)
            nc.scalar.copy(hflat[0:DK, 0:1024], ps[0:DK, 6:8, :].rearrange("p b n -> p (b n)")).then_inc(s["st_kept"], 1)
            for st in range(STREAMS):
                rsqrt_act(act, link, N_GLA + st, numbers(N_GLA + st, 1), numbers(N_GLA + st, 2))
            for st in range(STREAMS):
                act.wait_ge(s["goT_shown"], st + 1)
                nc.scalar.mul(cat[:, 0:4, P * st:P * (st + 1)], bank(st).rearrange("p (k n) -> p k n", n=P),
                              vecT[:, 0, R_ON:R_ON + 1]).then_inc(s["cat_gla"], 1)
            act.wait_ge(s["bias_next"], 64)
            act.wait_ge(s["stored"], layer * (16 * STORES) + 16 * STORES)
            squares(N_FFN)
            rsqrt_act(act, link, N_FFN, numbers(N_FFN, 1), numbers(N_FFN, 2))
            keep_hT(1)
            for st in range(STREAMS):
                act.wait_ge(s["logits_shown"], st + 1)
                nc.scalar.activation(scores[:, st, :], bank(2 + 4 * st, 0, EXPERTS), ACT.Sigmoid)\
                  .then_inc(s["scored"], 1)
            for st in range(STREAMS):
                nc.scalar.copy(hs[:, 0, st], h[:, st, :].rearrange("t (n k) -> t k n", k=KT)).then_inc(s["hs1"], 1)
            act.wait_ge(s["g2_shown"], 1)
            for st in range(STREAMS):
                last = nc.scalar.copy(g2[:, st, :], two(4 * st))
            last.then_inc(s["g2_kept"], 1)

            for part, left, done in ((1, "rest1", "hs2"), (2, "rest2", "hs3")):
                for st in range(STREAMS):
                    act.wait_ge(s[left], st + 1)
                    nc.scalar.copy(hs[:, part, st], h[:, st, :].rearrange("t (n k) -> t k n", k=KT))\
                      .then_inc(s[done], 1)
            for st in range(STREAMS):
                if st == 1:
                    act.wait_ge(s["tables_shown"], 1)
                    nc.scalar.copy(tables, ps[0:EXPERTS, 6, :].rearrange("p (a n) -> p a n", a=4))\
                      .then_inc(s["tables_kept"], 1)
                act.wait_ge(s["sh_gu"], st + 1)
                nc.scalar.activation(silu[:, st, :], bank(4 + st, 0, FF), ACT.Silu).then_inc(s["sh_silu"], 1)

            def keep_X(b, half):
                return nc.scalar.copy(X_e[:, b, KT // 2 * half:KT // 2 * (half + 1), :],
                                      bank(6).rearrange("p (k n) -> p k n", n=P))

            act.wait_ge(s["X_shown"], 1)
            keep_X(0, 0).then_inc(s["X_kept"], 1)
            for st in range(STREAMS):
                act.wait_ge(s["sh_turned"], st + 1)
                nc.scalar.copy(sh_actT[:, st, :], bank(4 + st, 0, FF)).then_inc(s["sh_kept"], 1)
            act.wait_ge(s["X_shown"], 2)
            keep_X(0, 1).then_inc(s["X_kept"], 1)
            act.wait_ge(s["sh_done"], STREAMS)
            act.wait_ge(s["places"], 1)
            with act.Fori(0, EPAIRS // TURN) as i:
                for q in range(TURN):
                    act.wait_ge(s["gu_done"], i * TURN + q + 1)
                    act.wait_ge(s["sh_act"], STREAMS)
                    nc.scalar.activation(silu[:, 0, :], bank(4, 0, FF), ACT.Silu).then_inc(s["silu_done"], 1)
                    act.wait_ge(s["turned"], i * TURN + q + 1)
                    nc.scalar.copy(turn, bank(5)).then_inc(s["turn_kept"], 1)
                    for half in range(2):
                        act.wait_ge(s["X_shown"], i * (2 * TURN) + 2 * q + 3 + half)
                        keep_X(1 - q, half).then_inc(s["X_kept"], 1)
                    tokens = act.value_load(most_i[0:1, bass.ds(i * TURN + q, 1)], min_val=0, max_val=SKEW * STREAMS * P)
                    def further(r):
                        m = (i * TURN + q) * (PASSES - 1) + r
                        for half in range(2):
                            act.wait_ge(s["over_Xs"], m * 2 - 1 + half)
                            keep_X(q, half).then_inc(s["over_Xk"], 1)
                        act.wait_ge(s["over_gu"], m)
                        nc.scalar.activation(silu[:, 1, :], bank(4, 0, FF), ACT.Silu)\
                          .then_inc(s["over_silu"], 1)
                        act.wait_ge(s["over_turned"], m)
                        nc.scalar.copy(turn_over, bank(5)).then_inc(s["over_kept"], 1)
                        act.wait_ge(s["over_done"], m)
                        act.sem_inc(s["over_left"], 1)

                    def skipped(k):
                        for name, n in (("over_Xk", 2), ("over_silu", 1), ("over_kept", 1)):
                            act.sem_inc(s[name], n * k)

                    with act.If(tokens > CAP[0]):
                        further(1)
                        with act.If(tokens > 2 * CAP[0]):
                            with act.Fori(2, PASSES) as r:
                                with act.If(tokens > r * CAP[0]):
                                    further(r)
                                with act.Else():
                                    skipped(1)
                        with act.Else():
                            skipped(PASSES - 2)
                    with act.Else():
                        skipped(PASSES - 1)

        @block.vector
        def _(dve):
            count = [0]

            def link(ins):
                count[0] += 1
                ins.then_inc(s["dve_step"], 1)
                dve.wait_ge(s["dve_step"], count[0])

            tt, ts, stt = nc.vector.tensor_tensor, nc.vector.tensor_scalar, nc.vector.scalar_tensor_tensor

            def two(b):
                return ps[:, b:b + 2, :].rearrange("p b n -> p (b n)")

            tmflat = tm[:].rearrange("p l n -> p (l n)")

            def modulate(k, norm):
                dve.wait_ge(s["square_done"], k + 1)
                rsqrt_dve(dve, link, norm, *[numbers(norm, j) for j in range(5)], 1.0 / D)
                dve.wait_ge(s["norm_in"], 16 * (k + 1))
                for st in range(STREAMS):
                    dve.wait_ge(s["mod_shown"], STREAMS * k + st + 1)
                    link(stt(out=tmflat, in0=two(4 * st), scalar=1.0, in1=gbc[:], op0=ALU.add, op1=ALU.mult))
                    link(stt(out=h[:, st, :], in0=x[:, st, :], scalar=numbers(norm, 4)[:, st:st + 1], in1=tmflat,
                             op0=ALU.mult, op1=ALU.mult))
                    tt(h[:, st, :], h[:, st, :], two(4 * st + 2), ALU.add).then_inc(s["h_ready"], 1)

            modulate(0, N_IN)
            for st in range(STREAMS):
                dve.wait_ge(s["la_log"], st + 1)
                z = la[:, st, :, :].rearrange("p a n -> p (a n)")
                link(stt(out=z, in0=bank(st), scalar=0.0, in1=z, op0=ALU.min, op1=ALU.subtract))
                ts(z, z, 1.0 / 16.0, None, ALU.mult).then_inc(s["la_ready"], 1)
            dve.wait_ge(s["conv_sig"], 1)
            for c in range(2):
                link(tt(hpad[:, c, :, HALO:HALO + P], ci[:, c, :].rearrange("p (s t) -> p s t", s=2),
                        csig[:, c, :].rearrange("p (s t) -> p s t", s=2), ALU.mult))
            dve.wait_ge(s["vec_ready"], 1)
            for t in range(TAPS):
                for c in range(2):
                    k = 2 * t + c
                    shifted = hpad[:, c, :, t:t + P]
                    wt = vecT[:, c, R_DW + t:R_DW + t + 1]
                    if t == 0:
                        ins = ts(cacc[:, c, :, :], shifted, wt, vecT[:, c, R_DWB:R_DWB + 1], ALU.mult, ALU.add)
                    else:
                        dve.wait_ge(s["tap"], k - 1)
                        ins = stt(out=cacc[:, c, :, :], in0=shifted, scalar=wt, in1=cacc[:, c, :, :],
                                  op0=ALU.mult, op1=ALU.add)
                    ins.then_inc(s["tap"], 1)
            dve.wait_ge(s["tap"], 2 * TAPS)
            nc.vector.memset(sm[:, 176:177], 0.0).then_inc(s["conv_ready"], 1)
            dve.wait_ge(s["proj_kept"], LAST_UNIT[3] + 1)
            dve.wait_ge(s["hT_ready"], STREAMS)
            link(tt(sq, nax[:, :, 0:512], nax[:, :, 0:512], ALU.mult))
            link(nc.vector.tensor_reduce(numbers(N_QK, 0), sq.rearrange("p s (g d) -> p (s g) d", d=DK), AX.X, ALU.add))
            rsqrt_dve(dve, link, N_QK, *[numbers(N_QK, j) for j in range(5)], 1.0 / DK)
            r = numbers(N_QK, 4)
            link(ts(r.rearrange("p (s g) -> p s g", s=2)[:, :, 0:HEADS], r.rearrange("p (s g) -> p s g", s=2)[:, :, 0:HEADS],
                    float(DK) ** -0.5, None, ALU.mult))
            for st in range(STREAMS):
                last = tt(nq[:, st, :].rearrange("p (g d) -> p g d", d=DK),
                          nax[:, st, 0:512].rearrange("p (g d) -> p g d", d=DK),
                          r[:, 8 * st:8 * (st + 1)].unsqueeze(2).broadcast_to([P, 8, DK]), ALU.mult)
            last.then_inc(s["nq_ready"], 1)
            dve.wait_ge(s["convT_shown"], 1)
            tok = bank(4).rearrange("p (s n) -> p s n", s=2)
            link(nc.vector.tensor_reduce(conv_mean, tok, AX.X, ALU.add))
            link(ts(conv_mean, conv_mean, -1.0 / CONV_CH, None, ALU.mult))
            for st in range(STREAMS):
                link(ts(cTok[:, st, :], tok[:, st, :], conv_mean[:, st:st + 1], None, ALU.add))
            link(tt(cSq, cTok, cTok, ALU.mult))
            link(nc.vector.tensor_reduce(numbers(N_CONV, 0), cSq, AX.X, ALU.add))
            rsqrt_dve(dve, link, N_CONV, *[numbers(N_CONV, j) for j in range(5)], 1.0 / CONV_CH)
            for st in range(STREAMS):
                last = ts(cTok[:, st, :], cTok[:, st, :], numbers(N_CONV, 4)[:, st:st + 1], None, ALU.mult)
            last.then_inc(s["ctok_ready"], 1)
            dve.wait_ge(s["conv_sig"], 2)
            y = cacc[:].rearrange("p c s t -> p c (s t)")
            tt(y, y, csig, ALU.mult).then_inc(s["cact_ready"], 1)
            for st in range(STREAMS):
                dve.wait_ge(s["scores_shown"], st + 1)
                sc = ps[:, 2:4, 0:256] if st == 0 else ps[:, 6:8, :]
                link(nc.vector.tensor_reduce(mx[:, 4 * st:4 * st + 4].rearrange("p (e a) -> p e a", e=2),
                                             sc.rearrange("p e (a k) -> p e a k", a=2), AX.X, ALU.max))
                ts(mx[:, 4 * st:4 * st + 4], mx[:, 4 * st:4 * st + 4], -1.0, None, ALU.mult).then_inc(s["max_ready"], 1)
            dve.wait_ge(s["p_exp"], STREAMS)
            link(nc.vector.reciprocal(p_inv, p_sum))
            tt(p0, p0, p_inv[:, 0:4].unsqueeze(2).broadcast_to([P, 4, P]), ALU.mult)
            tt(p1, p1, p_inv[:, 4:8].unsqueeze(2).broadcast_to([P, 4, 2 * P]), ALU.mult).then_inc(s["p_ready"], 1)
            dve.wait_ge(s["gg_sig"], 1)
            ggf = gg[:].rearrange("p s n -> p (s n)")
            link(tt(ggf, ggf, tmflat, ALU.mult))

            def combine(g):
                st, a, dr = g // 4, g // 2 % 2, g % 2
                n = LEVELS + (dr == 0)
                for e in range(2):
                    dve.wait_ge(s["pair_shown"], 2 * g + e + 1)
                    if st == 1 and dr == 0:
                        dve.wait_ge(s["o_shown"], 2 * a + e + 1)
                    b = (2, 6)[e]
                    tt(tm[:, 0:n, :], two(b).rearrange("p (l n) -> p l n", n=P)[:, 0:n, :],
                       (maskf, maskb)[dr][:, 0:n, :], ALU.mult).then_inc(s["masked"], 1)
                    dve.wait_ge(s["masked"], 2 * g + e + 1)
                    levels = tm[:, 0:n, :].rearrange("p l n -> p n l")
                    if dr == 0:
                        link(nc.vector.tensor_reduce(att[:, a, e, :], levels, AX.X, ALU.add))
                    else:
                        link(nc.vector.tensor_reduce(att2[:, 0:P], levels, AX.X, ALU.add))
                        tt(att[:, a, e, :], att[:, a, e, :], att2[:, 0:P], ALU.add).then_inc(s["att_ready"], 1)
                        dve.wait_ge(s["att_ready"], 2 * (g // 2) + e + 1)

            dve.wait_ge(s["pv_shown"], 1)
            decayed(dve, tt, 0)
            dve.wait_ge(s["matrices"], 1)
            for g in range(8):
                combine(g)
            dve.wait_ge(s["st_exp"], 1)
            for dr in range(2):
                last = tt(kd[:, dr, :], kd[:, dr, :], bank(2, 0, 256), ALU.mult)
            last.then_inc(s["kd_ready"], 1)
            for st in range(STREAMS):
                dve.wait_ge(s["o_shown"], 4 * (st + 1))
                o = bank(4 + st).rearrange("p (h n) -> p h n", n=DV)
                t4 = tm[:, 4 * st:4 * (st + 1), :]
                o_copy = hflat[:, 1024 + 512 * st:1536 + 512 * st].rearrange("p (h n) -> p h n", n=DV)
                link(nc.vector.tensor_copy(o_copy, o))
                link(tt(t4, o_copy, o_copy, ALU.mult))
                link(nc.vector.tensor_reduce(numbers(N_GLA + st, 0), t4, AX.X, ALU.add))
                rsqrt_dve(dve, link, N_GLA + st, *[numbers(N_GLA + st, j) for j in range(5)], 1.0 / DV)
                link(tt(t4, o_copy, numbers(N_GLA + st, 4).unsqueeze(2).broadcast_to([P, HEADS, DV]), ALU.mult))
                g4 = gg[:, st, :].rearrange("p (h n) -> p h n", n=DV)
                tt(g4, g4, t4, ALU.mult).then_inc(s["go_ready"], 1)
            dve.wait_ge(s["go_ready"], STREAMS)
            for half in range(2):
                for st in range(STREAMS):
                    u = 2 * half + st
                    dve.wait_ge(s["mix_shown"], u + 1)
                    t = tmflat[:, 512 * (u % 2):512 * (u % 2 + 1)]
                    nc.vector.tensor_copy(t, bank((4, 5, 0, 1)[u])).then_inc(s["dve_step"], 1)
                    count[0] += 1
                    dve.wait_ge(s["dve_step"], count[0])
                    link(tt(t, t, bank(PROJ_BANKS[u]), ALU.mult))
                    xs = x[:, st, 512 * half:512 * (half + 1)]
                    tt(xs, xs, t, ALU.add).then_inc(s["x_mid"], 1)
            dve.wait_ge(s["x_mid"], 4)
            modulate(1, N_FFN)
            dve.wait_ge(s["scored"], STREAMS)
            for st in range(STREAMS):
                last = tt(biased[:, st, :], scores[:, st, :], rbias[:], ALU.add)
            link(last)
            for st in range(STREAMS):
                for g in range(GROUPS):
                    last = nc.vector.max(top[:, st, g, :], biased[:, st, PER_GROUP * g:PER_GROUP * (g + 1)])
            link(last)
            link(tt(grp, top[:, :, :, 0], top[:, :, :, 1], ALU.add))
            other = grp.unsqueeze(2).broadcast_to([P, STREAMS, GROUPS, GROUPS])
            own = grp.unsqueeze(3).broadcast_to([P, STREAMS, GROUPS, GROUPS])
            earlier = tri8[:].unsqueeze(1).broadcast_to([P, STREAMS, GROUPS, GROUPS])
            link(tt(ties, other, own, ALU.is_equal))
            tt(beats, other, own, ALU.is_gt)
            link(tt(ties, ties, earlier, ALU.mult))
            link(tt(beats, beats, ties, ALU.add))
            link(nc.vector.tensor_reduce(rank, beats, AX.X, ALU.add))
            link(ts(rank, rank, TOP_GROUPS - 0.5, NEVER, ALU.is_gt, ALU.mult))
            bs = biased.rearrange("p s (g n) -> p s g n", n=PER_GROUP)
            link(tt(bs, bs, rank.unsqueeze(3).broadcast_to([P, STREAMS, GROUPS, PER_GROUP]), ALU.add))
            for st in range(STREAMS):
                last = nc.vector.max(best[:, st, :], biased[:, st, :])
            link(last)
            for st in range(STREAMS):
                last = nc.vector.match_replace(out=chosen[:, st, :], in_to_replace=best[:, st, :],
                                               in_values=biased[:, st, :], imm_value=3 * NEVER)
            link(last)
            link(ts(sel, chosen, 2 * NEVER, None, ALU.is_lt))
            nc.vector.memset(place[:, :, EXPERTS:], -1.0).then_inc(s["chosen_ready"], 1)
            link(tt(chosen, sel, scores, ALU.mult))
            link(nc.vector.tensor_reduce(tot, chosen, AX.X, ALU.add))
            link(nc.vector.reciprocal(tot, tot))
            for st in range(STREAMS):
                last = ts(gate[:, st, 0:EXPERTS], chosen[:, st, :], tot[:, st:st + 1], ROUTED_SCALE, ALU.mult, ALU.mult)
            link(last)

            dve.wait_ge(s["counted"], 1)
            for st in range(STREAMS):
                link(stt(out=place[:, st, 0:EXPERTS], in0=bank(2, 64 * st, 64 * (st + 1)), scalar=1.0,
                         in1=sel[:, st, :], op0=ALU.add, op1=ALU.mult))
                link(ts(place[:, st, 0:EXPERTS], place[:, st, 0:EXPERTS], -1.0, None, ALU.add))
            link(nc.vector.tensor_copy(own_load, ps[0:EXPERTS, 2, 192:192 + EXPERTS]))
            link(stt(out=own_key, in0=own_load, scalar=-float(EXPERTS), in1=expert_no[0:EXPERTS, :], op0=ALU.mult,
                     op1=ALU.add))
            link(ts(keys, ps[0:EXPERTS, 2, 128:128 + EXPERTS], -float(EXPERTS), None, ALU.mult))
            link(tt(keys, keys, wanted[0:EXPERTS, 0, 0:EXPERTS], ALU.add))
            link(tt(keys, own_key, keys, ALU.is_gt))
            link(nc.vector.tensor_reduce(load_rank, keys, AX.X, ALU.add))
            ts(order, rank_at[0:EXPERTS, :], load_rank, None, ALU.is_equal).then_inc(s["ordered"], 1)
            dve.wait_ge(s["sorted_shown"], 1)
            nc.vector.tensor_copy(order_i, ps[0:EXPERTS, 7, 256:256 + EXPERTS]).then_inc(s["order_ready"], 1)
            link(nc.vector.tensor_copy(load, ps[0:EXPERTS, 7, 320:320 + EXPERTS]))
            link(stt(out=most, in0=load[:, 1::2], scalar=float(SKEW), in1=load[:, 0::2], op0=ALU.mult, op1=ALU.max))
            nc.vector.tensor_copy(most_i, most)
            nc.vector.tensor_copy(place[:, :, 0:EXPERTS], bank(7, 0, 128).rearrange("p (s e) -> p s e", s=STREAMS))
            nc.vector.tensor_copy(gate[:, :, 0:EXPERTS], bank(7, 128, 256).rearrange("p (s e) -> p s e", s=STREAMS))\
              .then_inc(s["places"], 1)

            def onehot(out, pair, places):
                for c, (first, cap) in enumerate(zip(FIRST, CAP)):
                    last = tt(out[:, :, first:first + cap],
                              places[:, first:first + cap].unsqueeze(1).broadcast_to([P, STREAMS, cap]),
                              place[:, :, bass.ds(pair * 2 + c, 1)].broadcast_to([P, STREAMS, cap]), ALU.is_equal)
                return last

            def weigh(out, places, pair):
                for c, (first, cap) in enumerate(zip(FIRST, CAP)):
                    last = tt(out[:, :, first:first + cap], places[:, :, first:first + cap],
                              gate[:, :, bass.ds(pair * 2 + c, 1)].broadcast_to([P, STREAMS, cap]), ALU.mult)
                return last

            dve.wait_ge(s["places"], 1)
            onehot(G[0], 0, wanted[:, 0, :]).then_inc(s["G_ready"], 1)
            onehot(G[1], 1, wanted[:, 0, :]).then_inc(s["G_ready"], 1)
            dve.wait_ge(s["G_ready"], 1)
            weigh(S[0], G[0], 0).then_inc(s["S_ready"], 1)
            for st in range(STREAMS):
                dve.wait_ge(s["sh_silu"], st + 1)
                tt(acts[:, st, :], silu[:, st, :], bank(4 + st, FF, 2 * FF), ALU.mult).then_inc(s["sh_act"], 1)
            dve.wait_ge(s["sh_gu"], STREAMS)
            nc.vector.memset(Y[:, 0:512], 0.0).then_inc(s["Y_kept"], 1)
            nc.vector.memset(Y[:, 512:1024], 0.0).then_inc(s["Y_kept"], 1)
            dve.wait_ge(s["sh_turned"], STREAMS)
            with dve.Fori(0, EPAIRS // TURN) as i:
                for q in range(TURN):
                    pair = i * TURN + q
                    dve.wait_ge(s["silu_done"], i * TURN + q + 1)
                    tt(acts[:, 0, :], silu[:, 0, :], bank(4, FF, 2 * FF), ALU.mult).then_inc(s["act_done"], 1)
                    dve.wait_ge(s["Y_shown"], i * (2 * TURN) + 2 * q + 1)
                    nc.vector.tensor_copy(Y[:, 0:512], bank(7)).then_inc(s["Y_kept"], 1)
                    dve.wait_ge(s["G_ready"], i * TURN + q + 2)
                    weigh(S[0], G[1 - q], pair + 1).then_inc(s["S_ready"], 1)
                    dve.wait_ge(s["S_ready"], i * TURN + q + 1)
                    onehot(G[q], pair + 2, wanted[:, 0, :]).then_inc(s["G_ready"], 1)
                    dve.wait_ge(s["Y_shown"], i * (2 * TURN) + 2 * q + 2)
                    nc.vector.tensor_copy(Y[:, 512:1024], bank(7)).then_inc(s["Y_kept"], 1)
                    tokens = dve.value_load(most_i[0:1, bass.ds(i * TURN + q, 1)], min_val=0, max_val=SKEW * STREAMS * P)
                    def further(r):
                        m = (i * TURN + q) * (PASSES - 1) + r
                        steps = pair * PASSES + r
                        dve.wait_ge(s["over_want"], steps)
                        tt(want[:], want[:], wanted[:, 1, :], ALU.add).then_inc(s["over_want"], 1)
                        dve.wait_ge(s["over_want"], steps + 1)
                        onehot(G[2], pair, want).then_inc(s["over_G"], 1)
                        dve.wait_ge(s["over_G"], m)
                        weigh(S[1], G[2], pair).then_inc(s["over_GS"], 1)
                        dve.wait_ge(s["over_silu"], m)
                        tt(acts[:, 1, :], silu[:, 1, :], bank(4, FF, 2 * FF), ALU.mult)\
                          .then_inc(s["over_act"], 1)
                        for half in range(2):
                            dve.wait_ge(s["over_Ys"], m * 2 - 1 + half)
                            nc.vector.tensor_copy(Y_over[:, 512 * half:512 * (half + 1)], bank(7))\
                              .then_inc(s["over_Yk"], 1)
                        dve.wait_ge(s["over_done"], m)
                        dve.sem_inc(s["over_left"], 1)

                    def skipped(k):
                        for name, n in (("over_want", 1), ("over_G", 1), ("over_GS", 1), ("over_act", 1),
                                        ("over_Yk", 2)):
                            dve.sem_inc(s[name], n * k)

                    with dve.If(tokens > CAP[0]):
                        nc.vector.tensor_copy(want[:], wanted[:, 0, :]).then_inc(s["over_want"], 1)
                        further(1)
                        with dve.If(tokens > 2 * CAP[0]):
                            with dve.Fori(2, PASSES) as r:
                                with dve.If(tokens > r * CAP[0]):
                                    further(r)
                                with dve.Else():
                                    skipped(1)
                        with dve.Else():
                            skipped(PASSES - 2)
                    with dve.Else():
                        dve.sem_inc(s["over_want"], 1)
                        skipped(PASSES - 1)
            dve.wait_ge(s["scattered"], EPAIRS + 1)
            for st in range(STREAMS):
                link(tt(tmflat, two(2 * st), g2[:, st, :], ALU.mult))
                link(tt(x[:, st, :], x[:, st, :], tmflat, ALU.add))

        @block.gpsimd
        def _(pool):
            with pool.If(layer < 1):
                for lv in range(LEVELS):
                    w = P >> (lv + 1)
                    nb = P // (2 * w)
                    early, late = halves(lv)
                    blocks = [[-2 * w, nb], [0, w]]
                    keep(late[0], ALU.is_ge, 0.0, -w, blocks, 1)
                    keep(early[0], ALU.is_ge, 0.0, -1, [[-2 * w, nb], [-1, w]], 1)
                    keep(early[1], ALU.is_ge, 0.0, 0, [[-2 * w, nb], [-1, w]], 1)
                    keep(late[1], ALU.is_ge, 0.0, -w, blocks, 1)
                    keep(late[2], ALU.is_ge, 0.0, 0, blocks, 1)
                    step(nc.gpsimd.memset(early[2], 0.0))
                    keep(early[3], ALU.is_ge, 0.0, -w, blocks, 1)
                    step(nc.gpsimd.memset(late[3], 0.0))
                steps_done(pool)
                for lv in range(LEVELS):
                    w = P >> (lv + 1)
                    nb = P // (2 * w)
                    early, late = halves(lv)
                    blocks_up = [[2 * w, nb], [0, w]]
                    tok_up = [[2 * w, nb], [1, w]]
                    keep(late[0], ALU.is_ge, 0.0, w, tok_up, -1)
                    keep(early[0], ALU.is_ge, 0.0, w - 1, blocks_up, -1)
                    keep(early[1], ALU.is_ge, 0.0, w - 1, blocks_up, -1)
                    keep(late[1], ALU.is_ge, 0.0, w - 1, tok_up, -1)
                    keep(late[2], ALU.is_ge, 0.0, w - 1, blocks_up, -1)
                    keep(early[3], ALU.is_ge, 0.0, 2 * w - 1, blocks_up, -1)
                steps_done(pool)
                pool.sem_inc(s["matrices"], 1)
            with pool.Else():
                pool.sem_inc(s["matrices"], 1)
            pool.wait_ge(s["attn_in"], 16 * N_ATTN)
            nc.gpsimd.tensor_tensor(biasr, biasr, maskr[:].unsqueeze(1).broadcast_to([P, HEADS, P]), ALU.add)\
              .then_inc(s["bias_ready"], 1)
            pool.wait_ge(s["small_in"], 16 * N_SMALL)
            pool.wait_ge(s["nq_ready"], 1)
            nc.gpsimd.tensor_tensor(kco.rearrange("p (h d) -> p h d", h=HEADS),
                                    nq[:, 0, 256:512].rearrange("p (h d) -> p h d", h=HEADS),
                                    gk[:].unsqueeze(1).broadcast_to([P, HEADS, DK]), ALU.mult).then_inc(s["kco_ready"], 1)
            pool.wait_ge(s["kco_ready"], 1)
            dma_in(pool, A["new_cache_na_k"][0, layer].rearrange("h t d -> t h d"),
                   kco.rearrange("p (h d) -> p h d", h=HEADS), s["stored"])
            dma_in(pool, A["new_cache_na_v"][0, layer].rearrange("h t d -> t h d"),
                   nax[:, 0, 512:768].rearrange("p (h d) -> p h d", h=HEADS), s["stored"])
            pool.wait_ge(s["pv_shown"], 1)
            pool.wait_ge(s["X_ready"], 1)
            for g in range(1, 8):
                decayed(pool, nc.gpsimd.tensor_tensor, g)
            pool.wait_ge(s["st_kept"], 1)
            for dr in range(2):
                dma_in(pool, A["new_state_gla"][0, layer, dr].rearrange("h d v -> d h v"),
                       hflat[0:DK, 512 * dr:512 * (dr + 1)].rearrange("p (h v) -> p h v", h=HEADS), s["stored"])
            pool.wait_ge(s["stored"], layer * (16 * STORES) + 16 * STORES)
            pool.wait_ge(s["hT_shown"], 2 * STREAMS)
            for part, kept, left in ((0, "hs1", "rest1"), (1, "hs2", "rest2")):
                for st in range(STREAMS):
                    pool.wait_ge(s[kept], st + 1)
                    nc.gpsimd.tensor_tensor(h[:, st, :].rearrange("t (n k) -> t k n", k=KT),
                                            h[:, st, :].rearrange("t (n k) -> t k n", k=KT), hs[:, part, st],
                                            ALU.subtract).then_inc(s[left], 1)

    with nc.Block() as block:
        @block.gpsimd
        def _(pool):
            for name in SIGNALS:
                if name not in ("stored", "const_step", "x_loaded", "c_sig", "c_step", "y_out", "c_loaded", "const_set",
                                "first_in0", "first_in1", "first_in2", "first_in3", "first_done", "first_kept",
                                "first_bias"):
                    pool.sem_clear(s[name])
    layers.__exit__(None, None, None)

    with nc.Block() as block:
        @block.sync
        def _(sp):
            sp.dma_start(A["y_prompt"][0], x[:, 0, :]).then_inc(s["y_out"], 16)
            sp.dma_start(A["y_sample"][0], x[:, 1, :]).then_inc(s["y_out"], 16)
            sp.wait_ge(s["y_out"], 32)


_INS = ["x_prompt", "x_sample", "state_gla", "cache_na_k", "cache_na_v", "c", "c_ctx", "w_ada", "b_ada", "norm_mix",
        "norm_ffn", "w_in", "gla_w_gate", "gla_b_gate", "gla_out_norm", "conv_dw", "conv_dw_b", "conv_ln_g",
        "conv_ln_b", "conv_pw", "na_q_norm", "na_k_norm", "na_rpb", "w_out", "router_w", "router_bias", "exp_w_gate",
        "exp_w_up", "exp_w_down", "sh_w_gate", "sh_w_up", "sh_w_down"]
_OUTS = [("y_prompt", (1, 128, 1024)), ("y_sample", (1, 128, 1024)), ("new_state_gla", (1, 2, 2, 4, 64, 128)),
         ("new_cache_na_k", (1, 2, 4, 128, 64)), ("new_cache_na_v", (1, 2, 4, 128, 64))]


def kernel(**inputs):
    import numpy as _np
    import concourse.bacc as _bacc
    from concourse.bass_utils import run_bass_kernel_spmd as _run

    nc = _bacc.Bacc("TRN2", target_bir_lowering=False, num_devices=1)
    arrays, tensors = {}, {}
    for name in _INS:
        a = _np.ascontiguousarray(inputs[name])
        arrays[f"in_{name}"] = a
        tensors[name] = nc.dram_tensor(f"in_{name}", a.shape, F32, kind="ExternalInput").ap()
    for name, shape in _OUTS:
        tensors[name] = nc.dram_tensor(f"out_{name}", shape, F32, kind="ExternalOutput").ap()
    build(nc, tensors)
    r = _run(nc, [arrays], core_ids=[0])
    return tuple(r.results[0][f"out_{name}"] for name, _ in _OUTS)
```
